# Optimizing a Trainium2 kernel written in Bass

```python
import math
import jax, jax.numpy as jnp
from jax import lax
import numpy as np

D_MODEL = 1024
BATCH = 1
SEQ = 256
DEPTH = 1
DEC_BATCH = 8
DEC_SEQ = 4
PAST_LEN = 2048
PAGE_SIZE = 128

N_META = 16
RW_WIDTH = D_MODEL // 2
RW_HEAD_DIM = 64
RW_HEADS = RW_WIDTH // RW_HEAD_DIM
RW_DECAY_LORA = 64
RW_AAA_LORA = 64
RW_GATE_LORA = 128
RW_GN_EPS = RW_HEAD_DIM * 1e-5
GDN_WIDTH = D_MODEL // 2
GDN_HEAD_DIM = 128
GDN_HEADS = GDN_WIDTH // GDN_HEAD_DIM
GDN_CONV = 4
GDN_CHUNK = 64
GDN_CONV_CH = 3 * GDN_WIDTH
N_GROUPS = 4
EXPERTS_PER_GROUP = 8
N_EXPERTS = N_GROUPS * EXPERTS_PER_GROUP
EXPERT_FF = 512
TOP_K_IN_GROUP = 2
RMS_EPS = 1e-6

RW_SIZES = (RW_WIDTH, RW_WIDTH, RW_WIDTH, RW_DECAY_LORA, RW_AAA_LORA, RW_GATE_LORA)
RW_COLS = sum(RW_SIZES)
GDN_COLS = 4 * GDN_WIDTH + 2 * GDN_HEADS
IN_COLS = RW_COLS + GDN_COLS + 2 * D_MODEL

kernel_name = 'hybrid_rwkv7_gdn_hmoe_step'

def _split(x, sizes):
    return jnp.split(x, np.cumsum(sizes)[:-1].tolist(), axis=-1)

def rmsnorm(x, w):
    xf = x.astype(jnp.float32)
    y = xf * lax.rsqrt(jnp.mean(xf * xf, axis=-1, keepdims=True) + RMS_EPS)
    return (y * w.astype(jnp.float32)).astype(x.dtype)

def l2norm(x):
    return x * lax.rsqrt(jnp.sum(x * x, axis=-1, keepdims=True) + 1e-6)

def rwkv7_scan(S0, r, w, k, v, a_vec, b_vec):
    def step(S, inp):
        r_t, w_t, k_t, v_t, a_t, b_t = inp
        sa = jnp.einsum('bhij,bhj->bhi', S, a_t)
        S = S * w_t[:, :, None, :] + sa[..., :, None] * b_t[..., None, :] + v_t[..., :, None] * k_t[..., None, :]
        return S, jnp.einsum('bhij,bhj->bhi', S, r_t)
    xs = tuple(jnp.moveaxis(t, 1, 0) for t in (r, w, k, v, a_vec, b_vec))
    S, y = lax.scan(step, S0, xs)
    return jnp.moveaxis(y, 0, 1), S

def rwkv7_branch(cur, prev, S0, p):
    B, T, _ = cur.shape
    H, N = RW_HEADS, RW_HEAD_DIM
    f32 = jnp.float32
    c = lambda name: p[name].astype(f32)
    cf = cur.astype(f32)
    zc = cf + (prev.astype(f32) - cf) * c('mu_shift')
    r, k, v, xw, xa, xg = _split(zc, RW_SIZES)
    w_raw = -jax.nn.softplus(-(c('rw_w0') + jnp.tanh(xw) @ c('rw_w2'))) - 0.5
    decay = jnp.exp(-jnp.exp(w_raw))
    a = jax.nn.sigmoid(c('rw_a0') + xa @ c('rw_a2'))
    g = jax.nn.sigmoid(xg) @ c('rw_g2')
    hd = lambda t: t.reshape(B, T, H, N)
    kk = l2norm(hd(k * c('rw_k_k')))
    k = k * (1.0 + (a - 1.0) * c('rw_k_a'))
    a_h = hd(a)
    y, S = rwkv7_scan(S0.astype(f32), hd(r), hd(decay), hd(k), hd(v), -kk, kk * a_h)
    mu = jnp.mean(y, axis=-1, keepdims=True)
    var = jnp.mean(jnp.square(y - mu), axis=-1, keepdims=True)
    y = ((y - mu) * lax.rsqrt(var + RW_GN_EPS)).reshape(B, T, RW_WIDTH) * c('rw_lnx_w') + c('rw_lnx_b')
    bonus = jnp.sum(hd(r) * hd(k) * c('rw_r_k'), axis=-1, keepdims=True) * hd(v)
    y = (y + bonus.reshape(B, T, RW_WIDTH)) * g
    return y.astype(cur.dtype), S.astype(S0.dtype)

def gdn_chunked(S0, q, k, v, g, beta, chunk):
    B, L, H, Dk = q.shape
    Dv = v.shape[-1]
    n = L // chunk

    def blk(t):
        t = jnp.swapaxes(t, 1, 2)
        return t.reshape(B, H, n, chunk, *t.shape[3:])

    q, k, v, g, beta = blk(q), blk(k), blk(v), blk(g), blk(beta)
    g = jnp.cumsum(g, axis=-1)
    pos = jnp.arange(chunk)
    causal = pos[:, None] >= pos[None, :]
    strict = pos[:, None] > pos[None, :]
    decay = jnp.exp(jnp.where(causal, g[..., :, None] - g[..., None, :], -jnp.inf))
    kb = k * beta[..., None]
    A = jnp.where(strict, jnp.einsum('bhnid,bhnjd->bhnij', kb, k) * decay, 0.0)
    M = A + jnp.eye(chunk, dtype=A.dtype)
    rhs = jnp.concatenate([v * beta[..., None], kb * jnp.exp(g)[..., None]], axis=-1)
    sol = lax.linalg.triangular_solve(M, rhs, left_side=True, lower=True, unit_diagonal=True)
    u, w = sol[..., :Dv], sol[..., Dv:]
    qk = jnp.einsum('bhnid,bhnjd->bhnij', q, k) * decay
    q_dec = q * jnp.exp(g)[..., None]
    g_last = g[..., -1]
    k_dec = k * jnp.exp(g_last[..., None] - g)[..., None]

    def step(S, inp):
        u_n, w_n, qk_n, qd_n, kd_n, gl_n = inp
        v_new = u_n - jnp.einsum('bhcd,bhde->bhce', w_n, S)
        o = jnp.einsum('bhcd,bhde->bhce', qd_n, S) + jnp.einsum('bhij,bhje->bhie', qk_n, v_new)
        S = S * jnp.exp(gl_n)[..., None, None] + jnp.einsum('bhcd,bhce->bhde', kd_n, v_new)
        return S, o

    xs = tuple(jnp.moveaxis(t, 2, 0) for t in (u, w, qk, q_dec, k_dec, g_last))
    S, o = lax.scan(step, S0, xs)
    o = jnp.moveaxis(o, 0, 2).reshape(B, H, L, Dv)
    return jnp.swapaxes(o, 1, 2), S

def gdn_branch(qkv_raw, z, a_raw, b_raw, conv_prev, S0, segments, p):
    B, T, _ = qkv_raw.shape
    H, Dh = GDN_HEADS, GDN_HEAD_DIM
    f32 = jnp.float32
    xpad = jnp.concatenate([conv_prev.astype(qkv_raw.dtype), qkv_raw], axis=1)
    conv = lax.conv_general_dilated(xpad, p['gdn_conv_w'][:, None, :].astype(xpad.dtype), (1,), 'VALID',
                                    dimension_numbers=('NWC', 'WIO', 'NWC'), feature_group_count=GDN_CONV_CH)
    qkv = jax.nn.silu(conv.astype(f32))
    q, k, v = _split(qkv, (GDN_WIDTH, GDN_WIDTH, GDN_WIDTH))
    q = l2norm(q.reshape(B, T, H, Dh)) * (Dh ** -0.5)
    k = l2norm(k.reshape(B, T, H, Dh))
    v = v.reshape(B, T, H, Dh)
    g = -jnp.exp(p['gdn_A_log'].astype(f32)) * jax.nn.softplus(a_raw.astype(f32) + p['gdn_dt_bias'].astype(f32))
    beta = jax.nn.sigmoid(b_raw.astype(f32))
    S = S0.astype(f32)
    outs = []
    start = 0
    for length, chunk in segments:
        sl = slice(start, start + length)
        o, S = gdn_chunked(S, q[:, sl], k[:, sl], v[:, sl], g[:, sl], beta[:, sl], chunk)
        outs.append(o)
        start += length
    o = jnp.concatenate(outs, axis=1) if len(outs) > 1 else outs[0]
    o = rmsnorm(o, p['gdn_norm_w']) * jax.nn.silu(z.astype(f32).reshape(B, T, H, Dh))
    return o.reshape(B, T, GDN_WIDTH).astype(qkv_raw.dtype), xpad[:, T:], S.astype(S0.dtype)

def token_mixer(xn, shift_prev, wkv0, conv0, gdn0, segments, p):
    P = xn @ p['w_in']
    rw_cur, gdn_cols, gate_cols = _split(P, (RW_COLS, GDN_COLS, 2 * D_MODEL))
    prev_first = (shift_prev.astype(xn.dtype) @ p['w_in'][:, :RW_COLS])[:, None]
    rw_prev = jnp.concatenate([prev_first, rw_cur[:, :-1]], axis=1)
    yA, wkv = rwkv7_branch(rw_cur, rw_prev, wkv0, p)
    qkv_raw, z, a_raw, b_raw = _split(gdn_cols, (3 * GDN_WIDTH, GDN_WIDTH, GDN_HEADS, GDN_HEADS))
    yB, conv, gdn = gdn_branch(qkv_raw, z, a_raw, b_raw, conv0, gdn0, segments, p)
    gA, gB = _split(gate_cols, (D_MODEL, D_MODEL))
    merged = jax.nn.sigmoid(gA) * (yA @ p['w_oA']) + jax.nn.sigmoid(gB) * (yB @ p['w_oB'])
    return merged @ p['w_o'], xn[:, -1].astype(shift_prev.dtype), wkv, conv.astype(conv0.dtype), gdn

def hier_moe(x, p):
    B, T, D = x.shape
    f32 = jnp.float32
    xt = x.reshape(B * T, D)
    gprob = jax.nn.softmax((xt @ p['router_g'] + p['router_g_b']).astype(f32), axis=-1)
    gp, gidx = lax.top_k(gprob, 1)
    elog = (xt @ p['router_e'] + p['router_e_b']).astype(f32).reshape(-1, N_GROUPS, EXPERTS_PER_GROUP)
    elog = jnp.take_along_axis(elog, gidx[:, :, None], axis=1)[:, 0]
    ev, eidx = lax.top_k(elog, TOP_K_IN_GROUP)
    wts = gp * jax.nn.softmax(ev, axis=-1)
    eid = gidx * EXPERTS_PER_GROUP + eidx
    gate = jnp.sum(jax.nn.one_hot(eid, N_EXPERTS, dtype=f32) * wts[..., None], axis=1)

    def expert(acc, inp):
        wg, wu, wd, ge = inp
        h = jax.nn.silu(xt @ wg) * (xt @ wu)
        return acc + ge[:, None] * (h @ wd).astype(f32), None

    y, _ = lax.scan(expert, jnp.zeros(xt.shape, f32), (p['moe_w_gate'], p['moe_w_up'], p['moe_w_down'], gate.T))
    return y.astype(x.dtype).reshape(B, T, D)

def decoder_layer(h, n_meta, segments, shift_prev, wkv0, conv0, gdn0, p):
    xn = rmsnorm(h, p['norm1_w'])
    mix, shift, wkv, conv, gdn = token_mixer(xn, shift_prev, wkv0, conv0, gdn0, segments, p)
    h = (h + mix)[:, n_meta:]
    h = h + hier_moe(rmsnorm(h, p['norm2_w']), p)
    return h, (shift, wkv, conv, gdn)

def setup_inputs(seed: int = 0) -> dict:
    key = jax.random.key(seed)
    ks = iter(jax.random.split(key, 48))
    f32 = jnp.float32
    L = DEPTH
    nrm = lambda shape, scale=1.0: jax.random.normal(next(ks), shape, f32) * scale
    gain = lambda shape: 1.0 + nrm(shape, 0.01)
    dt = jnp.exp(jax.random.uniform(next(ks), (L, GDN_HEADS), f32, math.log(1e-3), math.log(1e-1)))
    return {
        'x_prompt': nrm((BATCH, SEQ, D_MODEL)),
        'x_sample': nrm((DEC_BATCH, DEC_SEQ, D_MODEL)),
        'state_shift': nrm((L, DEC_BATCH, D_MODEL)),
        'state_wkv': nrm((L, DEC_BATCH, RW_HEADS, RW_HEAD_DIM, RW_HEAD_DIM), 0.3),
        'state_conv': nrm((L, DEC_BATCH, GDN_CONV - 1, GDN_CONV_CH)),
        'state_gdn': nrm((L, DEC_BATCH, GDN_HEADS, GDN_HEAD_DIM, GDN_HEAD_DIM), 0.1),
        'meta_tokens': nrm((N_META, D_MODEL)),
        'norm1_w': gain((L, D_MODEL)),
        'w_in': nrm((L, D_MODEL, IN_COLS), D_MODEL ** -0.5),
        'mu_shift': jax.random.uniform(next(ks), (L, RW_COLS), f32),
        'rw_w0': -2.0 + nrm((L, RW_WIDTH), 0.5),
        'rw_w2': nrm((L, RW_DECAY_LORA, RW_WIDTH), 0.1),
        'rw_a0': nrm((L, RW_WIDTH), 0.1),
        'rw_a2': nrm((L, RW_AAA_LORA, RW_WIDTH), 0.1),
        'rw_g2': nrm((L, RW_GATE_LORA, RW_WIDTH), RW_GATE_LORA ** -0.5),
        'rw_k_k': 0.85 + nrm((L, RW_WIDTH), 0.05),
        'rw_k_a': 1.0 + nrm((L, RW_WIDTH), 0.05),
        'rw_r_k': nrm((L, RW_HEADS, RW_HEAD_DIM), 0.1),
        'rw_lnx_w': gain((L, RW_WIDTH)),
        'rw_lnx_b': nrm((L, RW_WIDTH), 0.01),
        'gdn_conv_w': nrm((L, GDN_CONV, GDN_CONV_CH), GDN_CONV ** -0.5),
        'gdn_A_log': jnp.log(jax.random.uniform(next(ks), (L, GDN_HEADS), f32, 1.0, 16.0)),
        'gdn_dt_bias': dt + jnp.log(-jnp.expm1(-dt)),
        'gdn_norm_w': gain((L, GDN_HEAD_DIM)),
        'w_oA': nrm((L, RW_WIDTH, D_MODEL), RW_WIDTH ** -0.5),
        'w_oB': nrm((L, GDN_WIDTH, D_MODEL), GDN_WIDTH ** -0.5),
        'w_o': nrm((L, D_MODEL, D_MODEL), D_MODEL ** -0.5),
        'norm2_w': gain((L, D_MODEL)),
        'router_g': nrm((L, D_MODEL, N_GROUPS), D_MODEL ** -0.5),
        'router_g_b': nrm((L, N_GROUPS), 0.01),
        'router_e': nrm((L, D_MODEL, N_EXPERTS), D_MODEL ** -0.5),
        'router_e_b': nrm((L, N_EXPERTS), 0.01),
        'moe_w_gate': nrm((L, N_EXPERTS, D_MODEL, EXPERT_FF), D_MODEL ** -0.5),
        'moe_w_up': nrm((L, N_EXPERTS, D_MODEL, EXPERT_FF), D_MODEL ** -0.5),
        'moe_w_down': nrm((L, N_EXPERTS, EXPERT_FF, D_MODEL), EXPERT_FF ** -0.5),
        'norm_f_w': gain((D_MODEL,)),
    }

def reference(x_prompt, x_sample, state_shift, state_wkv, state_conv, state_gdn, meta_tokens, norm1_w, w_in,
              mu_shift, rw_w0, rw_w2, rw_a0, rw_a2, rw_g2, rw_k_k, rw_k_a, rw_r_k, rw_lnx_w, rw_lnx_b, gdn_conv_w,
              gdn_A_log, gdn_dt_bias, gdn_norm_w, w_oA, w_oB, w_o, norm2_w, router_g, router_g_b, router_e,
              router_e_b, moe_w_gate, moe_w_up, moe_w_down, norm_f_w):
    stacked = dict(norm1_w=norm1_w, w_in=w_in, mu_shift=mu_shift, rw_w0=rw_w0, rw_w2=rw_w2, rw_a0=rw_a0,
                   rw_a2=rw_a2, rw_g2=rw_g2, rw_k_k=rw_k_k, rw_k_a=rw_k_a, rw_r_k=rw_r_k, rw_lnx_w=rw_lnx_w,
                   rw_lnx_b=rw_lnx_b, gdn_conv_w=gdn_conv_w, gdn_A_log=gdn_A_log, gdn_dt_bias=gdn_dt_bias,
                   gdn_norm_w=gdn_norm_w, w_oA=w_oA, w_oB=w_oB, w_o=w_o, norm2_w=norm2_w, router_g=router_g,
                   router_g_b=router_g_b, router_e=router_e, router_e_b=router_e_b, moe_w_gate=moe_w_gate,
                   moe_w_up=moe_w_up, moe_w_down=moe_w_down)
    B, S_len, _ = x_prompt.shape
    dt = x_prompt.dtype
    meta = jnp.broadcast_to(meta_tokens.astype(dt)[None], (B, N_META, D_MODEL))
    h_p = jnp.concatenate([meta, x_prompt], axis=1)
    h_s = x_sample
    seg_p = ((N_META, N_META), (S_len, GDN_CHUNK))
    seg_s = ((x_sample.shape[1], x_sample.shape[1]),)
    new_p, new_s = [], []
    for layer in range(DEPTH):
        p = {name: arr[layer] for name, arr in stacked.items()}
        n_drop = N_META if layer == DEPTH - 1 else 0
        h_p, st_p = decoder_layer(
            h_p, n_drop, seg_p,
            jnp.zeros((B, D_MODEL), dt),
            jnp.zeros((B, RW_HEADS, RW_HEAD_DIM, RW_HEAD_DIM), dt),
            jnp.zeros((B, GDN_CONV - 1, GDN_CONV_CH), dt),
            jnp.zeros((B, GDN_HEADS, GDN_HEAD_DIM, GDN_HEAD_DIM), dt), p)
        h_s, st_s = decoder_layer(h_s, 0, seg_s, state_shift[layer], state_wkv[layer], state_conv[layer],
                                  state_gdn[layer], p)
        new_p.append(st_p)
        new_s.append(st_s)
    y_prompt = rmsnorm(h_p, norm_f_w)
    y_sample = rmsnorm(h_s, norm_f_w)
    shift_p = jnp.stack([s[0] for s in new_p])
    wkv_p = jnp.stack([s[1] for s in new_p])
    conv_p = jnp.stack([s[2] for s in new_p])
    gdn_p = jnp.stack([s[3] for s in new_p])
    shift_s = jnp.stack([s[0] for s in new_s])
    wkv_s = jnp.stack([s[1] for s in new_s])
    conv_s = jnp.stack([s[2] for s in new_s])
    gdn_s = jnp.stack([s[3] for s in new_s])
    return (y_prompt, y_sample, shift_p, wkv_p, conv_p, gdn_p, shift_s, wkv_s, conv_s, gdn_s)


_drawn_inputs = setup_inputs


def setup_inputs(seed=0):
    import zlib

    import numpy as np

    out = dict(_drawn_inputs(seed))
    spreads = {}
    factors = {'rw_k_k': 8.674,
     'rw_lnx_w': 61.005,
     'gdn_norm_w': 45.972,
     'norm_f_w': 200.0,
     'norm1_w': 3.128,
     'rw_lnx_b': 64.0,
     'norm2_w': 8.0,
     'router_g_b': 8.0,
     'router_e_b': 32.673}
    for name, (base, spread) in spreads.items():
        noise = np.random.default_rng([zlib.crc32(name.encode()), seed]).standard_normal(out[name].shape)
        drawn = base * np.exp(spread * noise) if base else spread * noise
        out[name] = __import__('jax').numpy.asarray(drawn.astype(out[name].dtype))
    for name, factor in factors.items():
        out[name] = (out[name] * factor).astype(out[name].dtype)
    return out
```

```python
from contextlib import ExitStack

import numpy as np

import concourse.bass as bass
from concourse import mybir

F32 = mybir.dt.float32
I32 = mybir.dt.int32
ACT = mybir.ActivationFunctionType
ALU = mybir.AluOpType
AX = mybir.AxisListType

P = 128
D = 1024
KD = D // P
NSEQ, TSEQ, META, SEQ = 8, 4, 16, 256
C = 64
COL_META, COL_S, COL_P = 16, 32, 64
N = COL_P + SEQ
NC = N // C
M = N - COL_S
RW_T, QKV_T, Z_T = 14, 12, 4
IN_T = RW_T + QKV_T + Z_T
HR, HG = 8, 4
T4 = 4
G, EG, E, FF = 4, 8, 32, 512
LEVELS = 6
CAP = 64
E2 = E + 2
XC = 7 * NSEQ + 3 + META + SEQ
CONVN = XC - 3


class Cols:

    def __init__(self):
        self.at, self.width = {}, 0

    def add(self, name, n):
        self.at[name] = (self.width, self.width + n)
        self.width += n


CST = Cols()
for _name, _n in (("ident", P), ("ones", P), ("blockones", P), ("center", P), ("sum_r", T4 * 8),
                  ("spread_r", T4 * P), ("sum_g", 8 * 8), ("spread_g", 8 * P), ("gmask0", P),
                  ("gmask1", P), ("incl", N), ("strict", N), ("low", LEVELS * C), ("up", LEVELS * C),
                  ("seq", NSEQ + 1), ("carry", N), ("eps", 1), ("gn_eps", 1), ("one", 1),
                  ("first4", 4), ("first8", 8), ("before", P), ("iota", CAP), ("valid", 3)):
    CST.add(_name, _n)
PAR = Cols()
for _name, _n in (("norm1", KD), ("norm2", KD), ("normf", KD), ("mu", RW_T), ("w0", T4), ("a0", T4),
                  ("k_k", T4), ("k_a", T4), ("r_k", T4), ("ln_w", T4), ("ln_b", T4), ("conv", QKV_T * 4),
                  ("gdn_norm", 1), ("A_log", 1), ("dt_bias", 1), ("w2a2", 512), ("g2", 512), ("ab", KD * 8),
                  ("router", KD * 36), ("router_b", 36), ("conv_state", QKV_T * 24)):
    PAR.add(_name, _n)


def constants():
    c = np.zeros((P, CST.width), np.float32)

    def put(name, a, row=0):
        a = np.asarray(a, np.float32).reshape(len(a), -1)
        c[row:row + a.shape[0], CST.at[name][0]:CST.at[name][1]] = a

    i = np.arange(P)
    same = (i[:, None] // C == i[None] // C).astype(np.float32)
    put("ident", np.eye(P))
    put("ones", np.ones((P, P)))
    put("blockones", same)
    put("center", np.eye(P) - same / C)
    t, h = np.arange(T4), np.arange(8)
    put("sum_r", (2 * t[None, :, None] + (i // C)[:, None, None] == h[None, None]).astype(np.float32))
    put("spread_r", (h[:, None, None] == 2 * t[None, :, None] + (i // C)[None, None]).astype(np.float32))
    put("sum_g", np.broadcast_to((h[:, None] == h[None]), (P, 8, 8)))
    spread = np.broadcast_to((h[:, None, None] == h[None, :, None]), (8, 8, P))
    put("spread_g", spread)
    put("spread_g", spread, 32)
    seq = np.full(C, -1)
    seq[COL_META:COL_S] = NSEQ
    seq[COL_S:C] = np.arange(32) // TSEQ
    j = np.arange(C)
    together = [(seq[:, None] == seq[None]) & (seq[:, None] >= 0)] + [np.ones((C, C), bool)] * (NC - 1)
    incl = [g & (j[:, None] <= j[None]) for g in together]
    strict = [g & (j[:, None] < j[None]) for g in together]
    for n in (0, 1):
        put(f"gmask{n}", np.tile(np.concatenate([strict[n], incl[n]], 1), (2, 1)))
    put("incl", np.concatenate(incl, 1))
    put("strict", -np.concatenate(strict, 1).astype(np.float32))
    low = np.stack([(j[:, None] >> (n + 1) == j[None] >> (n + 1)) & (j[:, None] >> n & 1 == 1) & (j[None] >> n & 1 == 0)
                    for n in range(LEVELS)], 1)
    put("low", low)
    put("up", low.transpose(2, 1, 0))
    put("seq", np.tile(seq[:, None] == np.arange(NSEQ + 1)[None], (2, 1)))
    carry = np.ones(N)
    carry[[COL_META, *range(COL_S, C, TSEQ), *range(C, N, C)]] = 0
    put("carry", np.tile(carry, (P, 1)))
    put("eps", np.full(P, 1e-6))
    put("gn_eps", np.full(P, C * 1e-5))
    put("one", np.ones(P))
    put("first4", np.tile(np.arange(4, 0, -1), (P, 1)))
    put("first8", np.tile(np.arange(8, 0, -1), (P, 1)))
    put("before", i[:, None] < i[None])
    put("iota", np.tile(np.arange(CAP), (P, 1)))
    put("valid", i[:, None] + P * np.arange(3)[None] < M)
    return c


def build(nc, dram):
    ctx = ExitStack()
    with ctx:
        def sb(name, *shape):
            return ctx.enter_context(nc.sbuf_tensor(f"sb_{name}", [P, *shape], F32))

        def sem(name):
            return ctx.enter_context(nc.semaphore(name))

        cst = sb("cst", CST.width)
        par = sb("par", PAR.width)

        def K(name):
            return cst[:, CST.at[name][0]:CST.at[name][1]]

        def W(name):
            return par[:, PAR.at[name][0]:PAR.at[name][1]]

        def spread(ap, n):
            return ap.unsqueeze(len(ap.shape)).to_broadcast([*ap.shape, n])

        def over(ap, n):
            return ap.unsqueeze(1).to_broadcast([ap.shape[0], n, *ap.shape[1:]])

        xT = sb("xT", KD, N)
        yA = sb("yA", T4, M)
        yB = sb("yB", T4, M)
        rs = sb("rs", N)
        row_tmp = sb("row_tmp", N)
        ab_raw = sb("ab_raw", N)
        ARENA = 41100
        arena = sb("arena", ARENA)

        def at(start, *shape):
            n = int(np.prod(shape))
            assert start + n <= ARENA, (start, shape)
            v = arena[:, start:start + n]
            if len(shape) > 1:
                names = "abcde"[:len(shape)]
                v = v.rearrange(f"p ({' '.join(names)}) -> p {' '.join(names)}", **dict(zip(names, shape)))
            return v

        class Region:

            def __init__(self, start):
                self.pos = start

            def take(self, *shape):
                v = at(self.pos, *shape)
                self.pos += int(np.prod(shape))
                return v

        r = Region(0)
        xnT = r.take(KD, N)
        w_ring = [r.take(KD, P) for _ in range(2)]
        proj_at = r.pos
        proj = r.take(IN_T, N)
        xc = [r.take(XC) for _ in range(2)]
        conv_acc = [r.take(CONVN) for _ in range(2)]
        conv_out = r.take(QKV_T, 27)
        x_out = r.take(KD, NSEQ + 1)
        work_at = r.pos
        r = Region(work_at)
        temps_at = r.pos
        ta, tL, teL, tkk, t1, t2 = [r.take(T4, N) for _ in range(6)]
        tbonus = r.take(T4, N)
        tg = yB
        AR = r.take(T4, NC, 2, C)
        bk_at = r.pos
        BK = r.take(T4, NC, 2, C)
        GM = r.take(NC, HR, P)
        SV = r.take(NC, HR * C)
        BKt = r.take(NC, T4, P)
        PTs = r.take(T4, NC + NSEQ)
        small_r = rs
        r_end = r.pos
        r = Region(temps_at)
        XTr = r.take(NC, HR, C)
        invX = [r.take(HR, C) for _ in range(2)]
        invT = [r.take(HR, C) for _ in range(2)]
        Rs = r.take(HR * C)
        C0r = r.take(T4, 2, C)
        SVm = [r.take(HR * C) for _ in range(2)]
        STr = r.take(T4, P)
        assert r.pos <= temps_at + 6 * T4 * N
        r = Region(bk_at)
        ty, gn_sqv = r.take(T4, N), r.take(T4, M)
        SW = at(proj_at, NSEQ, T4, P)
        assert NSEQ * T4 * P <= RW_T * N
        r = Region(work_at)
        KQ = r.take(HG, NC, 2, C)
        qdec = r.take(HG, N)
        eGb = r.take(HG, N)
        Dincl = r.take(HG, N)
        Dstr = r.take(HG, N)
        GA = r.take(NC, HG, C)
        QKD = r.take(NC, HG, C)
        sqg = at(r.pos, 8, N)
        kdec = r.take(NC, HG, P)
        bV = r.take(NC, HG, P)
        XTg = r.take(NC, HG, C)
        invXg = [r.take(HR, C) for _ in range(2)]
        invTg = [r.take(HR, C) for _ in range(2)]
        Rg = r.take(HG, P)
        VN = r.take(HG * P)
        VNm = [r.take(HG * P) for _ in range(2)]
        Sg = r.take(HG, P)
        C0g = r.take(HG, 2, C)
        rows = r.take(N)
        srow = r.take(N)
        cols = r.take(NC, P)
        ecols = r.take(NC, 8)
        oT = r.take(HG, N)
        g_end = r.pos
        r = Region(work_at)
        wg_ring = [r.take(2, KD, P) for _ in range(2)]
        wo_ring = [r.take(2, T4, P) for _ in range(2)]
        wf_ring = [r.take(KD, P) for _ in range(2)]
        merged = r.take(KD, M)
        sgA = [r.take(M) for _ in range(2)]
        sgB = [r.take(M) for _ in range(2)]
        r = Region(0)
        hT = r.take(KD, M)
        xt2 = r.take(KD, 3 * P)
        acc = r.take(KD, M)
        rt = r.take(3, 36)
        rte = r.take(3, G, EG)
        rt8 = [r.take(3, EG) for _ in range(4)]
        rt4 = r.take(3, G)
        rt1 = [r.take(3) for _ in range(7)]
        gate = r.take(3, E2)
        member = r.take(3, E)
        slot = r.take(3, E2)
        flag_f = r.take(1)
        flag = r.take(1).bitcast(I32)
        pair_at = r.pos
        sel, selG = r.take(3, 2, CAP), r.take(3, 2, CAP)
        selT = r.take(3 * P)
        silu_s, hid_s = r.take(4, CAP), r.take(4, CAP)
        dense_at = r.pos
        gateT = r.take(3 * P)
        gsel = [r.take(M) for _ in range(2)]
        silu = [r.take(M) for _ in range(2)]
        hid = [r.take(4, M) for _ in range(2)]
        e_end = r.pos
        r = Region(dense_at)
        xtok = r.take(3, D)
        assert r.pos <= e_end
        r = Region(KD * M)
        xe = [r.take(KD, CAP) for _ in range(2)]
        yT = r.take(KD, 2 * CAP)
        ye = r.take(D)
        assert r.pos <= KD * M + KD * 3 * P
        r = Region(max(e_end, 0))
        ring_at = r.pos
        wgu = [r.take(2, KD, FF) for _ in range(1)]
        wdn = [r.take(4, D) for _ in range(1)]
        wgu.append(r.take(2, KD, FF))
        wdn.append(r.take(4, D))
        assert ring_at < work_at and r.pos <= ARENA

        bank = [ctx.enter_context(nc.psum_tensor(f"bank{i}", [P, 512], F32)) for i in range(8)]

        def bk(i, *shape):
            v = bank[i][:, 0:int(np.prod(shape))]
            if len(shape) > 1:
                names = "abcde"[:len(shape)]
                v = v.rearrange(f"p ({' '.join(names)}) -> p {' '.join(names)}", **dict(zip(names, shape)))
            return v

        S = {n: sem(n) for n in (
            "rms_sq", "rms_mm", "rms_root", "head_sq", "head_sum", "head_root", "head_inv", "head_spread",
            "ld_cst", "ld_par", "ld_x", "xn", "x_packed",
            "ld_w0", "ld_w1", "proj_done", "psum_free", "ab_done",
            "shift_step", "zc_done", "lora_in", "lora_mm", "lora_out", "cum", "exps",
            "bonus_in", "bonus_mm", "bk_done", "gram_r",
            "gm_done", "bar_done", "v_tr", "v_sb", "bt_tr", "bt_sb", "z_dead",
            "sv_zero", "ld_sw", 
            "s0_mm", "s0_k", "s0_sb", "ch_rhs", "ch_rhs_sb", "ch_sa", "ch_sa_sb", "ch_y", "ch_y_sb", "ch_st", "ch_st_sb",
            "svm", "sm_mm", "sm_sb", "gn_in", "gn_d", "yA",
            "xc_init", "xc_step", "xc_ready", "xc_used", "conv_step", "conv_done", "silu_done", "z_done",
            "ab_rows", "ab_lin", "g_rows", "g_cum", "g_exp", "g_kd", "g_bc", "g_bc_dve", "g_bc_act", "d_arg", "d_exp", "d_done", "cols_tr", "ecol", "ecol2",
            "kq_done", "gram_g", "ga_done", "kv_tr", "kv_sb",
            "rwkv_over", "yB",
            "ld_wg0", "ld_wg1", "ld_wf0", "ld_wf1", "op_mm", "op_sig", "op_free", "op_merge", "fin_mm", "h_done",
            "xt2", "rt_mm", "rt_sum", "rt_exp", "gate", "gt_tr", "gateT",
            "ld_e0", "ld_e1", "ld_d0", "ld_d1", "gsel", "gb_mm", "gu_mm", "silu", "hid", "dn_mm", "acc", "gu_free",
            "rt_member", "rt_pos", "flag", "xt_tr", "xtok", "sp_sel", "sp_selg", "sp_gather", "xe", "sp_gu", "sp_silu",
            "sp_hid", "sp_dn", "sp_yT", "sp_tr", "sp_ye", "sp_comb", "sp_acc", "sp_selT", "selT", "moe_done", "y_ready",
            "act_own", "dve_own", "moe_own", "ab_sb", "acc_init", "hid_step", "stores",
            "inv_t10", "inv_t11", "inv_t1s0", "inv_t1s1", "inv_t20", "inv_t21", "inv_upd0", "inv_upd1")}

        t_sq = AR.rearrange("p t c x s -> p (t c x s)").rearrange("p (k n) -> p k n", k=KD)
        xw, sgx = tbonus[0:C, 0, :], tbonus[:, 1, :]
        sqg_o = sqg.rearrange("p t n -> p (t n)")[:, 0:HG * M].rearrange("p (t n) -> p t n", t=HG)

        jobs_r = [([GM[0:C, c, h, 0:C] for h in range(HR)], invX[c % 2], invT[c % 2],
                   [XTr[0:C, c, h, :] for h in range(HR)], GM[0:C, c, :, 0:C], XTr[0:C, c]) for c in range(NC)]
        jobs_g = []
        for c in range(0, NC, 2):
            both = [(c_, h) for c_ in range(c, min(c + 2, NC)) for h in range(HG)]
            jobs_g.append(([GA[0:C, c_, h, :] for c_, h in both], invXg[c // 2 % 2], invTg[c // 2 % 2],
                           [XTg[0:C, c_, h, :] for c_, h in both],
                           GA[0:C, c:min(c + 2, NC)].rearrange("p c h s -> p (c h) s"),
                           XTg[0:C, c:c + len(both) // HG].rearrange("p c h s -> p (c h) s")))
        slot_jobs, used = [], [0, 0]
        for jobs in (jobs_r, jobs_g):
            for n in range(len(jobs)):
                slot_jobs.append(used[n % 2])
                used[n % 2] += 1

        block = ctx.enter_context(nc.Block())

        def own(eng, name):
            count = [0]

            def step(ins):
                count[0] += 1
                ins.then_inc(S[name], 1)
                eng.wait_ge(S[name], count[0])
            return step

        halves = [(0, slice(0, C)), (1, slice(C, P))]
        n_stores = 7

        @block.sync
        def _(sp):
            sp.dma_start(xT[:, :, :], dram["xT"]).then_inc(S["ld_x"], 16)
            sp.dma_start(cst[:, :], dram["cst"]).then_inc(S["ld_cst"], 16)
            for k in range(2):
                sp.dma_start(w_ring[k], dram["w_in"][k]).then_inc(S[f"ld_w{k}"], 16)
            sp.dma_start(par[:, :], dram["par"]).then_inc(S["ld_par"], 16)
            with sp.Fori(1, IN_T // 2) as i:
                for k in range(2):
                    sp.wait_ge(S["proj_done"], 2 * i + k - 1)
                    sp.dma_start(w_ring[k], dram["w_in"][bass.ds(2 * i + k, 1)].rearrange("a p k c -> p (a k) c"))\
                      .then_inc(S[f"ld_w{k}"], 16)
            sp.wait_ge(S["x_packed"], 1)
            sp.dma_start(dram["shift_out"], x_out).then_inc(S["stores"], 16)
            sp.wait_ge(S["z_dead"], 2)
            for par_, rows_ in halves:
                sp.dma_start(SW[rows_, :, :, par_ * C:par_ * C + C], dram["wkv_in"][rows_]).then_inc(S["ld_sw"], 16)
            sp.wait_ge(S["sm_sb"], NSEQ)
            for par_, rows_ in halves:
                sp.dma_start(dram["wkv_s"][rows_], SW[rows_, :, :, par_ * C:par_ * C + C]).then_inc(S["stores"], 16)
            sp.wait_ge(S["ch_st_sb"], NC)
            for par_, rows_ in halves:
                sp.dma_start(dram["wkv_p"][rows_], STr[rows_, :, par_ * C:par_ * C + C]).then_inc(S["stores"], 16)
            sp.wait_ge(S["conv_done"], QKV_T)
            sp.wait_ge(S["xc_ready"], QKV_T)
            sp.dma_start(dram["conv_out"], conv_out).then_inc(S["stores"], 16)
            sp.wait_ge(S["stores"], 16 * 6)
            sp.wait_ge(S["yA"], 1)
            sp.sem_inc(S["rwkv_over"], 1)
            sp.dma_start(SW, dram["gdn_in"]).then_inc(S["ld_sw"], 16)
            sp.wait_ge(S["sm_sb"], 2 * NSEQ)
            sp.dma_start(dram["gdn_s"], SW).then_inc(S["stores"], 16)
            sp.wait_ge(S["ch_st_sb"], 2 * NC)
            sp.dma_start(dram["gdn_p"], Sg).then_inc(S["stores"], 16)
            sp.wait_ge(S["yB"], 1)
            sp.wait_ge(S["stores"], 16 * 8)

            def load_out(i, k):
                one = dram["w_gab"][bass.ds(i, 1)] if not isinstance(i, int) else dram["w_gab"][i:i + 1]
                two = dram["w_oab"][bass.ds(i, 1)] if not isinstance(i, int) else dram["w_oab"][i:i + 1]
                sp.dma_start(wg_ring[k], one.rearrange("a p g k c -> p (a g) k c")).then_inc(S[f"ld_wg{k}"], 16)
                sp.dma_start(wo_ring[k], two.rearrange("a p g k c -> p (a g) k c")).then_inc(S[f"ld_wg{k}"], 16)

            for k in range(2):
                load_out(k, k)
            for k in range(2):
                sp.dma_start(wf_ring[k], dram["w_o"][k]).then_inc(S[f"ld_wf{k}"], 16)
            with sp.Fori(1, KD // 2) as i:
                for k in range(2):
                    sp.wait_ge(S["op_mm"], 2 * i + k - 1)
                    load_out(2 * i + k, k)
            with sp.Fori(1, KD // 2) as i:
                for k in range(2):
                    sp.wait_ge(S["fin_mm"], 2 * i + k - 1)
                    sp.dma_start(wf_ring[k], dram["w_o"][bass.ds(2 * i + k, 1)].rearrange("a p k c -> p (a k) c"))\
                      .then_inc(S[f"ld_wf{k}"], 16)
            sp.wait_ge(S["h_done"], KD)
            for k in range(2):
                sp.dma_start(wgu[k], dram["w_gu"][k]).then_inc(S[f"ld_e{k}"], 16)
                sp.dma_start(wdn[k], dram["w_dn"][k]).then_inc(S[f"ld_d{k}"], 16)

            def load_experts(gu_read, per_gu, dn_read, per_dn):
                with sp.Fori(1, E // 2) as i:
                    for k in range(2):
                        sp.wait_ge(S[gu_read], per_gu * (2 * i + k - 1))
                        sp.dma_start(wgu[k], dram["w_gu"][bass.ds(2 * i + k, 1)].rearrange("a p g k c -> p (a g) k c"))\
                          .then_inc(S[f"ld_e{k}"], 16)
                        sp.wait_ge(S[dn_read], per_dn * (2 * i + k - 1))
                        sp.dma_start(wdn[k], dram["w_dn"][bass.ds(2 * i + k, 1)].rearrange("a p k c -> p (a k) c"))\
                          .then_inc(S[f"ld_d{k}"], 16)

            sp.wait_ge(S["flag"], 1)
            crowded = sp.value_load(flag[0:1, 0:1], min_val=0, max_val=1)
            with sp.If(crowded < 1):
                load_experts("sp_gu", 1, "sp_dn", 1)
            with sp.Else():
                load_experts("gu_mm", 4, "dn_mm", KD)
            sp.wait_ge(S["y_ready"], 1)
            sp.dma_start(dram["y"], acc).then_inc(S["stores"], 16)
            sp.wait_ge(S["stores"], 16 * 9)

        @block.tensor
        def _(pe):
            mm = pe.matmul
            pe.wait_ge(S["ld_cst"], 16)
            pe.wait_ge(S["rms_sq"], 1)
            for k in range(KD):
                last = mm(bk(7, N), K("ones"), t_sq[:, k, :], start=(k == 0), stop=(k == KD - 1))
            last.then_inc(S["rms_mm"], 1)
            pe.wait_ge(S["xn"], 1)
            with pe.Fori(0, IN_T // 2) as i:
                for s in range(2):
                    pe.wait_ge(S[f"ld_w{s}"], 16 * i + 16)
                    pe.wait_ge(S["psum_free"], 2 * i + s + 1)
                    for k in range(KD):
                        last = mm(bk(s, N), w_ring[s][:, k, :], xnT[:, k, :], start=(k == 0), stop=(k == KD - 1))
                    last.then_inc(S["proj_done"], 1)
            pe.wait_ge(S["ld_par"], 16)
            wab = W("ab").rearrange("p (k c) -> p k c", k=KD)
            for b, lo, rows_ in ((2, 0, slice(0, 4)), (3, 4, slice(32, 36))):
                for k in range(KD):
                    last = mm(bank[b][rows_, 0:N], wab[:, k, lo:lo + 4], xnT[:, k, :], start=(k == 0), stop=(k == KD - 1))
                last.then_inc(S["ab_done"], 1)

            pe.wait_ge(S["ab_sb"], 2)
            pe.wait_ge(S["lora_in"], 2)
            for part in range(3):
                for t in range(T4):
                    if part:
                        pe.wait_ge(S["lora_out"], T4 * (part - 1) + t + 1)
                    lo = slice(t * P, t * P + P)
                    if part == 0:
                        ins = mm(bk(4 + t, N), W("w2a2")[0:C, lo], xw, start=True, stop=True)
                    elif part == 1:
                        ins = mm(bk(4 + t, N), W("w2a2")[C:P, lo], proj[C:P, 12, :], start=True, stop=True)
                    else:
                        ins = mm(bk(4 + t, N), W("g2")[:, lo], sgx, start=True, stop=True)
                    ins.then_inc(S["lora_mm"], 1)
            sum_r = K("sum_r").rearrange("p (t h) -> p t h", t=T4)
            spread_r = K("spread_r").rearrange("p (t c) -> p t c", t=T4)
            pe.wait_ge(S["head_sq"], 1)
            for t in range(T4):
                last = mm(bank[3][0:8, 0:N], sum_r[:, t, :], t2[:, t, :], start=(t == 0), stop=(t == T4 - 1))
            last.then_inc(S["head_sum"], 1)
            pe.wait_ge(S["head_inv"], 1)
            pe.wait_ge(S["lora_out"], 3 * T4)
            for t in range(T4):
                mm(bk(4 + t, N), spread_r[0:8, t, :], small_r[0:8, :], start=True, stop=True).then_inc(S["head_spread"], 1)
            pe.wait_ge(S["bonus_in"], 1)
            for t in range(T4):
                mm(bk(4 + t, N), K("blockones"), t2[:, t, :], start=True, stop=True).then_inc(S["bonus_mm"], 1)
            pe.wait_ge(S["psum_free"], IN_T + 2)
            flat = arena[:, proj_at:proj_at + IN_T * N]
            for c in range(NC):
                if c >= 2:
                    pe.wait_ge(S["v_sb"], c - 1)
                for t in range(T4):
                    lo = (8 + t) * N + C * c - C
                    last = pe.transpose(bank[c % 2][:, t * P:t * P + P], flat[:, lo:lo + P], K("ident"))
                last.then_inc(S["v_tr"], 1)
            pe.wait_ge(S["bk_done"], 1)
            pe.wait_ge(S["z_dead"], 1)
            for c in range(NC):
                for p_, rows_ in halves:
                    n = 2 * c + p_
                    if n >= 4:
                        pe.wait_ge(S["gm_done"], n - 3)
                    for t in range(T4):
                        last = mm(bank[4 + n % 4][:, t * P:t * P + P], BK[rows_, t, c].rearrange("p a b -> p (a b)"),
                                  AR[rows_, t, c].rearrange("p a b -> p (a b)"), start=True, stop=True)
                    last.then_inc(S["gram_r"], 1)
            pe.wait_ge(S["bar_done"], 1)
            pe.wait_ge(S["v_sb"], NC)
            for c in range(NC):
                if c >= 2:
                    pe.wait_ge(S["bt_sb"], c - 1)
                for t in range(T4):
                    last = pe.transpose(bank[c % 2][:, t * P:t * P + P], BK[:, t, c].rearrange("p a b -> p (a b)"), K("ident"))
                last.then_inc(S["bt_tr"], 1)

            jobs_done = [0]

            def invert(jobs):
                base = jobs_done[0]
                for pair in range(0, len(jobs), 2):
                    two = jobs[pair:pair + 2]
                    for level in range(LEVELS):
                        for q, (at_h, X, T1, XT_h, AT, XT) in enumerate(two):
                            n, slot = base + pair + q, q
                            pe.wait_ge(S[f"inv_upd{slot}"], (LEVELS + 1) * slot_jobs[n] + level + 1)
                            for h, a in enumerate(at_h):
                                rhs = K("ident")[0:C, 0:C] if level == 0 else X[0:C, h, :]
                                last = mm(bank[3 * slot][0:C, h * C:h * C + C], a, rhs, start=True, stop=True)
                            last.then_inc(S[f"inv_t1{slot}"], 1)
                        if level == 0:
                            continue
                        for q, (at_h, X, T1, XT_h, AT, XT) in enumerate(two):
                            n, slot = base + pair + q, q
                            pe.wait_ge(S[f"inv_t1s{slot}"], (LEVELS - 1) * slot_jobs[n] + level)
                            for h in range(len(at_h)):
                                if level < LEVELS - 1:
                                    mm(bank[3 * slot + 1][0:C, h * C:h * C + C], XT_h[h], T1[0:C, h, :], start=True, stop=True)
                                last = mm(bank[3 * slot + 2][0:C, h * C:h * C + C], T1[0:C, h, :], XT_h[h], start=True, stop=True)
                            last.then_inc(S[f"inv_t2{slot}"], 1)
                jobs_done[0] += len(jobs)
                for q in range(2):
                    n = max(n for n in range(jobs_done[0]) if (n if n < NC else n - NC) % 2 == q)
                    pe.wait_ge(S[f"inv_upd{q}"], (LEVELS + 1) * (slot_jobs[n] + 1))

            pe.wait_ge(S["gm_done"], 2 * NC)
            pe.wait_ge(S["bt_sb"], NC)
            invert(jobs_r)

            pe.wait_ge(S["ld_sw"], 32)
            pe.wait_ge(S["z_dead"], 2)
            c0 = bk(6, T4, 2, C)
            for b in range(NSEQ):
                lo = COL_S + TSEQ * b
                for t in range(T4):
                    last = mm(c0[:, t, :, lo:lo + TSEQ], SW[:, b, t, :], AR[:, t, 0, :, lo:lo + TSEQ], start=True, stop=True)
            last.then_inc(S["s0_mm"], 1)
            pe.wait_ge(S["s0_sb"], 1)
            for c in range(NC):
                if c:
                    pe.wait_ge(S["ch_st_sb"], c)
                for t in range(T4):
                    lhs, rhs = (C0r[:, t, 0, :], K("ident")) if c == 0 else (AR[:, t, c, 0, :], STr[:, t, :])
                    mm(bank[0][0:C, t * P:t * P + P], lhs, rhs, start=True, stop=False)
                    for h in (2 * t, 2 * t + 1):
                        last = mm(bank[0][0:C, h * C:h * C + C], GM[:, c, h, 0:C], SV[:, c, h * C:h * C + C],
                                  start=False, stop=(h % 2 == 1))
                last.then_inc(S["ch_rhs"], 1)
                pe.wait_ge(S["ch_rhs_sb"], c + 1)
                for h in range(HR):
                    last = mm(bank[1][0:C, h * C:h * C + C], XTr[0:C, c, h, :], Rs[0:C, h * C:h * C + C], start=True, stop=True)
                last.then_inc(S["ch_sa"], 1)
                pe.wait_ge(S["ch_sa_sb"], c + 1)
                if c == 0:
                    for b in range(NSEQ + 1):
                        pe.wait_ge(S["svm"], b + 1)
                        if b >= 2:
                            pe.wait_ge(S["sm_sb"], b - 1)
                        for t in range(T4):
                            last = mm(bank[4 + b % 2][:, t * P:t * P + P], BKt[:, 0, t, :], SVm[b % 2][:, t * P:t * P + P],
                                      start=True, stop=True)
                        last.then_inc(S["sm_mm"], 1)
                else:
                    for t in range(T4):
                        last = mm(bank[2][:, t * P:t * P + P], BKt[:, c, t, :], SV[:, c, t * P:t * P + P], start=True, stop=True)
                    last.then_inc(S["ch_st"], 1)
                if c:
                    pe.wait_ge(S["ch_y_sb"], c)
                for t in range(T4):
                    lhs, rhs = (K("ident"), C0r[:, t, 1, :]) if c == 0 else (STr[:, t, :], AR[:, t, c, 1, :])
                    mm(bank[3][:, t * C:t * C + C], lhs, rhs, start=True, stop=False)
                    for p_, rows_ in halves:
                        h = 2 * t + p_
                        last = mm(bank[3][rows_, t * C:t * C + C], SV[:, c, h * C:h * C + C], GM[:, c, h, C:P],
                                  start=False, stop=True)
                last.then_inc(S["ch_y"], 1)
            pe.wait_ge(S["ch_y_sb"], NC)
            for t in range(T4):
                mm(bk(4 + t, M), K("center"), ty[:, t, COL_S:], start=True, stop=True).then_inc(S["gn_d"], 1)
            pe.wait_ge(S["head_sq"], 2)
            for t in range(T4):
                last = mm(bank[3][0:8, 0:M], sum_r[:, t, :], gn_sqv[:, t, :], start=(t == 0), stop=(t == T4 - 1))
            last.then_inc(S["head_sum"], 1)
            pe.wait_ge(S["head_inv"], 2)
            for t in range(T4):
                mm(bk(4 + t, M), spread_r[0:8, t, :], small_r[0:8, 0:M], start=True, stop=True).then_inc(S["head_spread"], 1)

            sum_g = K("sum_g").rearrange("p (t h) -> p t h", t=8)
            spread_g = K("spread_g").rearrange("p (t c) -> p t c", t=8)
            pe.wait_ge(S["yA"], 1)
            pe.wait_ge(S["g_kd"], 1)
            for h in range(HG):
                if h:
                    pe.wait_ge(S["g_bc_dve"], 2 * h)
                    pe.wait_ge(S["g_bc_act"], h)
                mm(bank[4][0:C, 0:N], spread_g[0:4, h, 0:C], rows[0:4, :], start=True, stop=True).then_inc(S["g_bc"], 1)
                mm(bank[5][0:C, 0:N], spread_g[32:36, h, 0:C], rows[32:36, :], start=True, stop=True).then_inc(S["g_bc"], 1)
                mm(bk(6, N), spread_g[0:4, h, :], row_tmp[0:4, :], start=True, stop=True).then_inc(S["g_bc"], 1)
            for c in range(NC):
                last = pe.transpose(bank[7][0:C, c * 96:c * 96 + 96], rows[0:96, c * C:c * C + C], K("ident")[0:96, 0:96])
            last.then_inc(S["cols_tr"], 1)
            pe.wait_ge(S["head_sq"], 3)
            for t in range(8):
                last = mm(bank[0][0:8, 0:N], sum_g[:, t, :], sqg[:, t, :], start=(t == 0), stop=(t == 7))
            last.then_inc(S["head_sum"], 1)
            pe.wait_ge(S["head_inv"], 3)
            for t in range(8):
                if t >= 2:
                    pe.wait_ge(S["kq_done"], t - 1)
                mm(bk(1 + t % 2, N), spread_g[0:8, t, :], srow[0:8, :], start=True, stop=True).then_inc(S["head_spread"], 1)
            pe.wait_ge(S["kq_done"], 8)
            pe.wait_ge(S["ecol2"], 1)
            for c in range(NC):
                for w_ in range(2):
                    n = 2 * c + w_
                    if n >= 2:
                        pe.wait_ge(S["kv_sb"], n - 1)
                    for h in range(HG):
                        src = KQ[:, h, c, 0, :] if w_ == 0 else proj[:, 22 + h, c * C:c * C + C]
                        last = pe.transpose(bank[n % 2][0:C, h * P:h * P + P], src, K("ident"))
                    last.then_inc(S["kv_tr"], 1)
            pe.wait_ge(S["d_done"], 1)
            for c in range(NC):
                if c >= 2:
                    pe.wait_ge(S["ga_done"], c - 1)
                for h in range(HG):
                    last = mm(bank[2 + c % 2][0:C, h * P:h * P + P], KQ[:, h, c, 0, :],
                              KQ[:, h, c].rearrange("p a b -> p (a b)"), start=True, stop=True)
                last.then_inc(S["gram_g"], 1)
            pe.wait_ge(S["ga_done"], NC)
            pe.wait_ge(S["kv_sb"], 2 * NC)
            invert(jobs_g)
            pe.wait_ge(S["ld_sw"], 48)
            c0 = bk(6, HG, 2, C)
            for b in range(NSEQ):
                lo = COL_S + TSEQ * b
                for h in range(HG):
                    last = mm(c0[:, h, :, lo:lo + TSEQ], SW[:, b, h, :], KQ[:, h, 0, :, lo:lo + TSEQ], start=True, stop=True)
            last.then_inc(S["s0_mm"], 1)
            pe.wait_ge(S["s0_sb"], 2)
            for c in range(NC):
                if c:
                    pe.wait_ge(S["ch_st_sb"], NC + c)
                for h in range(HG):
                    lhs, rhs = (C0g[:, h, 0, :], K("ident")) if c == 0 else (KQ[:, h, c, 0, :], Sg[:, h, :])
                    last = mm(bank[0][0:C, h * P:h * P + P], lhs, rhs, start=True, stop=True)
                last.then_inc(S["ch_rhs"], 1)
                pe.wait_ge(S["ch_rhs_sb"], NC + c + 1)
                for h in range(HG):
                    last = mm(bank[1][0:C, h * P:h * P + P], XTg[0:C, c, h, :], Rg[0:C, h, :], start=True, stop=True)
                last.then_inc(S["ch_sa"], 1)
                pe.wait_ge(S["ch_sa_sb"], NC + c + 1)
                if c == 0:
                    for b in range(NSEQ + 1):
                        pe.wait_ge(S["svm"], NSEQ + 1 + b + 1)
                        if b >= 2:
                            pe.wait_ge(S["sm_sb"], NSEQ + b - 1)
                        for h in range(HG):
                            last = mm(bank[4 + b % 2][:, h * P:h * P + P], kdec[0:C, 0, h, :], VNm[b % 2][0:C, h * P:h * P + P],
                                      start=True, stop=True)
                        last.then_inc(S["sm_mm"], 1)
                else:
                    for h in range(HG):
                        last = mm(bank[2][:, h * P:h * P + P], kdec[0:C, c, h, :], VN[0:C, h * P:h * P + P], start=True, stop=True)
                    last.then_inc(S["ch_st"], 1)
                if c:
                    pe.wait_ge(S["ch_y_sb"], NC + c)
                for h in range(HG):
                    lhs, rhs = (K("ident"), C0g[:, h, 1, :]) if c == 0 else (Sg[:, h, :], qdec[:, h, c * C:c * C + C])
                    mm(bank[3][:, h * C:h * C + C], lhs, rhs, start=True, stop=False)
                    last = mm(bank[3][:, h * C:h * C + C], VN[0:C, h * P:h * P + P], QKD[0:C, c, h, :], start=False, stop=True)
                last.then_inc(S["ch_y"], 1)
            pe.wait_ge(S["head_sq"], 4)
            for h in range(HG):
                last = mm(bank[0][0:8, 0:M], sum_g[:, h, :], sqg_o[:, h, :], start=(h == 0), stop=(h == HG - 1))
            last.then_inc(S["head_sum"], 1)
            pe.wait_ge(S["head_inv"], 4)
            for h in range(HG):
                mm(bk(4 + h, M), spread_g[0:8, h, :], srow[0:8, 0:M], start=True, stop=True).then_inc(S["head_spread"], 1)

            pe.wait_ge(S["yB"], 1)
            with pe.Fori(0, KD // 2) as i:
                for s in range(2):
                    pe.wait_ge(S[f"ld_wg{s}"], 32 * i + 32)
                    pe.wait_ge(S["op_free"], 2 * i + s + 1)
                    for g in range(2):
                        for k in range(KD):
                            mm(bk(4 * s + g, M), wg_ring[s][:, g, k, :], xnT[:, k, COL_S:], start=(k == 0), stop=(k == KD - 1))
                    for g, y_ in ((0, yA), (1, yB)):
                        for k in range(T4):
                            last = mm(bk(4 * s + 2 + g, M), wo_ring[s][:, g, k, :], y_[:, k, :], start=(k == 0), stop=(k == T4 - 1))
                    last.then_inc(S["op_mm"], 1)
            pe.wait_ge(S["op_merge"], KD)
            with pe.Fori(0, KD // 2) as i:
                for s in range(2):
                    pe.wait_ge(S[f"ld_wf{s}"], 16 * i + 16)
                    pe.wait_ge(S["op_free"], KD + 2 * i + s + 1)
                    for k in range(KD):
                        last = mm(bk(s, M), wf_ring[s][:, k, :], merged[:, k, :], start=(k == 0), stop=(k == KD - 1))
                    last.then_inc(S["fin_mm"], 1)
            pe.wait_ge(S["rms_sq"], 2)
            for k in range(KD):
                last = mm(bk(7, M), K("ones"), acc[:, k, :], start=(k == 0), stop=(k == KD - 1))
            last.then_inc(S["rms_mm"], 1)
            pe.wait_ge(S["xt2"], 1)
            router = W("router").rearrange("p (k c) -> p k c", k=KD)
            for m in range(3):
                for k in range(KD):
                    last = mm(bank[6][:, m * 36:m * 36 + 36], xt2[:, k, m * P:m * P + P], router[:, k, :],
                              start=(k == 0), stop=(k == KD - 1))
            last.then_inc(S["rt_mm"], 1)
            pe.wait_ge(S["rt_member"], 1)
            for m in range(3):
                for q in range(m + 1):
                    last = mm(bank[6][:, m * E:m * E + E], K("before" if q == m else "ones"), member[:, q, :],
                              start=(q == 0), stop=(q == m))
            for m in range(3):
                last = mm(bank[6][:, 3 * E:4 * E], K("ones"), member[:, m, :], start=(m == 0), stop=(m == 2))
            last.then_inc(S["rt_pos"], 1)

            def dense():
                pe.wait_ge(S["gate"], 1)
                for m in range(3):
                    last = pe.transpose(bank[7][0:E, m * P:m * P + P], gate[:, m, 0:E], K("ident"))
                last.then_inc(S["gt_tr"], 1)
                pe.wait_ge(S["gateT"], 1)
                with pe.Fori(0, E // 2) as i:
                    for s in range(2):
                        e = 2 * i + s
                        pe.wait_ge(S["gsel"], e + 1)
                        mm(bk(6, M), K("ones")[0:E, :], gsel[s][0:E, :], start=True, stop=True).then_inc(S["gb_mm"], 1)
                        pe.wait_ge(S[f"ld_e{s}"], 16 * i + 16)
                        for f in range(4):
                            pe.wait_ge(S["gu_free"], 4 * e + f + 1)
                            for g in range(2):
                                for k in range(KD):
                                    last = mm(bk(2 * (f % 2) + g, M), wgu[s][:, g, k, f * P:f * P + P], xt2[:, k, 0:M],
                                              start=(k == 0), stop=(k == KD - 1))
                            last.then_inc(S["gu_mm"], 1)
                        pe.wait_ge(S[f"ld_d{s}"], 16 * i + 16)
                        pe.wait_ge(S["hid"], 4 * e + 4)
                        for j in range(KD):
                            pe.wait_ge(S["acc"], KD * e + j + 1)
                            for k in range(4):
                                last = mm(bk(4 + j % 2, M), wdn[s][:, k, j * P:j * P + P], hid[s][:, k, :], start=(k == 0), stop=(k == 3))
                            last.then_inc(S["dn_mm"], 1)

            def sparse():
                for m in range(3):
                    for half in range(2):
                        n = 2 * m + half
                        if n >= 4:
                            pe.wait_ge(S["xtok"], n - 3)
                        for k in range(4):
                            last = pe.transpose(bank[n % 4][:, k * P:k * P + P], xt2[:, 4 * half + k, m * P:m * P + P], K("ident"))
                        last.then_inc(S["xt_tr"], 1)
                pe.wait_ge(S["xtok"], 6)

                def gather(s):
                    for k in range(KD):
                        for m in range(3):
                            last = mm(bank[2][:, k * CAP:k * CAP + CAP], xtok[:, m, k * P:k * P + P], sel[:, m, s, :],
                                      start=(m == 0), stop=(m == 2))
                    last.then_inc(S["sp_gather"], 1)

                def gate_up(i, s, first):
                    pe.wait_ge(S[f"ld_e{s}"], 16 * i + 16)
                    pe.wait_ge(S["xe"], 2 * i + s + 1)
                    if not first:
                        pe.wait_ge(S["sp_hid"], 2 * i + s)
                    for g in range(2):
                        for f in range(4):
                            for k in range(KD):
                                last = mm(bank[g][:, f * CAP:f * CAP + CAP], wgu[s][:, g, k, f * P:f * P + P],
                                          xe[s][:, k, :], start=(k == 0), stop=(k == KD - 1))
                    last.then_inc(S["sp_gu"], 1)

                def down(i, s, first):
                    pe.wait_ge(S[f"ld_d{s}"], 16 * i + 16)
                    pe.wait_ge(S["sp_hid"], 2 * i + s + 1)
                    if not first:
                        pe.wait_ge(S["sp_yT"], 2 * i + s)
                    for j in range(KD):
                        for k in range(4):
                            last = mm(bank[3][:, j * CAP:j * CAP + CAP], wdn[s][:, k, j * P:j * P + P], hid_s[:, k, :],
                                      start=(k == 0), stop=(k == 3))
                    last.then_inc(S["sp_dn"], 1)

                def rows_of(i):
                    pe.wait_ge(S["sp_yT"], 2 * i)
                    pe.wait_ge(S["selT"], i)
                    for j in range(KD):
                        last = pe.transpose(bank[4 + j // 4][:, j % 4 * P:j % 4 * P + P], yT[:, j, :], K("ident"))
                    last.then_inc(S["sp_tr"], 1)

                def combine(i):
                    pe.wait_ge(S["sp_ye"], i)
                    for j in range(KD):
                        pe.wait_ge(S["sp_acc"], KD * (i - 1) + j + 1)
                        mm(bk(6 + j % 2, M), ye[:, j * P:j * P + P], selT[:, 0:M], start=True, stop=True).then_inc(S["sp_comb"], 1)

                def pair(i, first):
                    gate_up(i, 0, first)
                    gather(1)
                    if not first:
                        rows_of(i)
                    down(i, 0, first)
                    gate_up(i, 1, False)
                    if not first:
                        combine(i)
                    pe.wait_ge(S["sp_sel"], i + 2)
                    gather(0)
                    pe.wait_ge(S["sp_selg"], i + 1)
                    for m in range(3):
                        last = pe.transpose(bank[5][:, m * P:m * P + P], selG[:, m].rearrange("p s c -> p (s c)"), K("ident"))
                    last.then_inc(S["sp_selT"], 1)
                    down(i, 1, False)

                pe.wait_ge(S["sp_sel"], 1)
                gather(0)
                pair(0, True)
                with pe.Fori(1, E // 2) as i:
                    pair(i, False)
                rows_of(E // 2)
                combine(E // 2)

            pe.wait_ge(S["flag"], 1)
            crowded = pe.value_load(flag[0:1, 0:1], min_val=0, max_val=1)
            with pe.If(crowded < 1):
                sparse()
            with pe.Else():
                dense()
            pe.wait_ge(S["rms_sq"], 3)
            for k in range(KD):
                last = mm(bk(7, M), K("ones"), xt2[:, k, 0:M], start=(k == 0), stop=(k == KD - 1))
            last.then_inc(S["rms_mm"], 1)

        @block.scalar
        def _(act):
            A = nc.scalar.activation
            step = own(act, "act_own")
            act.wait_ge(S["ld_x"], 16)
            A(t_sq, xT[:, :, :], ACT.Square).then_inc(S["rms_sq"], 1)
            act.wait_ge(S["rms_mm"], 1)
            A(rs[:, :], bk(7, N), ACT.Sqrt, bias=K("eps"), scale=1.0 / D).then_inc(S["rms_root"], 1)
            act.sem_inc(S["psum_free"], 2)
            act.sem_inc(S["op_free"], 2)
            act.sem_inc(S["silu_done"], 2)
            with act.Fori(0, IN_T // 2) as i:
                for s in range(2):
                    act.wait_ge(S["proj_done"], 2 * i + s + 1)
                    A(proj[:, bass.ds(2 * i + s, 1), :], bk(s, 1, N), ACT.Copy).then_inc(S["psum_free"], 1)
            act.wait_ge(S["ab_done"], 2)
            A(ab_raw[0:4, :], bank[2][0:4, 0:N], ACT.Copy).then_inc(S["ab_sb"], 1)
            A(ab_raw[32:36, :], bank[3][32:36, 0:N], ACT.Copy).then_inc(S["ab_sb"], 1)
            act.wait_ge(S["zc_done"], 1)
            A(sgx, proj[:, 13, :], ACT.Sigmoid).then_inc(S["lora_in"], 1)
            A(xw, proj[0:C, 12, :], ACT.Tanh).then_inc(S["lora_in"], 1)
            for part, (dst, bias) in enumerate(((tL, "w0"), (ta, "a0"), (tg, None))):
                for t in range(T4):
                    act.wait_ge(S["lora_mm"], T4 * part + t + 1)
                    if bias:
                        ins = A(dst[:, t, :], bk(4 + t, N), ACT.Sigmoid, bias=W(bias)[:, t:t + 1])
                    else:
                        ins = A(dst[:, t, :], bk(4 + t, N)[:, COL_S:], ACT.Copy)
                    ins.then_inc(S["lora_out"], 1)
            act.wait_ge(S["cum"], 2)
            A(teL[:, :, :], tL[:, :, :], ACT.Exp).then_inc(S["exps"], 1)
            A(t1[:, :, :], t1[:, :, :], ACT.Exp).then_inc(S["exps"], 1)
            act.wait_ge(S["exps"], 1)
            A(tL[:, :, :], tL[:, :, :], ACT.Exp, scale=-1.0).then_inc(S["exps"], 1)
            act.wait_ge(S["head_sum"], 1)
            A(small_r[0:8, :], bank[3][0:8, 0:N], ACT.Sqrt, bias=K("eps")[0:8]).then_inc(S["head_root"], 1)
            for c in range(NC):
                act.wait_ge(S["v_tr"], c + 1)
                A(SV[C:P, c, :], bank[c % 2][C:P, :], ACT.Copy).then_inc(S["v_sb"], 1)
            for c in range(NC):
                act.wait_ge(S["bt_tr"], c + 1)
                A(BKt[:, c].rearrange("p a b -> p (a b)"), bank[c % 2][:, :], ACT.Copy).then_inc(S["bt_sb"], 1)
            jobs_done = [0]

            def invert(jobs):
                base = jobs_done[0]
                for pair in range(0, len(jobs), 2):
                    two = jobs[pair:pair + 2]
                    for level in range(1, LEVELS):
                        for q, (at_h, X, T1, XT_h, AT, XT) in enumerate(two):
                            n = base + pair + q
                            w_ = len(at_h) * C
                            act.wait_ge(S[f"inv_t1{q}"], LEVELS * slot_jobs[n] + level + 1)
                            A(T1[0:C].rearrange("p a b -> p (a b)")[:, 0:w_], bank[3 * q][0:C, 0:w_], ACT.Copy)\
                                .then_inc(S[f"inv_t1s{q}"], 1)
                jobs_done[0] += len(jobs)

            invert(jobs_r)
            act.wait_ge(S["s0_mm"], 1)
            c0 = bk(6, T4, 2, C)
            for x in range(2):
                step(A(C0r[:, :, x, COL_S:], c0[:, :, x, COL_S:], ACT.Copy))
            act.wait_ge(S["sv_zero"], 3)
            act.sem_inc(S["s0_sb"], 1)
            for c in range(NC):
                act.wait_ge(S["ch_rhs"], c + 1)
                A(Rs[0:C, :], bank[0][0:C, :], ACT.Copy).then_inc(S["ch_rhs_sb"], 1)
                act.wait_ge(S["ch_sa"], c + 1)
                A(SV[0:C, c, :], bank[1][0:C, :], ACT.Copy).then_inc(S["ch_sa_sb"], 1)
                act.wait_ge(S["ch_y"], c + 1)
                A(ty[:, :, c * C:c * C + C], bk(3, T4, C), ACT.Copy).then_inc(S["ch_y_sb"], 1)
            for t in range(T4):
                act.wait_ge(S["gn_in"], t + 1)
                ins = A(gn_sqv[:, t, :], ty[:, t, COL_S:], ACT.Square)
            ins.then_inc(S["head_sq"], 1)
            act.wait_ge(S["head_sum"], 2)
            A(small_r[0:8, 0:M], bank[3][0:8, 0:M], ACT.Sqrt, bias=K("gn_eps")[0:8], scale=1.0 / C).then_inc(S["head_root"], 1)

            nc.scalar.preload_act_table(ACT.Silu)
            with act.Fori(0, QKV_T // 2) as i:
                for s in range(2):
                    n = 2 * i + s
                    act.wait_ge(S["conv_done"], n + 1)
                    cv = conv_acc[s].unsqueeze(1)
                    dst = proj[:, bass.ds(n + RW_T, 1), :]
                    A(dst[:, :, COL_S:COL_P].rearrange("p a (b t) -> p (a b) t", t=TSEQ),
                      cv[:, :, 0:7 * NSEQ].rearrange("p a (b t) -> p (a b) t", t=7)[:, :, 0:TSEQ], ACT.Silu)
                    A(dst[:, :, COL_META:COL_S], cv[:, :, 56:56 + META], ACT.Silu)
                    A(dst[:, :, COL_P:], cv[:, :, 56 + META:], ACT.Silu).then_inc(S["silu_done"], 1)
            A(proj[:, RW_T + QKV_T:, :], proj[:, RW_T + QKV_T:, :], ACT.Silu).then_inc(S["z_done"], 1)
            act.wait_ge(S["rwkv_over"], 1)
            act.wait_ge(S["ab_rows"], 1)
            act.wait_ge(S["silu_done"], QKV_T + 2)
            A(sqg[:, 0:8, :], proj[:, RW_T:RW_T + 8, :], ACT.Square).then_inc(S["head_sq"], 1)
            A(rows[32:36, :], ab_raw[32:36, :], ACT.Sigmoid).then_inc(S["ab_lin"], 1)
            nc.scalar.preload_act_table_set("natural_log_exp_and_others")
            step(A(row_tmp[0:4, :], ab_raw[0:4, :], ACT.Abs, bias=W("dt_bias")[0:4]))
            step(A(row_tmp[0:4, :], row_tmp[0:4, :], ACT.Exp, scale=-1.0))
            step(A(row_tmp[0:4, :], row_tmp[0:4, :], ACT.Ln, bias=K("one")[0:4]))
            A(rs[0:4, 0:1], W("A_log")[0:4], ACT.Exp).then_inc(S["g_rows"], 1)
            act.wait_ge(S["g_cum"], 1)
            A(row_tmp[0:4, :], rows[0:4, :], ACT.Exp).then_inc(S["g_exp"], 1)
            for h in range(HG):
                act.wait_ge(S["g_bc"], 3 * h + 3)
                A(eGb[:, h, :], bk(6, N), ACT.Copy).then_inc(S["g_bc_act"], 1)
            act.wait_ge(S["cols_tr"], 1)
            tr = bank[7][0:C, 0:NC * 96].rearrange("p (c r) -> p c r", c=NC)
            step(A(cols[0:C, :, 0:96], tr, ACT.Copy))
            A(ecols[0:C, :, 0:4], tr[:, :, 0:4], ACT.Exp)
            A(ecols[0:C, :, 4:8], tr[:, :, 64:68], ACT.Exp).then_inc(S["ecol"], 1)
            act.wait_ge(S["d_arg"], 1)
            A(Dincl[0:C], Dincl[0:C], ACT.Exp).then_inc(S["d_exp"], 1)
            act.wait_ge(S["head_sum"], 3)
            A(srow[0:8, :], bank[0][0:8, 0:N], ACT.Sqrt, bias=K("eps")[0:8]).then_inc(S["head_root"], 1)
            invert(jobs_g)
            act.wait_ge(S["s0_mm"], 2)
            c0 = bk(6, HG, 2, C)
            step(A(C0g[:, :, 0, COL_S:], c0[:, :, 0, COL_S:], ACT.Copy))
            act.sem_inc(S["s0_k"], 1)
            act.wait_ge(S["sv_zero"], 5)
            act.sem_inc(S["s0_sb"], 1)
            for c in range(NC):
                act.wait_ge(S["ch_sa"], NC + c + 1)
                A(VN[0:C, :], bank[1][0:C, :], ACT.Copy).then_inc(S["ch_sa_sb"], 1)
                act.wait_ge(S["ch_y"], NC + c + 1)
                A(oT[:, :, c * C:c * C + C], bk(3, HG, C), ACT.Copy).then_inc(S["ch_y_sb"], 1)
            act.wait_ge(S["ch_y_sb"], 2 * NC)
            A(sqg_o, oT[:, :, COL_S:], ACT.Square).then_inc(S["head_sq"], 1)
            act.wait_ge(S["head_sum"], 4)
            A(srow[0:8, 0:M], bank[0][0:8, 0:M], ACT.Sqrt, bias=K("eps")[0:8], scale=1.0 / P).then_inc(S["head_root"], 1)

            nc.scalar.preload_act_table(ACT.Sigmoid)
            act.wait_ge(S["yB"], 1)
            with act.Fori(0, KD // 2) as i:
                for s in range(2):
                    act.wait_ge(S["op_mm"], 2 * i + s + 1)
                    act.wait_ge(S["op_free"], 2 * i + s + 1)
                    A(sgA[s], bk(4 * s, M), ACT.Sigmoid)
                    A(sgB[s], bk(4 * s + 1, M), ACT.Sigmoid).then_inc(S["op_sig"], 1)
            act.wait_ge(S["h_done"], KD)
            A(acc, hT, ACT.Square).then_inc(S["rms_sq"], 1)
            act.wait_ge(S["rms_mm"], 2)
            A(rs[:, 0:M], bk(7, M), ACT.Sqrt, bias=K("eps"), scale=1.0 / D).then_inc(S["rms_root"], 1)
            nc.scalar.preload_act_table(ACT.Exp)
            act.wait_ge(S["rt_sum"], 1)
            step(A(rt4, rt4, ACT.Exp))
            A(rt1[3], rt1[3], ACT.Exp).then_inc(S["rt_exp"], 1)
            def dense():
                act.wait_ge(S["gt_tr"], 1)
                A(gateT[0:E, :], bank[7][0:E, 0:3 * P], ACT.Copy).then_inc(S["gateT"], 1)
                nc.scalar.preload_act_table(ACT.Silu)
                with act.Fori(0, E // 2) as i:
                    for s in range(2):
                        for f in range(4):
                            act.wait_ge(S["gu_mm"], 8 * i + 4 * s + f + 1)
                            act.wait_ge(S["gu_free"], 8 * i + 4 * s + f + 1)
                            A(silu[f % 2], bk(2 * (f % 2), M), ACT.Silu).then_inc(S["silu"], 1)

            def sparse():
                for n in range(6):
                    act.wait_ge(S["xt_tr"], n + 1)
                    A(xtok[:, n // 2, n % 2 * 512:n % 2 * 512 + 512], bank[n % 4][:, :], ACT.Copy).then_inc(S["xtok"], 1)

                def take(e, s):
                    act.wait_ge(S["sp_gather"], e + 1)
                    A(xe[s].rearrange("p k c -> p (k c)"), bank[2][:, :], ACT.Copy).then_inc(S["xe"], 1)

                def silu_of(e):
                    act.wait_ge(S["sp_gu"], e + 1)
                    A(silu_s.rearrange("p f c -> p (f c)"), bk(0, 4 * CAP), ACT.Silu).then_inc(S["sp_silu"], 1)

                def rows_of(i):
                    act.wait_ge(S["sp_tr"], i)
                    for half in range(2):
                        ins = A(ye[:, half * 512:half * 512 + 512], bank[4 + half][:, :], ACT.Copy)
                    ins.then_inc(S["sp_ye"], 1)

                def pair(i, first):
                    silu_of(2 * i)
                    take(2 * i + 1, 1)
                    if not first:
                        rows_of(i)
                    silu_of(2 * i + 1)
                    take(2 * i + 2, 0)
                    act.wait_ge(S["sp_selT"], i + 1)
                    A(selT[:, 0:3 * P], bk(5, 3 * P), ACT.Copy).then_inc(S["selT"], 1)

                take(0, 0)
                nc.scalar.preload_act_table(ACT.Silu)
                pair(0, True)
                with act.Fori(1, E // 2) as i:
                    pair(i, False)
                rows_of(E // 2)

            act.wait_ge(S["flag"], 1)
            crowded = act.value_load(flag[0:1, 0:1], min_val=0, max_val=1)
            with act.If(crowded < 1):
                sparse()
            with act.Else():
                dense()
            act.wait_ge(S["moe_done"], 1)
            A(xt2[:, :, 0:M], acc, ACT.Square).then_inc(S["rms_sq"], 1)
            act.wait_ge(S["rms_mm"], 3)
            A(rs[:, 0:M], bk(7, M), ACT.Sqrt, bias=K("eps"), scale=1.0 / D).then_inc(S["rms_root"], 1)

        @block.gpsimd
        def _(pool):
            pool.wait_ge(S["ld_par"], 16)
            pool.wait_ge(S["xc_init"], 2)
            pool.wait_ge(S["psum_free"], 2 + IN_T)
            state = W("conv_state").rearrange("p (q b j) -> p q b j", q=QKV_T, b=NSEQ)
            out = conv_out
            with pool.Fori(0, QKV_T // 2) as i:
                for s in range(2):
                    n = 2 * i + s
                    pool.wait_ge(S["xc_used"], n + 1)
                    seqs = xc[s][:, 0:7 * NSEQ].rearrange("p (b t) -> p b t", t=7)
                    src = proj[:, bass.ds(n + RW_T, 1), :]
                    src_s = src[:, :, COL_S:COL_P].rearrange("p a (b t) -> p (a b) t", t=TSEQ)
                    cps = [
                        (seqs[:, :, 0:3], state[:, bass.ds(n, 1)].rearrange("p a b j -> p (a b) j")),
                        (seqs[:, :, 3:7], src_s),
                        (xc[s][:, 59:59 + META], src[:, :, COL_META:COL_S].rearrange("p a b -> p (a b)")),
                        (xc[s][:, 59 + META:], src[:, :, COL_P:].rearrange("p a b -> p (a b)")),
                        (out[:, bass.ds(n, 1), 0:24].rearrange("p a (b j) -> p (a b) j", j=3), src_s[:, :, 1:4]),
                        (out[:, bass.ds(n, 1), 24:27], src[:, :, N - 3:]),
                    ]
                    for d_, s_ in cps:
                        ins = nc.gpsimd.tensor_copy(d_, s_)
                        ins.then_inc(S["xc_step"], 1)
                    pool.wait_ge(S["xc_step"], 12 * i + 6 * s + 6)
                    pool.sem_inc(S["xc_ready"], 1)

        @block.vector
        def _(dve):
            V = nc.vector
            step = own(dve, "dve_own")
            TT, TS, STT, CP = V.tensor_tensor, V.tensor_scalar, V.scalar_tensor_tensor, V.tensor_copy
            step(V.memset(xc[0][:, 56:59], 0.0))
            step(V.memset(xc[1][:, 56:59], 0.0))
            dve.sem_inc(S["xc_init"], 2)
            dve.sem_inc(S["xc_used"], 2)
            dve.sem_inc(S["gu_free"], 2)
            dve.sem_inc(S["acc"], 2)
            dve.wait_ge(S["ld_par"], 16)
            dve.wait_ge(S["ld_cst"], 16)
            dve.wait_ge(S["rms_root"], 1)
            dve.wait_ge(S["ld_x"], 16)
            step(V.reciprocal(rs[:, :], rs[:, :]))
            for k in range(KD):
                last = STT(xnT[:, k, :], xT[:, k, :], W("norm1")[:, k:k + 1], rs[:, :], ALU.mult, ALU.mult)
            step(last)
            CP(xnT[:, :, 0:NSEQ], xT[:, :, 0:NSEQ]).then_inc(S["xn"], 1)
            dve.wait_ge(S["xn"], 1)
            CP(x_out[:, :, 0:NSEQ], xnT[:, :, COL_S + TSEQ - 1:COL_P:TSEQ])
            step(CP(x_out[:, :, NSEQ:], xnT[:, :, N - 1:]))
            dve.sem_inc(S["x_packed"], 1)
            step(V.memset(row_tmp[:, 0:1], 0.0))
            with dve.Fori(0, RW_T) as i:
                dve.wait_ge(S["psum_free"], i + 3)
                z = proj[:, bass.ds(i, 1), :].rearrange("p a b -> p (a b)")
                TT(row_tmp[:, 1:N], z[:, 0:N - 1], z[:, 1:N], ALU.subtract).then_inc(S["shift_step"], 1)
                dve.wait_ge(S["shift_step"], 4 * i + 1)
                TT(row_tmp[:, COL_S:COL_P:TSEQ], z[:, 0:NSEQ], z[:, COL_S:COL_P:TSEQ], ALU.subtract).then_inc(S["shift_step"], 1)
                TT(row_tmp[:, COL_P:COL_P + 1], z[:, COL_S - 1:COL_S], z[:, COL_P:COL_P + 1], ALU.subtract)\
                    .then_inc(S["shift_step"], 1)
                dve.wait_ge(S["shift_step"], 4 * i + 3)
                STT(z, row_tmp[:, :], W("mu")[:, bass.ds(i, 1)], z, ALU.mult, ALU.add).then_inc(S["shift_step"], 1)
                dve.wait_ge(S["shift_step"], 4 * i + 4)
            dve.sem_inc(S["zc_done"], 1)
            zr, zk, zv = proj[:, 0:4, :], proj[:, 4:8, :], proj[:, 8:12, :]
            step(TT(tkk[:, :, :], zk, spread(W("k_k"), N), ALU.mult))
            TT(t2[:, :, :], tkk[:, :, :], tkk[:, :, :], ALU.mult).then_inc(S["head_sq"], 1)
            dve.wait_ge(S["lora_out"], T4)
            step(TS(t1[:, :, :], tL[:, :, :], -float(np.exp(-0.5)), None, ALU.mult))
            for t in range(T4):
                last = V.tensor_tensor_scan(tL[:, t, :], K("carry"), t1[:, t, :], 0.0, ALU.mult, ALU.add)
            last.then_inc(S["cum"], 1)
            dve.wait_ge(S["cum"], 1)
            TT(t1[:, :, :], tL[:, :, :], t1[:, :, :], ALU.subtract).then_inc(S["cum"], 1)
            dve.wait_ge(S["head_root"], 1)
            V.reciprocal(small_r[0:8, :], small_r[0:8, :]).then_inc(S["head_inv"], 1)
            for t in range(T4):
                dve.wait_ge(S["head_spread"], t + 1)
                last = TT(tkk[:, t, :], tkk[:, t, :], bk(4 + t, N), ALU.mult)
            step(last)
            dve.wait_ge(S["exps"], 3)
            AR3 = AR.rearrange("p t c x s -> p (t c) x s")
            BK3 = BK.rearrange("p t c x s -> p (t c) x s")

            def ch(v):
                return v.rearrange("p t (c s) -> p (t c) s", s=C)

            step(STT(AR3[:, :, 0, :], ch(tkk), -1.0, ch(t1), ALU.mult, ALU.mult))
            step(TT(AR3[:, :, 1, :], ch(zr), ch(teL), ALU.mult))
            step(TT(t1[:, :, :], tkk[:, :, :], ta[:, :, :], ALU.mult))
            step(TT(BK3[:, :, 0, :], ch(t1), ch(tL), ALU.mult))
            step(STT(ta[:, :, :], ta[:, :, :], 1.0, spread(W("k_a"), N), ALU.subtract, ALU.mult))
            step(STT(ta[:, :, :], ta[:, :, :], 1.0, zk, ALU.add, ALU.mult))
            TT(BK3[:, :, 1, :], ch(ta), ch(tL), ALU.mult).then_inc(S["bk_done"], 1)
            CP(PTs[:, :, 1:NC], teL[:, :, 2 * C - 1:N:C])
            CP(PTs[:, :, 0:1], teL[:, :, COL_S - 1:COL_S])
            step(CP(PTs[:, :, NC:], teL[:, :, COL_S + TSEQ - 1:COL_P:TSEQ]))
            step(TT(t2[:, :, :], zr, ta[:, :, :], ALU.mult))
            TT(t2[:, :, :], t2[:, :, :], spread(W("r_k"), N), ALU.mult).then_inc(S["bonus_in"], 1)
            for t in range(T4):
                dve.wait_ge(S["bonus_mm"], t + 1)
                last = TT(tbonus[:, t, :], zv[:, t, :], bk(4 + t, N), ALU.mult)
            step(last)
            dve.sem_inc(S["z_dead"], 1)
            for c in range(NC):
                for p_, _ in halves:
                    n = 2 * c + p_
                    dve.wait_ge(S["gram_r"], n + 1)
                    TT(GM[:, c, p_::2, :], bk(4 + n % 4, T4, P), over(K("gmask0" if c == 0 else "gmask1"), T4), ALU.mult)\
                        .then_inc(S["gm_done"], 1)
            for x in range(2):
                TT(BK[:, :, 1:, x, :], BK[:, :, 1:, x, :], spread(PTs[:, :, 1:NC], C), ALU.mult)
                v = BK[:, :, 0, x, COL_S:].rearrange("p t (b s) -> p t b s", s=TSEQ)
                TT(v, v, spread(PTs[:, :, NC:], TSEQ), ALU.mult)
                v = BK[:, :, 0, x, COL_META:COL_S]
                last = TT(v, v, PTs[:, :, 0:1].to_broadcast([P, T4, META]), ALU.mult)
            step(last)
            dve.sem_inc(S["bar_done"], 1)
            V.memset(SV[0:C], 0.0).then_inc(S["sv_zero"], 1)
            dve.wait_ge(S["v_sb"], NC)
            for p_, rows_ in halves:
                last = V.memset(SW[rows_, :, :, (1 - p_) * C:(2 - p_) * C], 0.0)
            step(last)
            dve.sem_inc(S["z_dead"], 1)
            V.memset(C0r[:, :, :, 0:COL_S], 0.0).then_inc(S["sv_zero"], 1)
            V.memset(STr, 0.0).then_inc(S["sv_zero"], 1)

            jobs_done = [0]
            low = K("low").rearrange("p (l c) -> p l c", l=LEVELS).bitcast(I32)
            up = K("up").rearrange("p (l c) -> p l c", l=LEVELS).bitcast(I32)

            def invert(jobs):
                base = jobs_done[0]
                for pair in range(0, len(jobs), 2):
                    two = jobs[pair:pair + 2]
                    for q, (at_h, X, T1, XT_h, AT, XT) in enumerate(two):
                        n = base + pair + q
                        nh = len(at_h)
                        CP(X[0:C, 0:nh, :], over(K("ident")[0:C, 0:C], nh))
                        step(CP(XT, over(K("ident")[0:C, 0:C], nh)))
                        V.copy_predicated(XT, over(up[0:C, 0, :], nh), AT).then_inc(S[f"inv_upd{q}"], 1)
                    for level in range(LEVELS):
                        for q, (at_h, X, T1, XT_h, AT, XT) in enumerate(two):
                            n = base + pair + q
                            nh = len(at_h)
                            m_low, m_up = over(low[0:C, level, :], nh), over(up[0:C, level, :], nh)
                            if level == 0:
                                dve.wait_ge(S[f"inv_t1{q}"], LEVELS * slot_jobs[n] + 1)
                                V.copy_predicated(X[0:C, 0:nh, :], m_low, bk(3 * q, HR, C)[0:C, 0:nh, :])\
                                    .then_inc(S[f"inv_upd{q}"], 1)
                                continue
                            dve.wait_ge(S[f"inv_t2{q}"], (LEVELS - 1) * slot_jobs[n] + level)
                            if level < LEVELS - 1:
                                V.copy_predicated(X[0:C, 0:nh, :], m_low, bk(3 * q + 1, HR, C)[0:C, 0:nh, :])
                            V.copy_predicated(XT, m_up, bk(3 * q + 2, HR, C)[0:C, 0:nh, :]).then_inc(S[f"inv_upd{q}"], 1)
                jobs_done[0] += len(jobs)

            dve.wait_ge(S["gm_done"], 2 * NC)
            invert(jobs_r)
            for c in range(NC):
                if c == 0:
                    dve.wait_ge(S["ch_sa_sb"], 1)
                    dve.wait_ge(S["ld_sw"], 32)
                    dve.wait_ge(S["s0_mm"], 1)
                    for b in range(NSEQ + 1):
                        if b >= 2:
                            dve.wait_ge(S["sm_mm"], b - 1)
                        TS(SVm[b % 2], SV[:, 0, :], K("seq")[:, b:b + 1], None, ALU.mult).then_inc(S["svm"], 1)
                        if b < NSEQ:
                            for p_, rows_ in halves:
                                v = SW[rows_, b, :, p_ * C:p_ * C + C]
                                last = TT(v, v, spread(PTs[rows_, :, NC + b], C), ALU.mult)
                            step(last)
                        dve.wait_ge(S["sm_mm"], b + 1)
                        for p_, rows_ in halves:
                            src = bk(4 + b % 2, T4, P)[rows_, :, p_ * C:p_ * C + C]
                            if b < NSEQ:
                                v = SW[rows_, b, :, p_ * C:p_ * C + C]
                                last = TT(v, v, src, ALU.add)
                            else:
                                last = CP(STr[rows_, :, p_ * C:p_ * C + C], src)
                        last.then_inc(S["sm_sb" if b < NSEQ else "ch_st_sb"], 1)
                    continue
                dve.wait_ge(S["ch_st"], c)
                dve.wait_ge(S["ch_y"], c + 1)
                for p_, rows_ in halves:
                    v = STr[rows_, :, p_ * C:p_ * C + C]
                    last = TT(v, v, spread(PTs[rows_, :, c], C), ALU.mult)
                step(last)
                for p_, rows_ in halves:
                    v = STr[rows_, :, p_ * C:p_ * C + C]
                    last = TT(v, v, bk(2, T4, P)[rows_, :, p_ * C:p_ * C + C], ALU.add)
                last.then_inc(S["ch_st_sb"], 1)
            for t in range(T4):
                dve.wait_ge(S["gn_d"], t + 1)
                CP(ty[:, t, COL_S:], bk(4 + t, M)).then_inc(S["gn_in"], 1)
            dve.wait_ge(S["gn_in"], T4)
            dve.wait_ge(S["head_root"], 2)
            V.reciprocal(small_r[0:8, 0:M], small_r[0:8, 0:M]).then_inc(S["head_inv"], 1)
            for t in range(T4):
                dve.wait_ge(S["head_spread"], T4 + t + 1)
                y = ty[:, t, COL_S:]
                step(TT(y, y, bk(4 + t, M), ALU.mult))
                step(TS(y, y, W("ln_w")[:, t:t + 1], W("ln_b")[:, t:t + 1], ALU.mult, ALU.add))
            y = ty[:, :, COL_S:]
            step(TT(y, y, tbonus[:, :, COL_S:], ALU.add))
            TT(yA[:, :, :], y, tg[:, :, :], ALU.mult).then_inc(S["yA"], 1)

            cw = W("conv").rearrange("p (q j) -> p q j", q=QKV_T)
            with dve.Fori(0, QKV_T // 2) as i:
                for s in range(2):
                    n = 2 * i + s
                    dve.wait_ge(S["xc_ready"], n + 1)
                    dve.wait_ge(S["silu_done"], n + 1)
                    for j in range(4):
                        w_ = cw[:, bass.ds(n, 1), j]
                        x = xc[s][:, j:j + CONVN]
                        if j == 0:
                            ins = TS(conv_acc[s], x, w_, None, ALU.mult)
                        else:
                            ins = STT(conv_acc[s], x, w_, conv_acc[s], ALU.mult, ALU.add)
                        if j < 3:
                            ins.then_inc(S["conv_step"], 1)
                            dve.wait_ge(S["conv_step"], 6 * i + 3 * s + j + 1)
                    ins.then_inc(S["conv_done"], 1)
                    dve.wait_ge(S["conv_done"], n + 1)
                    dve.sem_inc(S["xc_used"], 1)
            dve.wait_ge(S["rwkv_over"], 1)
            step(V.memset(rows, 0.0))
            dve.sem_inc(S["ab_rows"], 1)
            step(TS(srow[0:4, :], ab_raw[0:4, :], W("dt_bias")[0:4], 0.0, ALU.add, ALU.max))
            dve.wait_ge(S["g_rows"], 1)
            step(TT(srow[0:4, :], srow[0:4, :], row_tmp[0:4, :], ALU.add))
            step(TS(srow[0:4, :], srow[0:4, :], rs[0:4, 0:1], -1.0, ALU.mult, ALU.mult))
            V.tensor_tensor_scan(rows[0:4, :], K("carry")[0:4], srow[0:4, :], 0.0, ALU.mult, ALU.add).then_inc(S["g_cum"], 1)
            dve.wait_ge(S["g_cum"], 1)
            g = rows[0:4, :]
            TT(rows[64:68, COL_P:].rearrange("p (c s) -> p c s", s=C),
               g[:, 2 * C - 1:N:C].unsqueeze(2).to_broadcast([4, NC - 1, C]),
               g[:, COL_P:].rearrange("p (c s) -> p c s", s=C), ALU.subtract)
            TT(rows[64:68, COL_META:COL_S], g[:, COL_S - 1:COL_S].to_broadcast([4, META]), g[:, COL_META:COL_S], ALU.subtract)
            step(TT(rows[64:68, COL_S:COL_P].rearrange("p (b s) -> p b s", s=TSEQ),
                    g[:, COL_S + TSEQ - 1:COL_P:TSEQ].unsqueeze(2).to_broadcast([4, NSEQ, TSEQ]),
                    g[:, COL_S:COL_P].rearrange("p (b s) -> p b s", s=TSEQ), ALU.subtract))
            dve.wait_ge(S["ab_lin"], 1)
            dve.wait_ge(S["g_exp"], 1)
            dve.sem_inc(S["g_kd"], 1)
            for h in range(HG):
                dve.wait_ge(S["g_bc"], 3 * h + 2)
                CP(Dincl[0:C, h, :], bank[4][0:C, 0:N]).then_inc(S["g_bc_dve"], 1)
                TT(Dstr[0:C, h, :], K("strict")[0:C], bank[5][0:C, 0:N], ALU.mult).then_inc(S["g_bc_dve"], 1)
            dve.wait_ge(S["ecol"], 1)
            dve.wait_ge(S["g_bc_dve"], 2 * HG)
            for h in range(HG):
                v = Dincl[0:C, h, :].rearrange("p (c s) -> p c s", s=C)
                last = TT(v, v, spread(cols[0:C, :, h], C), ALU.subtract)
            step(last)
            TS(Dincl[0:C], Dincl[0:C], 0.0, None, ALU.min).then_inc(S["d_arg"], 1)
            STT(cols[0:C, :, 96:100], cols[0:C, :, 32:36], -1.0, ecols[0:C, :, 0:4], ALU.mult, ALU.mult).then_inc(S["ecol2"], 1)
            dve.wait_ge(S["d_exp"], 1)
            step(TT(Dstr[0:C], Dstr[0:C], Dincl[0:C], ALU.mult))
            TT(Dincl[0:C], Dincl[0:C], over(K("incl")[0:C], HG), ALU.mult).then_inc(S["d_done"], 1)
            dve.wait_ge(S["head_root"], 3)
            V.reciprocal(srow[0:8, :], srow[0:8, :]).then_inc(S["head_inv"], 1)
            dve.wait_ge(S["silu_done"], QKV_T + 2)
            for t in range(8):
                dve.wait_ge(S["head_spread"], 2 * T4 + t + 1)
                src = proj[:, RW_T + t, :].rearrange("p (c s) -> p c s", s=C)
                ps = bk(1 + t % 2, NC, C)
                if t < 4:
                    ins = STT(KQ[:, t, :, 1, :], src, float(P ** -0.5), ps, ALU.mult, ALU.mult)
                else:
                    ins = TT(KQ[:, t - 4, :, 0, :], src, ps, ALU.mult)
                ins.then_inc(S["kq_done"], 1)
            dve.wait_ge(S["kq_done"], 8)
            dve.wait_ge(S["g_bc_act"], HG)
            for h in range(HG):
                last = TT(qdec[:, h, :].rearrange("p (c s) -> p c s", s=C), KQ[:, h, :, 1, :],
                          eGb[:, h, :].rearrange("p (c s) -> p c s", s=C), ALU.mult)
            step(last)
            for c in range(NC):
                for w_ in range(2):
                    n = 2 * c + w_
                    dve.wait_ge(S["kv_tr"], n + 1)
                    col = ecols[0:C, c, 4:8] if w_ == 0 else cols[0:C, c, 32:36]
                    TT((kdec, bV)[w_][0:C, c], bk(n % 2, HG, P)[0:C], spread(col, P), ALU.mult).then_inc(S["kv_sb"], 1)
            for c in range(NC):
                dve.wait_ge(S["gram_g"], c + 1)
                ps = bk(2 + c % 2, HG, 2, C)[0:C]
                TT(GA[0:C, c], ps[:, :, 0, :], Dstr[0:C, :, c * C:c * C + C], ALU.mult)
                TT(QKD[0:C, c], ps[:, :, 1, :], Dincl[0:C, :, c * C:c * C + C], ALU.mult).then_inc(S["ga_done"], 1)
            V.memset(C0g[:, :, :, 0:COL_S], 0.0).then_inc(S["sv_zero"], 1)
            dve.wait_ge(S["ga_done"], NC)
            invert(jobs_g)
            dve.wait_ge(S["s0_k"], 1)
            TT(C0g[:, :, 1, COL_S:], bk(6, HG, 2, C)[:, :, 1, COL_S:], eGb[:, :, COL_S:COL_P], ALU.mult).then_inc(S["sv_zero"], 1)
            for c in range(NC):
                dve.wait_ge(S["ch_rhs"], NC + c + 1)
                step(TT(Rg[0:C], bk(0, HG, P)[0:C], spread(cols[0:C, c, 96:100], P), ALU.mult))
                TT(Rg[0:C], Rg[0:C], bV[0:C, c], ALU.add).then_inc(S["ch_rhs_sb"], 1)
                if c == 0:
                    dve.wait_ge(S["ch_sa_sb"], NC + 1)
                    dve.wait_ge(S["ld_sw"], 48)
                    for b in range(NSEQ + 1):
                        if b >= 2:
                            dve.wait_ge(S["sm_mm"], NSEQ + 1 + b - 1)
                        TS(VNm[b % 2][0:C], VN[0:C, :], K("seq")[0:C, b:b + 1], None, ALU.mult).then_inc(S["svm"], 1)
                        if b < NSEQ:
                            lo = COL_S + TSEQ * b + TSEQ - 1
                            step(TT(SW[:, b], SW[:, b], eGb[:, :, lo:lo + 1].to_broadcast([P, HG, P]), ALU.mult))
                        dve.wait_ge(S["sm_mm"], NSEQ + 1 + b + 1)
                        if b < NSEQ:
                            TT(SW[:, b], SW[:, b], bk(4 + b % 2, HG, P), ALU.add).then_inc(S["sm_sb"], 1)
                        else:
                            CP(Sg, bk(4 + b % 2, HG, P)).then_inc(S["ch_st_sb"], 1)
                    continue
                dve.wait_ge(S["ch_st"], NC - 1 + c)
                dve.wait_ge(S["ch_y"], NC + c + 1)
                lo = c * C + C - 1
                step(TT(Sg, Sg, eGb[:, :, lo:lo + 1].to_broadcast([P, HG, P]), ALU.mult))
                TT(Sg, Sg, bk(2, HG, P), ALU.add).then_inc(S["ch_st_sb"], 1)
            dve.wait_ge(S["head_root"], 4)
            V.reciprocal(srow[0:8, 0:M], srow[0:8, 0:M]).then_inc(S["head_inv"], 1)
            dve.wait_ge(S["z_done"], 1)
            for h in range(HG):
                dve.wait_ge(S["head_spread"], 2 * T4 + 8 + h + 1)
                o = oT[:, h, COL_S:]
                step(STT(o, o, W("gdn_norm"), bk(4 + h, M), ALU.mult, ALU.mult))
            TT(yB[:, :, :], oT[:, :, COL_S:], proj[:, RW_T + QKV_T:, COL_S:], ALU.mult).then_inc(S["yB"], 1)

            with dve.Fori(0, KD // 2) as i:
                for s in range(2):
                    n = 2 * i + s
                    dve.wait_ge(S["op_sig"], n + 1)
                    TT(sgA[s], sgA[s], bk(4 * s + 2, M), ALU.mult).then_inc(S["moe_own"], 1)
                    TT(sgB[s], sgB[s], bk(4 * s + 3, M), ALU.mult).then_inc(S["moe_own"], 1)
                    dve.wait_ge(S["moe_own"], 4 * i + 2 * s + 2)
                    TT(merged[:, bass.ds(n, 1), :], sgA[s].unsqueeze(1), sgB[s].unsqueeze(1), ALU.add).then_inc(S["op_merge"], 1)
                    dve.wait_ge(S["op_merge"], n + 1)
                    dve.sem_inc(S["op_free"], 1)
            with dve.Fori(0, KD // 2) as i:
                for s in range(2):
                    n = 2 * i + s
                    dve.wait_ge(S["fin_mm"], n + 1)
                    TT(hT[:, bass.ds(n, 1), :], xT[:, bass.ds(n, 1), COL_S:], bk(s, 1, M), ALU.add).then_inc(S["h_done"], 1)
                    dve.wait_ge(S["h_done"], n + 1)
                    dve.sem_inc(S["op_free"], 1)
            V.memset(xt2[:, :, M:], 0.0)
            dve.wait_ge(S["rms_root"], 2)
            step(V.reciprocal(rs[:, 0:M], rs[:, 0:M]))
            for k in range(KD):
                last = STT(xt2[:, k, 0:M], hT[:, k, :], W("norm2")[:, k:k + 1], rs[:, 0:M], ALU.mult, ALU.mult)
            last.then_inc(S["xt2"], 1)
            dve.wait_ge(S["rt_mm"], 1)
            step(TT(rt, bk(6, 3, 36), over(W("router_b"), 3), ALU.add))
            gl = rt[:, :, 0:G]
            el = rt[:, :, G:].rearrange("p m (g e) -> p m g e", g=G)
            gm, den, m1, m2, w1, w2, tmp = rt1

            def first_of(dst, src, top, order, n):
                step(TT(dst, src, spread(top, n), ALU.is_equal))
                step(TT(dst, dst, over(order, 3), ALU.mult))
                step(V.tensor_reduce(tmp, dst, AX.X, ALU.max))
                step(TT(dst, dst, spread(tmp, n), ALU.is_equal))

            ohg, oh1, oh2, ev = rt8[0][:, :, 0:G], rt8[1], rt8[2], rt8[3]
            step(V.tensor_reduce(gm, gl, AX.X, ALU.max))
            step(TT(rt4, gl, spread(gm, G), ALU.subtract))
            first_of(ohg, gl, gm, K("first4"), G)
            for m in range(3):
                last = TT(rte[:, m], el[:, m], spread(ohg[:, m], EG), ALU.mult)
            step(last)
            step(V.tensor_reduce(ev, rte.rearrange("p m g e -> p m e g"), AX.X, ALU.add))
            step(V.tensor_reduce(m1, ev, AX.X, ALU.max))
            first_of(oh1, ev, m1, K("first8"), EG)
            step(STT(ev, oh1, -1e30, ev, ALU.mult, ALU.add))
            step(V.tensor_reduce(m2, ev, AX.X, ALU.max))
            first_of(oh2, ev, m2, K("first8"), EG)
            step(TT(m2, m2, m1, ALU.subtract))
            dve.sem_inc(S["rt_sum"], 1)
            step(TT(ev, oh1, oh2, ALU.add))
            step(TT(ev, ev, spread(K("valid"), EG), ALU.mult))
            for m in range(3):
                last = TT(member[:, m].rearrange("p (g e) -> p g e", g=G), spread(ohg[:, m], EG), over(ev[:, m], G), ALU.mult)
            last.then_inc(S["rt_member"], 1)
            V.memset(slot, -1.0)
            V.memset(gate, 0.0)
            dve.wait_ge(S["rt_exp"], 1)
            step(V.tensor_reduce(den, rt4, AX.X, ALU.add))
            step(STT(w1, m2, 1.0, den, ALU.add, ALU.mult))
            step(V.reciprocal(w1, w1))
            step(TT(w2, w1, m2, ALU.mult))
            step(TT(oh1, oh1, spread(w1, EG), ALU.mult))
            step(TT(oh2, oh2, spread(w2, EG), ALU.mult))
            step(TT(oh1, oh1, oh2, ALU.add))
            for m in range(3):
                last = TT(gate[:, m, 0:E].rearrange("p (g e) -> p g e", g=G), spread(ohg[:, m], EG), over(oh1[:, m], G), ALU.mult)
            last.then_inc(S["gate"], 1)
            dve.wait_ge(S["rt_pos"], 1)
            step(STT(slot[:, :, 0:E], bk(6, 3, E), 1.0, member, ALU.add, ALU.mult))
            step(TS(slot[:, :, 0:E], slot[:, :, 0:E], -1.0, None, ALU.add))
            step(V.tensor_reduce(flag_f, bank[6][:, 3 * E:4 * E], AX.X, ALU.max))
            TS(flag, flag_f, CAP + 0.5, None, ALU.is_gt).then_inc(S["flag"], 1)
            CP(acc, hT).then_inc(S["acc_init"], 1)
            dve.wait_ge(S["acc_init"], 1)

            def dense():
                dve.wait_ge(S["gateT"], 1)
                for s in range(2):
                    TS(gsel[s][0:E], gateT[0:E, 0:M], K("ident")[0:E, s:s + 1], None, ALU.mult).then_inc(S["gsel"], 1)
                with dve.Fori(0, E // 2) as i:
                    for s in range(2):
                        e = 2 * i + s
                        dve.wait_ge(S["gb_mm"], e + 1)
                        for f in range(4):
                            dve.wait_ge(S["silu"], 4 * e + f + 1)
                            TT(hid[s][:, f, :], silu[f % 2], bk(2 * (f % 2) + 1, M), ALU.mult).then_inc(S["hid_step"], 1)
                            dve.wait_ge(S["hid_step"], 8 * i + 4 * s + f + 1)
                            TT(hid[s][:, f, :], hid[s][:, f, :], bk(6, M), ALU.mult).then_inc(S["hid"], 1)
                            dve.wait_ge(S["hid"], 4 * e + f + 1)
                            dve.sem_inc(S["gu_free"], 1)
                        TS(gsel[s][0:E], gateT[0:E, 0:M], K("ident")[0:E, bass.ds(e + 2, 1)], None, ALU.mult).then_inc(S["gsel"], 1)
                        for j in range(KD):
                            dve.wait_ge(S["dn_mm"], KD * e + j + 1)
                            TT(acc[:, j, :], acc[:, j, :], bk(4 + j % 2, M), ALU.add).then_inc(S["acc"], 1)

                dve.wait_ge(S["acc"], 2 + KD * E)
                dve.sem_inc(S["moe_done"], 1)

            def sparse():
                dve.sem_inc(S["sp_acc"], 2)

                def select(i):
                    for s in range(2):
                        ins = TT(sel[:, :, s, :], over(K("iota"), 3),
                                 slot[:, :, bass.ds(2 * i + s, 1)].to_broadcast([P, 3, CAP]), ALU.is_equal)
                    ins.then_inc(S["sp_sel"], 1)

                def weigh(i):
                    for s in range(2):
                        ins = TT(selG[:, :, s, :], sel[:, :, s, :],
                                 gate[:, :, bass.ds(2 * i + s, 1)].to_broadcast([P, 3, CAP]), ALU.mult)
                    ins.then_inc(S["sp_selg"], 1)

                def hidden(e):
                    dve.wait_ge(S["sp_silu"], e + 1)
                    TT(hid_s.rearrange("p f c -> p (f c)"), silu_s.rearrange("p f c -> p (f c)"), bk(1, 4 * CAP), ALU.mult)\
                        .then_inc(S["sp_hid"], 1)

                def result(e, s):
                    dve.wait_ge(S["sp_dn"], e + 1)
                    CP(yT[:, :, s * CAP:s * CAP + CAP], bk(3, KD, CAP)).then_inc(S["sp_yT"], 1)

                def add(i):
                    for j in range(KD):
                        dve.wait_ge(S["sp_comb"], KD * (i - 1) + j + 1)
                        TT(acc[:, j, :], acc[:, j, :], bk(6 + j % 2, M), ALU.add).then_inc(S["sp_acc"], 1)

                def pair(i, first):
                    hidden(2 * i)
                    dve.wait_ge(S["sp_gather"], 2 * i + 2)
                    dve.wait_ge(S["sp_selg"], i + 1)
                    select(i + 1)
                    result(2 * i, 0)
                    hidden(2 * i + 1)
                    if not first:
                        add(i)
                        dve.wait_ge(S["sp_acc"], KD * i + 2)
                    dve.wait_ge(S["sp_selT"], i + 1)
                    dve.wait_ge(S["sp_sel"], i + 2)
                    weigh(i + 1)
                    result(2 * i + 1, 1)

                select(0)
                dve.wait_ge(S["sp_sel"], 1)
                weigh(0)
                pair(0, True)
                with dve.Fori(1, E // 2) as i:
                    pair(i, False)
                add(E // 2)
                dve.wait_ge(S["sp_acc"], KD * (E // 2) + 2)
                dve.sem_inc(S["moe_done"], 1)

            dve.wait_ge(S["flag"], 1)
            dve.wait_ge(S["gate"], 1)
            crowded = dve.value_load(flag[0:1, 0:1], min_val=0, max_val=1)
            with dve.If(crowded < 1):
                sparse()
            with dve.Else():
                dense()
            dve.wait_ge(S["rms_root"], 3)
            step(V.reciprocal(rs[:, 0:M], rs[:, 0:M]))
            for k in range(KD):
                last = STT(acc[:, k, :], acc[:, k, :], W("normf")[:, k:k + 1], rs[:, 0:M], ALU.mult, ALU.mult)
            last.then_inc(S["y_ready"], 1)


SHAPES = dict(
    xT=(P, KD, N), cst=(P, CST.width), par=(P, PAR.width), w_in=(IN_T, P, KD, P), wkv_in=(P, NSEQ, T4, C),
    gdn_in=(P, NSEQ, HG, P), w_gab=(KD, P, 2, KD, P), w_oab=(KD, P, 2, T4, P), w_o=(KD, P, KD, P),
    w_gu=(E, P, 2, KD, FF), w_dn=(E, P, 4, D))
OUT_SHAPES = dict(
    y=(P, KD, M), shift_out=(P, KD, NSEQ + 1), wkv_p=(P, T4, C), wkv_s=(P, NSEQ, T4, C), conv_out=(P, QKV_T, 27),
    gdn_p=(P, HG, P), gdn_s=(P, NSEQ, HG, P))


def kernel(**inputs):
    import concourse.bacc as bacc
    from concourse.bass_utils import run_bass_kernel_spmd as run

    x = {k: np.asarray(v) for k, v in inputs.items()}

    def feat(a):
        a = a.reshape(a.shape[0] // P, P, -1)
        return a.transpose(1, 0, 2).reshape(P, -1)

    tokens = np.concatenate([x["state_shift"][0], np.zeros((NSEQ, D), np.float32), x["meta_tokens"],
                             x["x_sample"].reshape(-1, D), x["x_prompt"][0]])
    par = np.zeros((P, PAR.width), np.float32)

    def put(name, a, row=0):
        a = a.reshape(a.shape[0], -1)
        lo = PAR.at[name][0]
        par[row:row + a.shape[0], lo:lo + a.shape[1]] = a

    w_in = x["w_in"][0]
    cut = IN_T * P
    put("norm1", feat(x["norm1_w"][0]))
    put("norm2", feat(x["norm2_w"][0]))
    put("normf", feat(x["norm_f_w"]))
    put("mu", feat(x["mu_shift"][0]))
    for name, key in (("w0", "rw_w0"), ("a0", "rw_a0"), ("k_k", "rw_k_k"), ("k_a", "rw_k_a"), ("r_k", "rw_r_k"),
                      ("ln_w", "rw_lnx_w"), ("ln_b", "rw_lnx_b")):
        put(name, feat(x[key][0].reshape(-1)))
    put("conv", feat(x["gdn_conv_w"][0].T))
    put("gdn_norm", x["gdn_norm_w"][0][:, None])
    put("A_log", x["gdn_A_log"][0][:, None])
    put("dt_bias", x["gdn_dt_bias"][0][:, None])
    put("w2a2", x["rw_w2"][0])
    put("w2a2", x["rw_a2"][0], C)
    put("g2", x["rw_g2"][0])
    put("ab", feat(w_in[:, cut:cut + 8]))
    put("router", feat(np.concatenate([x["router_g"][0], x["router_e"][0]], 1)))
    put("router_b", np.broadcast_to(np.concatenate([x["router_g_b"][0], x["router_e_b"][0]]), (P, 36)))
    put("conv_state", feat(x["state_conv"][0].transpose(2, 0, 1).reshape(QKV_T * P, NSEQ * 3)))

    def tiles(w):
        return w.reshape(w.shape[0] // P, P, w.shape[1] // P, P).transpose(2, 1, 0, 3)

    gates = cut + 8
    wg, wu = (x[f"moe_w_{n}"][0].reshape(E, KD, P, FF).transpose(0, 2, 1, 3) for n in ("gate", "up"))
    arrays = dict(
        xT=feat(tokens.T).reshape(P, KD, N), cst=constants(), par=par, w_in=tiles(w_in[:, :cut]),
        wkv_in=x["state_wkv"][0].reshape(NSEQ, T4, 2, C, C).transpose(2, 4, 0, 1, 3).reshape(P, NSEQ, T4, C),
        gdn_in=x["state_gdn"][0].transpose(2, 0, 1, 3),
        w_gab=np.stack([tiles(w_in[:, gates:gates + D]), tiles(w_in[:, gates + D:])], 2),
        w_oab=np.stack([tiles(x["w_oA"][0]), tiles(x["w_oB"][0])], 2), w_o=tiles(x["w_o"][0]),
        w_gu=np.stack([wg, wu], 2), w_dn=x["moe_w_down"][0].reshape(E, 4, P, D).transpose(0, 2, 1, 3))
    nc = bacc.Bacc("TRN2", target_bir_lowering=False, num_devices=1)
    dram = {}
    for name, shape in SHAPES.items():
        arrays[name] = np.ascontiguousarray(arrays[name])
        assert arrays[name].shape == shape, (name, arrays[name].shape, shape)
        dram[name] = nc.dram_tensor(name, shape, F32, kind="ExternalInput").ap()
    for name, shape in OUT_SHAPES.items():
        dram[name] = nc.dram_tensor(name, shape, F32, kind="ExternalOutput").ap()
    build(nc, dram)
    r = run(nc, [arrays], core_ids=[0]).results[0]
    y = r["y"].transpose(2, 1, 0).reshape(M, D)
    shift = r["shift_out"].transpose(2, 1, 0).reshape(NSEQ + 1, D)
    conv = r["conv_out"].transpose(2, 1, 0).reshape(NSEQ + 1, 3, QKV_T * P)
    wkv_p = r["wkv_p"].reshape(2, C, T4, C).transpose(2, 0, 3, 1).reshape(1, 1, HR, C, C)
    wkv_s = r["wkv_s"].reshape(2, C, NSEQ, T4, C).transpose(2, 3, 0, 4, 1).reshape(1, NSEQ, HR, C, C)
    return (y[32:][None], y[:32].reshape(NSEQ, TSEQ, D), shift[None, NSEQ:], wkv_p, conv[None, NSEQ:],
            r["gdn_p"].transpose(1, 0, 2)[None, None], shift[None, :NSEQ], wkv_s, conv[None, :NSEQ],
            r["gdn_s"].transpose(1, 2, 0, 3)[None])
```

```python
from contextlib import ExitStack

import numpy as np

import concourse.bass as bass
from concourse import mybir

F32 = mybir.dt.float32
I32 = mybir.dt.int32
ACT = mybir.ActivationFunctionType
ALU = mybir.AluOpType
AX = mybir.AxisListType

P = 128
D = 1024
KD = D // P
NSEQ, TSEQ, META, SEQ = 8, 4, 16, 256
C = 64
COL_META, COL_S, COL_P = 16, 32, 64
N = COL_P + SEQ
NC = N // C
M = N - COL_S
RW_T, QKV_T, Z_T = 14, 12, 4
IN_T = RW_T + QKV_T + Z_T
HR, HG = 8, 4
T4 = 4
G, EG, E, FF = 4, 8, 32, 512
LEVELS = 6
SEG = (RW_T // 2, 9, 11, 13)
CAP = 64
E2 = E + 4
XC = 7 * NSEQ + 3 + META + SEQ
CONVN = XC - 3


class Cols:

    def __init__(self):
        self.at, self.width = {}, 0

    def add(self, name, n):
        self.at[name] = (self.width, self.width + n)
        self.width += n


CST = Cols()
for _name, _n in (("ident", P), ("ones", P), ("blockones", P), ("center", P), ("sum_r", T4 * 8),
                  ("spread_r", T4 * P), ("sum_g", 8 * 8), ("spread_g", 8 * P), ("gmask0", P),
                  ("gmask1", P), ("incl", N), ("strict", N), ("low", LEVELS * C), ("up", LEVELS * C),
                  ("seq", NSEQ + 1), ("carry", N), ("eps", 1), ("gn_eps", 1), ("one", 1),
                  ("first4", 4), ("first8", 8), ("before", P), ("iota", CAP), ("valid", 3)):
    CST.add(_name, _n)
PAR = Cols()
for _name, _n in (("norm1", KD), ("norm2", KD), ("normf", KD), ("mu", RW_T), ("w0", T4), ("a0", T4),
                  ("k_k", T4), ("k_a", T4), ("r_k", T4), ("ln_w", T4), ("ln_b", T4), ("conv", QKV_T * 4),
                  ("gdn_norm", 1), ("A_log", 1), ("dt_bias", 1), ("w2a2", 512), ("g2", 512), ("ab", KD * 8),
                  ("router", KD * 36), ("router_b", 36), ("conv_state", QKV_T * 24)):
    PAR.add(_name, _n)


def constants():
    c = np.zeros((P, CST.width), np.float32)

    def put(name, a, row=0):
        a = np.asarray(a, np.float32).reshape(len(a), -1)
        c[row:row + a.shape[0], CST.at[name][0]:CST.at[name][1]] = a

    i = np.arange(P)
    same = (i[:, None] // C == i[None] // C).astype(np.float32)
    put("ident", np.eye(P))
    put("ones", np.ones((P, P)))
    put("blockones", same)
    put("center", np.eye(P) - same / C)
    t, h = np.arange(T4), np.arange(8)
    put("sum_r", (2 * t[None, :, None] + (i // C)[:, None, None] == h[None, None]).astype(np.float32))
    put("spread_r", (h[:, None, None] == 2 * t[None, :, None] + (i // C)[None, None]).astype(np.float32))
    put("sum_g", np.broadcast_to((h[:, None] == h[None]), (P, 8, 8)))
    spread = np.broadcast_to((h[:, None, None] == h[None, :, None]), (8, 8, P))
    put("spread_g", spread)
    put("spread_g", spread, 32)
    seq = np.full(C, -1)
    seq[COL_META:COL_S] = NSEQ
    seq[COL_S:C] = np.arange(32) // TSEQ
    j = np.arange(C)
    together = [(seq[:, None] == seq[None]) & (seq[:, None] >= 0)] + [np.ones((C, C), bool)] * (NC - 1)
    incl = [g & (j[:, None] <= j[None]) for g in together]
    strict = [g & (j[:, None] < j[None]) for g in together]
    for n in (0, 1):
        put(f"gmask{n}", np.tile(np.concatenate([strict[n], incl[n]], 1), (2, 1)))
    put("incl", np.concatenate(incl, 1))
    put("strict", -np.concatenate(strict, 1).astype(np.float32))
    low = np.stack([(j[:, None] >> (n + 1) == j[None] >> (n + 1)) & (j[:, None] >> n & 1 == 1) & (j[None] >> n & 1 == 0)
                    for n in range(LEVELS)], 1)
    put("low", np.tile(low, (2, 1, 1)))
    put("up", np.tile(low.transpose(2, 1, 0), (2, 1, 1)))
    put("seq", np.tile(seq[:, None] == np.arange(NSEQ + 1)[None], (2, 1)))
    carry = np.ones(N)
    carry[[COL_META, *range(COL_S, C, TSEQ), *range(C, N, C)]] = 0
    put("carry", np.tile(carry, (P, 1)))
    put("eps", np.full(P, 1e-6))
    put("gn_eps", np.full(P, C * 1e-5))
    put("one", np.ones(P))
    put("first4", np.tile(np.arange(4, 0, -1), (P, 1)))
    put("first8", np.tile(np.arange(8, 0, -1), (P, 1)))
    put("before", i[:, None] < i[None])
    put("iota", np.tile(np.arange(CAP), (P, 1)))
    put("valid", i[:, None] + P * np.arange(3)[None] < M)
    return c


def build(nc, dram):
    ctx = ExitStack()
    with ctx:
        def sb(name, *shape):
            return ctx.enter_context(nc.sbuf_tensor(f"sb_{name}", [P, *shape], F32))

        def sem(name):
            return ctx.enter_context(nc.semaphore(name))

        cst = sb("cst", CST.width)
        par = sb("par", PAR.width)

        def K(name):
            return cst[:, CST.at[name][0]:CST.at[name][1]]

        def W(name):
            return par[:, PAR.at[name][0]:PAR.at[name][1]]

        def spread(ap, n):
            return ap.unsqueeze(len(ap.shape)).to_broadcast([*ap.shape, n])

        def over(ap, n):
            return ap.unsqueeze(1).to_broadcast([ap.shape[0], n, *ap.shape[1:]])

        xT = sb("xT", KD, N)
        yA = sb("yA", T4, M)
        yB = sb("yB", T4, M)
        rs = sb("rs", N)
        row_tmp = sb("row_tmp", N)
        ab_raw = sb("ab_raw", N)
        ARENA = 41100
        arena = sb("arena", ARENA)

        def at(start, *shape):
            n = int(np.prod(shape))
            assert start + n <= ARENA, (start, shape)
            v = arena[:, start:start + n]
            if len(shape) > 1:
                names = "abcde"[:len(shape)]
                v = v.rearrange(f"p ({' '.join(names)}) -> p {' '.join(names)}", **dict(zip(names, shape)))
            return v

        class Region:

            def __init__(self, start):
                self.pos = start

            def take(self, *shape):
                v = at(self.pos, *shape)
                self.pos += int(np.prod(shape))
                return v

        r = Region(0)
        xnT = r.take(KD, N)
        w_ring = [r.take(KD, P) for _ in range(2)]
        proj_at = r.pos
        proj = r.take(IN_T, N)
        xc = [r.take(XC) for _ in range(2)]
        conv_acc = [r.take(CONVN) for _ in range(2)]
        conv_out = r.take(QKV_T, 27)
        x_out = r.take(KD, NSEQ + 1)
        work_at = r.pos
        r = Region(work_at)
        temps_at = r.pos
        ta, tL, teL, tkk, t1, t2 = [r.take(T4, N) for _ in range(6)]
        tbonus = r.take(T4, N)
        tg = yB
        AR = r.take(T4, NC, 2, C)
        bk_at = r.pos
        BK = r.take(T4, NC, 2, C)
        GM = r.take(NC, HR, P)
        SV = r.take(NC, HR * C)
        BKt = r.take(NC, T4, P)
        PTs = r.take(T4, NC + NSEQ)
        small_r = rs
        r_end = r.pos
        r = Region(temps_at)
        XTr = r.take(NC, HR, C)
        invX = [r.take(T4, P) for _ in range(2)]
        invT = [r.take(T4, P) for _ in range(2)]
        Rs = r.take(HR * C)
        C0r = r.take(T4, 2, C)
        SVm = [r.take(HR * C) for _ in range(2)]
        STr = r.take(T4, P)
        assert r.pos <= temps_at + 6 * T4 * N
        r = Region(bk_at)
        ty, gn_sqv = r.take(T4, N), r.take(T4, M)
        r = Region(KD * N)
        invA, invXT = [r.take(T4, P) for _ in range(2)], [r.take(T4, P) for _ in range(2)]
        assert r.pos <= proj_at
        SW = at(proj_at, NSEQ, T4, P)
        assert NSEQ * T4 * P <= RW_T * N
        r = Region(work_at)
        KQ = r.take(HG, NC, 2, C)
        qdec = r.take(HG, N)
        eGb = r.take(HG, N)
        Dincl = r.take(HG, N)
        Dstr = r.take(HG, N)
        GA = r.take(NC, HG, C)
        QKD = r.take(NC, HG, C)
        sqg = at(r.pos, 8, N)
        kdec = r.take(NC, HG, P)
        bV = r.take(NC, HG, P)
        XTg = r.take(NC, HG, C)
        invXg, invTg = ([r.take(T4, P) for _ in range(2)] for _ in range(2))
        Rg = r.take(HG, P)
        VN = r.take(HG * P)
        VNm = [r.take(HG * P) for _ in range(2)]
        Sg = r.take(HG, P)
        C0g = r.take(HG, 2, C)
        rows = r.take(N)
        srow = r.take(N)
        cols = r.take(NC, P)
        ecols = r.take(NC, 8)
        oT = r.take(HG, N)
        g_end = r.pos
        r = Region(KD * N)
        wg_ring = [r.take(2, KD, P) for _ in range(2)]
        wo_ring = [r.take(2, T4, P) for _ in range(2)]
        wf_ring = [r.take(KD, P) for _ in range(2)]
        merged = r.take(KD, M)
        sgA = [r.take(M) for _ in range(2)]
        sgB = [r.take(M) for _ in range(2)]
        assert r.pos <= work_at
        r = Region(0)
        hT = r.take(KD, M)
        xt2 = r.take(KD, 3 * P)
        acc = r.take(KD, M)
        rt = r.take(3, 36)
        rte = r.take(3, G, EG)
        rt8 = [r.take(3, EG) for _ in range(4)]
        rt4 = r.take(3, G)
        rt1 = [r.take(3) for _ in range(7)]
        gate = r.take(3, E2)
        member = r.take(3, E)
        slot = r.take(3, E2)
        flag_f = r.take(1)
        flag = r.take(1).bitcast(I32)
        pair_at = r.pos
        sel, selG = r.take(3, 2, CAP), r.take(3, 2, CAP)
        selT = r.take(3 * P)
        hidT = r.take(4, 2 * CAP)
        dense_at = r.pos
        gateT = r.take(3 * P)
        gsel = [r.take(M) for _ in range(2)]
        silu = [r.take(M) for _ in range(2)]
        hid = [r.take(4, M) for _ in range(2)]
        e_end = r.pos
        r = Region(dense_at)
        xtok = r.take(3, D)
        assert r.pos <= e_end
        r = Region(KD * M)
        xe = r.take(KD, 2 * CAP)
        ye = r.take(D)
        silu_s, hid_s = r.take(FF), r.take(FF)
        assert r.pos <= KD * M + KD * 3 * P
        assert e_end <= work_at
        r = Region(work_at)
        wgu = [r.take(2, KD, FF) for _ in range(1)]
        wdn = [r.take(4, D) for _ in range(1)]
        wgu.append(r.take(2, KD, FF))
        wdn.append(r.take(4, D))

        bank = [ctx.enter_context(nc.psum_tensor(f"bank{i}", [P, 512], F32)) for i in range(8)]

        def bk(i, *shape):
            v = bank[i][:, 0:int(np.prod(shape))]
            if len(shape) > 1:
                names = "abcde"[:len(shape)]
                v = v.rearrange(f"p ({' '.join(names)}) -> p {' '.join(names)}", **dict(zip(names, shape)))
            return v

        S = {n: sem(n) for n in (
            "rms_sq", "rms_mm", "rms_root", "head_sq", "head_sum", "head_root", "head_inv", "head_spread",
            "ld_cst", "ld_par", "ld_x", "xn", "x_packed",
            "ld_w0", "ld_w1", "proj_done", "psum_free", "ab_done",
            "shift_step", "zc_done", "lora_in", "lora_mm", "lora_out", "cum", "exps",
            "bonus_in", "bonus_mm", "bk_done", "gram_r",
            "gm_done", "bar_done", "v_tr", "v_sb", "bt_tr", "bt_sb", "z_dead",
            "sv_zero", "ld_sw", 
            "s0_mm", "s0_k", "s0_sb", "ch_rhs", "ch_rhs_sb", "ch_sa", "ch_sa_sb", "ch_y", "ch_y_sb", "ch_st", "ch_st_sb",
            "svm", "sm_mm", "sm_sb", "gn_in", "gn_d", "yA",
            "xc_init", "xc_step", "xc_ready", "xc_used", "conv_step", "conv_done", "silu_done", "z_done",
            "ab_rows", "ab_lin", "g_rows", "g_cum", "g_exp", "g_kd", "g_bc", "g_bc_dve", "g_bc_act", "d_arg", "d_exp", "d_done", "cols_tr", "ecol", "ecol2",
            "kq_done", "gram_g", "ga_done", "kv_tr", "kv_sb",
            "rwkv_over", "yB",
            "ld_wg0", "ld_wg1", "ld_wf0", "ld_wf1", "op_mm", "op_sig", "op_free", "op_merge", "fin_mm", "h_done",
            "xt2", "rt_mm", "rt_sum", "rt_exp", "gate",
            "ld_e0", "ld_e1", "ld_d0", "ld_d1", "acc", "gu_free",
            "rt_member", "rt_pos", "flag", "xt_tr", "xtok", "sp_sel", "sp_selg", "sp_gather", "xe", "sp_gate", "sp_up", "sp_silu",
            "sp_hid", "sp_ht", "hidT", "sp_dn", "sp_ye", "ld_gate", "ld_up", "ld_dn", "sp_comb", "sp_acc", "sp_selT", "selT", "moe_done", "y_ready",
            "act_own", "dve_own", "moe_own", "ab_sb", "acc_init", "stores",
            "at_zero", "inv_out", "inv_at0", "inv_at1", "inv_t10", "inv_t11", "inv_t1s0", "inv_t1s1", "inv_t20", "inv_t21", "inv_upd0", "inv_upd1")}
        for dense_step, same_as in (("gsel", "sp_sel"), ("gb_mm", "sp_comb"), ("gu_mm", "sp_gate"), ("silu", "sp_silu"),
                                    ("hid_step", "hidT"), ("hid", "sp_hid"), ("dn_mm", "sp_dn"), ("gt_tr", "sp_selT"),
                                    ("gateT", "selT")):
            S[dense_step] = S[same_as]

        t_sq = AR.rearrange("p t c x s -> p (t c x s)").rearrange("p (k n) -> p k n", k=KD)
        xw, sgx = tbonus[0:C, 0, :], tbonus[:, 1, :]
        sqg_o = sqg.rearrange("p t n -> p (t n)")[:, 0:HG * M].rearrange("p (t n) -> p t n", t=HG)

        jobs_r = [(GM[0:C, c, :, 0:C], XTr[0:C, c], T4, LEVELS if c else 4, invA[q], invX[q], invT[q], invXT[q])
                  for q, c in ((0, 1), (1, 2), (0, 3), (1, 4), (0, 0))]
        jobs_g = []
        for n, c in enumerate(range(0, NC, 2)):
            end, q = min(c + 2, NC), n % 2
            jobs_g.append((GA[0:C, c:end].rearrange("p c h s -> p (c h) s"), XTg[0:C, c:end].rearrange("p c h s -> p (c h) s"),
                           (end - c) * HG // 2, LEVELS, invA[q], invXg[q], invTg[q], invXT[q]))
        before = {}
        slot_sum = [[0, 0], [0, 0]]
        for name, jobs in (("r", jobs_r), ("g", jobs_g)):
            before[name] = []
            for n, job in enumerate(jobs):
                before[name].append(tuple(slot_sum[n % 2]))
                slot_sum[n % 2][0] += 1
                slot_sum[n % 2][1] += job[3]

        def rounds(name):
            jobs = jobs_r if name == "r" else jobs_g
            for n in range(0, len(jobs), 2):
                yield [(q, *before[name][n + q], job) for q, job in enumerate(jobs[n:n + 2])]

        def heads(v, odd):
            return v[:, odd::2, :]

        def blocks(v, odd, n):
            return v[C:P, 0:n, C:P] if odd else v[0:C, 0:n, 0:C]

        def halved(v, n):
            return v[:, 0:n, :].rearrange("p t (x s) -> p (t x) s", x=2)

        block = ctx.enter_context(nc.Block())

        def own(eng, name):
            count = [0]

            def step(ins):
                count[0] += 1
                ins.then_inc(S[name], 1)
                eng.wait_ge(S[name], count[0])
            return step

        halves = [(0, slice(0, C)), (1, slice(C, P))]
        n_stores = 7

        @block.sync
        def _(sp):
            sp.dma_start(xT[:, :, :], dram["xT"]).then_inc(S["ld_x"], 16)
            sp.dma_start(cst[:, :], dram["cst"]).then_inc(S["ld_cst"], 16)
            for k in range(2):
                sp.dma_start(w_ring[k], dram["w_in"][k]).then_inc(S[f"ld_w{k}"], 16)
            sp.dma_start(par[:, :], dram["par"]).then_inc(S["ld_par"], 16)
            with sp.Fori(1, IN_T // 2) as i:
                for k in range(2):
                    sp.wait_ge(S["proj_done"], 2 * i + k - 1)
                    sp.dma_start(w_ring[k], dram["w_in"][bass.ds(2 * i + k, 1)].rearrange("a p k c -> p (a k) c"))\
                      .then_inc(S[f"ld_w{k}"], 16)
            sp.wait_ge(S["x_packed"], 1)
            sp.dma_start(dram["shift_out"], x_out).then_inc(S["stores"], 16)
            sp.wait_ge(S["z_dead"], 2)
            for par_, rows_ in halves:
                sp.dma_start(SW[rows_, :, :, par_ * C:par_ * C + C], dram["wkv_in"][rows_]).then_inc(S["ld_sw"], 16)
            sp.wait_ge(S["sm_sb"], NSEQ)
            for par_, rows_ in halves:
                sp.dma_start(dram["wkv_s"][rows_], SW[rows_, :, :, par_ * C:par_ * C + C]).then_inc(S["stores"], 16)
            sp.wait_ge(S["ch_st_sb"], NC)
            for par_, rows_ in halves:
                sp.dma_start(dram["wkv_p"][rows_], STr[rows_, :, par_ * C:par_ * C + C]).then_inc(S["stores"], 16)
            sp.wait_ge(S["conv_done"], QKV_T)
            sp.wait_ge(S["xc_ready"], QKV_T)
            sp.dma_start(dram["conv_out"], conv_out).then_inc(S["stores"], 16)
            sp.wait_ge(S["stores"], 16 * 6)
            sp.wait_ge(S["yA"], 1)
            sp.sem_inc(S["rwkv_over"], 1)
            sp.dma_start(SW, dram["gdn_in"]).then_inc(S["ld_sw"], 16)
            sp.wait_ge(S["sm_sb"], 2 * NSEQ)
            sp.dma_start(dram["gdn_s"], SW).then_inc(S["stores"], 16)
            sp.wait_ge(S["ch_st_sb"], 2 * NC)
            sp.dma_start(dram["gdn_p"], Sg).then_inc(S["stores"], 16)
            sp.wait_ge(S["yB"], 1)
            sp.wait_ge(S["stores"], 16 * 8)

            def load_out(i, k):
                one = dram["w_gab"][bass.ds(i, 1)] if not isinstance(i, int) else dram["w_gab"][i:i + 1]
                two = dram["w_oab"][bass.ds(i, 1)] if not isinstance(i, int) else dram["w_oab"][i:i + 1]
                sp.dma_start(wg_ring[k], one.rearrange("a p g k c -> p (a g) k c")).then_inc(S[f"ld_wg{k}"], 16)
                sp.dma_start(wo_ring[k], two.rearrange("a p g k c -> p (a g) k c")).then_inc(S[f"ld_wg{k}"], 16)

            parts = (("ld_gate", "sp_gate"), ("ld_up", "sp_up"), ("ld_dn", "sp_dn"))

            def load_pair(i, part):
                for k in range(2):
                    if part < 2:
                        src = dram["w_gu"][bass.ds(2 * i + k, 1), :, part].rearrange("a p k c -> p (a k) c")
                        dst = wgu[k][:, part]
                    else:
                        src = dram["w_dn"][bass.ds(2 * i + k, 1)].rearrange("a p k c -> p (a k) c")
                        dst = wdn[k]
                    sp.dma_start(dst, src).then_inc(S[parts[part][0]], 16)

            for k in range(2):
                load_out(k, k)
            for k in range(2):
                sp.dma_start(wf_ring[k], dram["w_o"][k]).then_inc(S[f"ld_wf{k}"], 16)
            for i in range(1, KD // 2):
                for k in range(2):
                    sp.wait_ge(S["op_mm"], 2 * i + k - 1)
                    load_out(2 * i + k, k)
                load_pair(0, i - 1)
            with sp.Fori(1, KD // 2) as i:
                for k in range(2):
                    sp.wait_ge(S["fin_mm"], 2 * i + k - 1)
                    sp.dma_start(wf_ring[k], dram["w_o"][bass.ds(2 * i + k, 1)].rearrange("a p k c -> p (a k) c"))\
                      .then_inc(S[f"ld_wf{k}"], 16)
            def load_by_pairs():
                with sp.Fori(1, E // 2) as i:
                    for part in range(3):
                        sp.wait_ge(S[parts[part][1]], i)
                        load_pair(i, part)

            def load_by_experts():
                for ld, _ in parts:
                    sp.wait_ge(S[ld], 32)
                for k in range(2):
                    sp.sem_inc(S[f"ld_e{k}"], 16)
                    sp.sem_inc(S[f"ld_d{k}"], 16)
                with sp.Fori(1, E // 2) as i:
                    for k in range(2):
                        sp.wait_ge(S["gu_mm"], 4 * (2 * i + k - 1))
                        sp.dma_start(wgu[k], dram["w_gu"][bass.ds(2 * i + k, 1)].rearrange("a p g k c -> p (a g) k c"))\
                          .then_inc(S[f"ld_e{k}"], 16)
                        sp.wait_ge(S["dn_mm"], KD * (2 * i + k - 1))
                        sp.dma_start(wdn[k], dram["w_dn"][bass.ds(2 * i + k, 1)].rearrange("a p k c -> p (a k) c"))\
                          .then_inc(S[f"ld_d{k}"], 16)

            sp.wait_ge(S["flag"], 1)
            crowded = sp.value_load(flag[0:1, 0:1], min_val=0, max_val=1)
            with sp.If(crowded < 1):
                load_by_pairs()
            with sp.Else():
                load_by_experts()
            sp.wait_ge(S["y_ready"], 1)
            sp.dma_start(dram["y"], acc).then_inc(S["stores"], 16)
            sp.wait_ge(S["stores"], 16 * 9)

        @block.tensor
        def _(pe):
            mm = pe.matmul
            pe.wait_ge(S["ld_cst"], 16)
            pe.wait_ge(S["rms_sq"], 1)
            for k in range(KD):
                last = mm(bk(7, N), K("ones"), t_sq[:, k, :], start=(k == 0), stop=(k == KD - 1))
            last.then_inc(S["rms_mm"], 1)
            pe.wait_ge(S["xn"], 1)

            def project_in(first, end):
                with pe.Fori(first, end) as i:
                    for s in range(2):
                        pe.wait_ge(S[f"ld_w{s}"], 16 * i + 16)
                        pe.wait_ge(S["psum_free"], 2 * i + s + 1)
                        for k in range(KD):
                            last = mm(bk(s, N), w_ring[s][:, k, :], xnT[:, k, :], start=(k == 0), stop=(k == KD - 1))
                        last.then_inc(S["proj_done"], 1)

            project_in(0, SEG[0])
            pe.wait_ge(S["ld_par"], 16)
            wab = W("ab").rearrange("p (k c) -> p k c", k=KD)
            for b, lo, rows_ in ((2, 0, slice(0, 4)), (3, 4, slice(32, 36))):
                for k in range(KD):
                    last = mm(bank[b][rows_, 0:N], wab[:, k, lo:lo + 4], xnT[:, k, :], start=(k == 0), stop=(k == KD - 1))
                last.then_inc(S["ab_done"], 1)

            project_in(SEG[0], SEG[1])
            pe.wait_ge(S["ab_sb"], 2)
            pe.wait_ge(S["lora_in"], 2)
            for part in range(3):
                for t in range(T4):
                    if part:
                        pe.wait_ge(S["lora_out"], T4 * (part - 1) + t + 1)
                    lo = slice(t * P, t * P + P)
                    if part == 0:
                        ins = mm(bk(4 + t, N), W("w2a2")[0:C, lo], xw, start=True, stop=True)
                    elif part == 1:
                        ins = mm(bk(4 + t, N), W("w2a2")[C:P, lo], proj[C:P, 12, :], start=True, stop=True)
                    else:
                        ins = mm(bk(4 + t, N), W("g2")[:, lo], sgx, start=True, stop=True)
                    ins.then_inc(S["lora_mm"], 1)
            sum_r = K("sum_r").rearrange("p (t h) -> p t h", t=T4)
            spread_r = K("spread_r").rearrange("p (t c) -> p t c", t=T4)
            pe.wait_ge(S["head_sq"], 1)
            for t in range(T4):
                last = mm(bank[3][0:8, 0:N], sum_r[:, t, :], t2[:, t, :], start=(t == 0), stop=(t == T4 - 1))
            last.then_inc(S["head_sum"], 1)
            project_in(SEG[1], SEG[2])
            pe.wait_ge(S["head_inv"], 1)
            pe.wait_ge(S["lora_out"], 3 * T4)
            for t in range(T4):
                mm(bk(4 + t, N), spread_r[0:8, t, :], small_r[0:8, :], start=True, stop=True).then_inc(S["head_spread"], 1)
            project_in(SEG[2], SEG[3])
            pe.wait_ge(S["bonus_in"], 1)
            for t in range(T4):
                mm(bk(4 + t, N), K("blockones"), t2[:, t, :], start=True, stop=True).then_inc(S["bonus_mm"], 1)
            pe.wait_ge(S["bk_done"], 1)
            pe.wait_ge(S["z_dead"], 1)
            for c in range(NC):
                for p_, rows_ in halves:
                    n = 2 * c + p_
                    if n >= 4:
                        pe.wait_ge(S["gm_done"], n - 3)
                    for t in range(T4):
                        last = mm(bank[4 + n % 4][:, t * P:t * P + P], BK[rows_, t, c].rearrange("p a b -> p (a b)"),
                                  AR[rows_, t, c].rearrange("p a b -> p (a b)"), start=True, stop=True)
                    last.then_inc(S["gram_r"], 1)
            project_in(SEG[3], IN_T // 2)
            pe.wait_ge(S["psum_free"], IN_T + 2)
            flat = arena[:, proj_at:proj_at + IN_T * N]
            for c in range(NC):
                if c >= 2:
                    pe.wait_ge(S["v_sb"], c - 1)
                for t in range(T4):
                    lo = (8 + t) * N + C * c - C
                    last = pe.transpose(bank[c % 2][:, t * P:t * P + P], flat[:, lo:lo + P], K("ident"))
                last.then_inc(S["v_tr"], 1)
            pe.wait_ge(S["bar_done"], 1)
            pe.wait_ge(S["v_sb"], NC)
            for c in range(NC):
                if c >= 2:
                    pe.wait_ge(S["bt_sb"], c - 1)
                for t in range(T4):
                    last = pe.transpose(bank[c % 2][:, t * P:t * P + P], BK[:, t, c].rearrange("p a b -> p (a b)"), K("ident"))
                last.then_inc(S["bt_tr"], 1)

            def invert(name):
                for two in rounds(name):
                    for level in range(LEVELS):
                        now = [j for j in two if level < j[3][3]]
                        for slot, n_jobs, n_levels, (_, _, n, levels, A_T, X, T1, X_T) in now:
                            pe.wait_ge(S[f"inv_upd{slot}"], n_levels + n_jobs + level + 1)
                            for t in range(n):
                                rhs = K("ident") if level == 0 else X[:, t, :]
                                last = mm(bank[3 * slot][:, t * P:t * P + P], A_T[:, t, :], rhs, start=True, stop=True)
                            last.then_inc(S[f"inv_t1{slot}"], 1)
                        if level == 0:
                            continue
                        for slot, n_jobs, n_levels, (_, _, n, levels, A_T, X, T1, X_T) in now:
                            pe.wait_ge(S[f"inv_t1s{slot}"], n_levels - n_jobs + level)
                            for t in range(n):
                                if level < levels - 1:
                                    mm(bank[3 * slot + 1][:, t * P:t * P + P], X_T[:, t, :], T1[:, t, :], start=True, stop=True)
                                last = mm(bank[3 * slot + 2][:, t * P:t * P + P], T1[:, t, :], X_T[:, t, :], start=True, stop=True)
                            last.then_inc(S[f"inv_t2{slot}"], 1)
                pe.wait_ge(S["inv_out"], len(jobs_r) + (len(jobs_g) if name == "g" else 0))

            pe.wait_ge(S["gm_done"], 2 * NC)
            pe.wait_ge(S["bt_sb"], NC)
            invert("r")

            pe.wait_ge(S["ld_sw"], 32)
            pe.wait_ge(S["z_dead"], 2)
            c0 = bk(6, T4, 2, C)
            for b in range(NSEQ):
                lo = COL_S + TSEQ * b
                for t in range(T4):
                    last = mm(c0[:, t, :, lo:lo + TSEQ], SW[:, b, t, :], AR[:, t, 0, :, lo:lo + TSEQ], start=True, stop=True)
            last.then_inc(S["s0_mm"], 1)
            pe.wait_ge(S["s0_sb"], 1)
            for c in range(NC):
                if c:
                    pe.wait_ge(S["ch_st_sb"], c)
                for t in range(T4):
                    lhs, rhs = (C0r[:, t, 0, :], K("ident")) if c == 0 else (AR[:, t, c, 0, :], STr[:, t, :])
                    mm(bank[0][0:C, t * P:t * P + P], lhs, rhs, start=True, stop=False)
                    for h in (2 * t, 2 * t + 1):
                        last = mm(bank[0][0:C, h * C:h * C + C], GM[:, c, h, 0:C], SV[:, c, h * C:h * C + C],
                                  start=False, stop=(h % 2 == 1))
                last.then_inc(S["ch_rhs"], 1)
                pe.wait_ge(S["ch_rhs_sb"], c + 1)
                for h in range(HR):
                    last = mm(bank[1][0:C, h * C:h * C + C], XTr[0:C, c, h, :], Rs[0:C, h * C:h * C + C], start=True, stop=True)
                last.then_inc(S["ch_sa"], 1)
                pe.wait_ge(S["ch_sa_sb"], c + 1)
                if c == 0:
                    for b in range(NSEQ + 1):
                        pe.wait_ge(S["svm"], b + 1)
                        if b >= 2:
                            pe.wait_ge(S["sm_sb"], b - 1)
                        for t in range(T4):
                            last = mm(bank[4 + b % 2][:, t * P:t * P + P], BKt[:, 0, t, :], SVm[b % 2][:, t * P:t * P + P],
                                      start=True, stop=True)
                        last.then_inc(S["sm_mm"], 1)
                else:
                    for t in range(T4):
                        last = mm(bank[2][:, t * P:t * P + P], BKt[:, c, t, :], SV[:, c, t * P:t * P + P], start=True, stop=True)
                    last.then_inc(S["ch_st"], 1)
                if c:
                    pe.wait_ge(S["ch_y_sb"], c)
                for t in range(T4):
                    lhs, rhs = (K("ident"), C0r[:, t, 1, :]) if c == 0 else (STr[:, t, :], AR[:, t, c, 1, :])
                    mm(bank[3][:, t * C:t * C + C], lhs, rhs, start=True, stop=False)
                    for p_, rows_ in halves:
                        h = 2 * t + p_
                        last = mm(bank[3][rows_, t * C:t * C + C], SV[:, c, h * C:h * C + C], GM[:, c, h, C:P],
                                  start=False, stop=True)
                last.then_inc(S["ch_y"], 1)
            pe.wait_ge(S["ch_y_sb"], NC)
            for t in range(T4):
                mm(bk(4 + t, M), K("center"), ty[:, t, COL_S:], start=True, stop=True).then_inc(S["gn_d"], 1)
            pe.wait_ge(S["head_sq"], 2)
            for t in range(T4):
                last = mm(bank[3][0:8, 0:M], sum_r[:, t, :], gn_sqv[:, t, :], start=(t == 0), stop=(t == T4 - 1))
            last.then_inc(S["head_sum"], 1)
            pe.wait_ge(S["head_inv"], 2)
            for t in range(T4):
                mm(bk(4 + t, M), spread_r[0:8, t, :], small_r[0:8, 0:M], start=True, stop=True).then_inc(S["head_spread"], 1)

            sum_g = K("sum_g").rearrange("p (t h) -> p t h", t=8)
            spread_g = K("spread_g").rearrange("p (t c) -> p t c", t=8)
            pe.wait_ge(S["yA"], 1)
            pe.wait_ge(S["g_kd"], 1)
            for h in range(HG):
                if h:
                    pe.wait_ge(S["g_bc_dve"], 2 * h)
                    pe.wait_ge(S["g_bc_act"], h)
                mm(bank[4][0:C, 0:N], spread_g[0:4, h, 0:C], rows[0:4, :], start=True, stop=True).then_inc(S["g_bc"], 1)
                mm(bank[5][0:C, 0:N], spread_g[32:36, h, 0:C], rows[32:36, :], start=True, stop=True).then_inc(S["g_bc"], 1)
                mm(bk(6, N), spread_g[0:4, h, :], row_tmp[0:4, :], start=True, stop=True).then_inc(S["g_bc"], 1)
            for c in range(NC):
                last = pe.transpose(bank[7][0:C, c * 96:c * 96 + 96], rows[0:96, c * C:c * C + C], K("ident")[0:96, 0:96])
            last.then_inc(S["cols_tr"], 1)
            pe.wait_ge(S["head_sq"], 3)
            for t in range(8):
                last = mm(bank[0][0:8, 0:N], sum_g[:, t, :], sqg[:, t, :], start=(t == 0), stop=(t == 7))
            last.then_inc(S["head_sum"], 1)
            pe.wait_ge(S["head_inv"], 3)
            for t in range(8):
                if t >= 2:
                    pe.wait_ge(S["kq_done"], t - 1)
                mm(bk(1 + t % 2, N), spread_g[0:8, t, :], srow[0:8, :], start=True, stop=True).then_inc(S["head_spread"], 1)
            pe.wait_ge(S["kq_done"], 8)
            pe.wait_ge(S["ecol2"], 1)
            for c in range(NC):
                for w_ in range(2):
                    n = 2 * c + w_
                    if n >= 2:
                        pe.wait_ge(S["kv_sb"], n - 1)
                    for h in range(HG):
                        src = KQ[:, h, c, 0, :] if w_ == 0 else proj[:, 22 + h, c * C:c * C + C]
                        last = pe.transpose(bank[n % 2][0:C, h * P:h * P + P], src, K("ident"))
                    last.then_inc(S["kv_tr"], 1)
            pe.wait_ge(S["d_done"], 1)
            for c in range(NC):
                if c >= 2:
                    pe.wait_ge(S["ga_done"], c - 1)
                for h in range(HG):
                    last = mm(bank[2 + c % 2][0:C, h * P:h * P + P], KQ[:, h, c, 0, :],
                              KQ[:, h, c].rearrange("p a b -> p (a b)"), start=True, stop=True)
                last.then_inc(S["gram_g"], 1)
            pe.wait_ge(S["ga_done"], NC)
            pe.wait_ge(S["kv_sb"], 2 * NC)
            invert("g")
            pe.wait_ge(S["ld_sw"], 48)
            c0 = bk(6, HG, 2, C)
            for b in range(NSEQ):
                lo = COL_S + TSEQ * b
                for h in range(HG):
                    last = mm(c0[:, h, :, lo:lo + TSEQ], SW[:, b, h, :], KQ[:, h, 0, :, lo:lo + TSEQ], start=True, stop=True)
            last.then_inc(S["s0_mm"], 1)
            pe.wait_ge(S["s0_sb"], 2)
            for c in range(NC):
                if c:
                    pe.wait_ge(S["ch_st_sb"], NC + c)
                for h in range(HG):
                    lhs, rhs = (C0g[:, h, 0, :], K("ident")) if c == 0 else (KQ[:, h, c, 0, :], Sg[:, h, :])
                    last = mm(bank[0][0:C, h * P:h * P + P], lhs, rhs, start=True, stop=True)
                last.then_inc(S["ch_rhs"], 1)
                pe.wait_ge(S["ch_rhs_sb"], NC + c + 1)
                for h in range(HG):
                    last = mm(bank[1][0:C, h * P:h * P + P], XTg[0:C, c, h, :], Rg[0:C, h, :], start=True, stop=True)
                last.then_inc(S["ch_sa"], 1)
                pe.wait_ge(S["ch_sa_sb"], NC + c + 1)
                if c == 0:
                    for b in range(NSEQ + 1):
                        pe.wait_ge(S["svm"], NSEQ + 1 + b + 1)
                        if b >= 2:
                            pe.wait_ge(S["sm_sb"], NSEQ + b - 1)
                        for h in range(HG):
                            last = mm(bank[4 + b % 2][:, h * P:h * P + P], kdec[0:C, 0, h, :], VNm[b % 2][0:C, h * P:h * P + P],
                                      start=True, stop=True)
                        last.then_inc(S["sm_mm"], 1)
                else:
                    for h in range(HG):
                        last = mm(bank[2][:, h * P:h * P + P], kdec[0:C, c, h, :], VN[0:C, h * P:h * P + P], start=True, stop=True)
                    last.then_inc(S["ch_st"], 1)
                if c:
                    pe.wait_ge(S["ch_y_sb"], NC + c)
                for h in range(HG):
                    lhs, rhs = (K("ident"), C0g[:, h, 1, :]) if c == 0 else (Sg[:, h, :], qdec[:, h, c * C:c * C + C])
                    mm(bank[3][:, h * C:h * C + C], lhs, rhs, start=True, stop=False)
                    last = mm(bank[3][:, h * C:h * C + C], VN[0:C, h * P:h * P + P], QKD[0:C, c, h, :], start=False, stop=True)
                last.then_inc(S["ch_y"], 1)
            pe.wait_ge(S["head_sq"], 4)
            for h in range(HG):
                last = mm(bank[0][0:8, 0:M], sum_g[:, h, :], sqg_o[:, h, :], start=(h == 0), stop=(h == HG - 1))
            last.then_inc(S["head_sum"], 1)
            pe.wait_ge(S["head_inv"], 4)
            for h in range(HG):
                mm(bk(4 + h, M), spread_g[0:8, h, :], srow[0:8, 0:M], start=True, stop=True).then_inc(S["head_spread"], 1)

            pe.wait_ge(S["yB"], 1)
            with pe.Fori(0, KD // 2) as i:
                for s in range(2):
                    pe.wait_ge(S[f"ld_wg{s}"], 32 * i + 32)
                    pe.wait_ge(S["op_free"], 2 * i + s + 1)
                    for g in range(2):
                        for k in range(KD):
                            mm(bk(4 * s + g, M), wg_ring[s][:, g, k, :], xnT[:, k, COL_S:], start=(k == 0), stop=(k == KD - 1))
                    for g, y_ in ((0, yA), (1, yB)):
                        for k in range(T4):
                            last = mm(bk(4 * s + 2 + g, M), wo_ring[s][:, g, k, :], y_[:, k, :], start=(k == 0), stop=(k == T4 - 1))
                    last.then_inc(S["op_mm"], 1)
            pe.wait_ge(S["op_merge"], KD)
            with pe.Fori(0, KD // 2) as i:
                for s in range(2):
                    pe.wait_ge(S[f"ld_wf{s}"], 16 * i + 16)
                    pe.wait_ge(S["op_free"], KD + 2 * i + s + 1)
                    for k in range(KD):
                        last = mm(bk(s, M), wf_ring[s][:, k, :], merged[:, k, :], start=(k == 0), stop=(k == KD - 1))
                    last.then_inc(S["fin_mm"], 1)
            pe.wait_ge(S["rms_sq"], 2)
            for k in range(KD):
                last = mm(bk(7, M), K("ones"), acc[:, k, :], start=(k == 0), stop=(k == KD - 1))
            last.then_inc(S["rms_mm"], 1)
            pe.wait_ge(S["xt2"], 1)
            router = W("router").rearrange("p (k c) -> p k c", k=KD)
            for m in range(3):
                for k in range(KD):
                    last = mm(bank[6][:, m * 36:m * 36 + 36], xt2[:, k, m * P:m * P + P], router[:, k, :],
                              start=(k == 0), stop=(k == KD - 1))
            last.then_inc(S["rt_mm"], 1)
            pe.wait_ge(S["rt_member"], 1)
            for m in range(3):
                for q in range(m + 1):
                    last = mm(bank[6][:, m * E:m * E + E], K("before" if q == m else "ones"), member[:, q, :],
                              start=(q == 0), stop=(q == m))
            for m in range(3):
                last = mm(bank[6][:, 3 * E:4 * E], K("ones"), member[:, m, :], start=(m == 0), stop=(m == 2))
            last.then_inc(S["rt_pos"], 1)

            def dense():
                pe.wait_ge(S["gate"], 1)
                for m in range(3):
                    last = pe.transpose(bank[7][0:E, m * P:m * P + P], gate[:, m, 0:E], K("ident"))
                last.then_inc(S["gt_tr"], 1)
                pe.wait_ge(S["gateT"], 1)
                with pe.Fori(0, E // 2) as i:
                    for s in range(2):
                        e = 2 * i + s
                        pe.wait_ge(S["gsel"], e + 1)
                        mm(bk(6, M), K("ones")[0:E, :], gsel[s][0:E, :], start=True, stop=True).then_inc(S["gb_mm"], 1)
                        pe.wait_ge(S[f"ld_e{s}"], 16 * i + 16)
                        for f in range(4):
                            pe.wait_ge(S["gu_free"], 4 * e + f + 1)
                            for g in range(2):
                                for k in range(KD):
                                    last = mm(bk(2 * (f % 2) + g, M), wgu[s][:, g, k, f * P:f * P + P], xt2[:, k, 0:M],
                                              start=(k == 0), stop=(k == KD - 1))
                            last.then_inc(S["gu_mm"], 1)
                        pe.wait_ge(S[f"ld_d{s}"], 16 * i + 16)
                        pe.wait_ge(S["hid"], 4 * e + 4)
                        for j in range(KD):
                            pe.wait_ge(S["acc"], KD * e + j + 1)
                            for k in range(4):
                                last = mm(bk(4 + j % 2, M), wdn[s][:, k, j * P:j * P + P], hid[s][:, k, :], start=(k == 0), stop=(k == 3))
                            last.then_inc(S["dn_mm"], 1)

            def sparse():
                for m in range(3):
                    for half in range(2):
                        n = 2 * m + half
                        if n >= 4:
                            pe.wait_ge(S["xtok"], n - 3)
                        for k in range(4):
                            last = pe.transpose(bank[n % 4][:, k * P:k * P + P], xt2[:, 4 * half + k, m * P:m * P + P], K("ident"))
                        last.then_inc(S["xt_tr"], 1)
                pe.wait_ge(S["xtok"], 6)

                def gather():
                    for k in range(KD):
                        for m in range(3):
                            last = mm(bank[2 + k // 4][:, k % 4 * P:k % 4 * P + P], xtok[:, m, k * P:k * P + P],
                                      sel[:, m].rearrange("p s c -> p (s c)"), start=(m == 0), stop=(m == 2))
                    last.then_inc(S["sp_gather"], 1)

                def project(b, n_k, rows, weights):
                    for k in range(n_k):
                        for s in range(2):
                            half = slice(s * CAP, s * CAP + CAP)
                            last = mm(bank[b][half, :], rows[:, k, half], weights(s, k), start=(k == 0), stop=(k == n_k - 1))
                    return last

                def hidden(i, first):
                    pe.wait_ge(S["ld_gate"], 32 * i + 32)
                    pe.wait_ge(S["xe"], i + 1)
                    if not first:
                        pe.wait_ge(S["hidT"], i)
                    project(0, KD, xe, lambda s, k: wgu[s][:, 0, k, :]).then_inc(S["sp_gate"], 1)
                    pe.wait_ge(S["ld_up"], 32 * i + 32)
                    if not first:
                        pe.wait_ge(S["selT"], i)
                    project(1, KD, xe, lambda s, k: wgu[s][:, 1, k, :]).then_inc(S["sp_up"], 1)

                def turn_hidden(i):
                    pe.wait_ge(S["sp_hid"], i + 1)
                    for f in range(4):
                        last = pe.transpose(bank[0][:, f * P:f * P + P], hid_s[:, f * P:f * P + P], K("ident"))
                    last.then_inc(S["sp_ht"], 1)

                def turn_gates(i):
                    pe.wait_ge(S["sp_selg"], i + 1)
                    for m in range(3):
                        last = pe.transpose(bank[1][:, m * P:m * P + P], selG[:, m].rearrange("p s c -> p (s c)"), K("ident"))
                    last.then_inc(S["sp_selT"], 1)

                def combine(i):
                    pe.wait_ge(S["sp_ye"], i)
                    pe.wait_ge(S["selT"], i)
                    for j in range(KD):
                        pe.wait_ge(S["sp_acc"], KD * (i - 1) + j + 1)
                        mm(bk(6 + j % 2, M), ye[:, j * P:j * P + P], selT[:, 0:M], start=True, stop=True).then_inc(S["sp_comb"], 1)

                def down(i, first):
                    pe.wait_ge(S["ld_dn"], 32 * i + 32)
                    pe.wait_ge(S["hidT"], i + 1)
                    if not first:
                        pe.wait_ge(S["sp_ye"], i)
                    for half in range(2):
                        last = project(4 + half, 4, hidT, lambda s, k: wdn[s][:, k, half * 512:half * 512 + 512])
                    last.then_inc(S["sp_dn"], 1)

                def pair(i, first):
                    hidden(i, first)
                    pe.wait_ge(S["sp_sel"], i + 2)
                    gather()
                    turn_hidden(i)
                    if not first:
                        combine(i)
                    turn_gates(i)
                    down(i, first)

                pe.wait_ge(S["sp_sel"], 1)
                gather()
                pair(0, True)
                with pe.Fori(1, E // 2) as i:
                    pair(i, False)
                combine(E // 2)

            pe.wait_ge(S["flag"], 1)
            crowded = pe.value_load(flag[0:1, 0:1], min_val=0, max_val=1)
            with pe.If(crowded < 1):
                sparse()
            with pe.Else():
                dense()
            pe.wait_ge(S["rms_sq"], 3)
            for k in range(KD):
                last = mm(bk(7, M), K("ones"), xt2[:, k, 0:M], start=(k == 0), stop=(k == KD - 1))
            last.then_inc(S["rms_mm"], 1)

        @block.scalar
        def _(act):
            A = nc.scalar.activation
            step = own(act, "act_own")
            act.wait_ge(S["ld_x"], 16)
            A(t_sq, xT[:, :, :], ACT.Square).then_inc(S["rms_sq"], 1)
            act.wait_ge(S["rms_mm"], 1)
            A(rs[:, :], bk(7, N), ACT.Sqrt, bias=K("eps"), scale=1.0 / D).then_inc(S["rms_root"], 1)
            act.sem_inc(S["psum_free"], 2)
            act.sem_inc(S["op_free"], 2)
            act.sem_inc(S["silu_done"], 2)

            def evict(first, end):
                with act.Fori(first, end) as i:
                    for s in range(2):
                        act.wait_ge(S["proj_done"], 2 * i + s + 1)
                        A(proj[:, bass.ds(2 * i + s, 1), :], bk(s, 1, N), ACT.Copy).then_inc(S["psum_free"], 1)

            evict(0, SEG[0])
            act.wait_ge(S["ab_done"], 2)
            A(ab_raw[0:4, :], bank[2][0:4, 0:N], ACT.Copy).then_inc(S["ab_sb"], 1)
            A(ab_raw[32:36, :], bank[3][32:36, 0:N], ACT.Copy).then_inc(S["ab_sb"], 1)
            act.wait_ge(S["zc_done"], 1)
            A(sgx, proj[:, 13, :], ACT.Sigmoid).then_inc(S["lora_in"], 1)
            A(xw, proj[0:C, 12, :], ACT.Tanh).then_inc(S["lora_in"], 1)
            evict(SEG[0], SEG[1])
            for part, (dst, bias) in enumerate(((tL, "w0"), (ta, "a0"), (tg, None))):
                for t in range(T4):
                    act.wait_ge(S["lora_mm"], T4 * part + t + 1)
                    if bias:
                        ins = A(dst[:, t, :], bk(4 + t, N), ACT.Sigmoid, bias=W(bias)[:, t:t + 1])
                    else:
                        ins = A(dst[:, t, :], bk(4 + t, N)[:, COL_S:], ACT.Copy)
                    ins.then_inc(S["lora_out"], 1)
            evict(SEG[1], SEG[2])
            act.wait_ge(S["cum"], 2)
            A(teL[:, :, :], tL[:, :, :], ACT.Exp).then_inc(S["exps"], 1)
            A(t1[:, :, :], t1[:, :, :], ACT.Exp).then_inc(S["exps"], 1)
            act.wait_ge(S["exps"], 1)
            A(tL[:, :, :], tL[:, :, :], ACT.Exp, scale=-1.0).then_inc(S["exps"], 1)
            act.wait_ge(S["head_sum"], 1)
            A(small_r[0:8, :], bank[3][0:8, 0:N], ACT.Sqrt, bias=K("eps")[0:8]).then_inc(S["head_root"], 1)
            evict(SEG[2], IN_T // 2)
            for c in range(NC):
                act.wait_ge(S["v_tr"], c + 1)
                A(SV[C:P, c, :], bank[c % 2][C:P, :], ACT.Copy).then_inc(S["v_sb"], 1)
            for c in range(NC):
                act.wait_ge(S["bt_tr"], c + 1)
                A(BKt[:, c].rearrange("p a b -> p (a b)"), bank[c % 2][:, :], ACT.Copy).then_inc(S["bt_sb"], 1)
            def silu_conv(n):
                act.wait_ge(S["conv_done"], n + 1)
                cv, dst = conv_acc[n % 2], proj[:, RW_T + n, :]
                A(dst[:, COL_S:COL_P].rearrange("p (b t) -> p b t", t=TSEQ),
                  cv[:, 0:7 * NSEQ].rearrange("p (b t) -> p b t", t=7)[:, :, 0:TSEQ], ACT.Silu)
                A(dst[:, COL_META:COL_S], cv[:, 56:56 + META], ACT.Silu)
                A(dst[:, COL_P:], cv[:, 56 + META:], ACT.Silu).then_inc(S["silu_done"], 1)

            def invert(name):
                n_conv = 0
                for two in rounds(name):
                    for slot, _, _, (src, _, n, _, A_T, _, _, _) in two:
                        for odd in range(2):
                            ins = A(blocks(A_T, odd, n), heads(src, odd), ACT.Copy)
                        ins.then_inc(S[f"inv_at{slot}"], 1)
                    for level in range(LEVELS):
                        if name == "r" and 0 < n_conv <= QKV_T:
                            silu_conv(n_conv - 1)
                        n_conv += 1
                        for slot, n_jobs, n_levels, (_, _, n, levels, _, _, T1, _) in two:
                            if 0 < level < levels:
                                act.wait_ge(S[f"inv_t1{slot}"], n_levels + level + 1)
                                A(T1[:, 0:n].rearrange("p a b -> p (a b)"), bank[3 * slot][:, 0:n * P], ACT.Copy)\
                                    .then_inc(S[f"inv_t1s{slot}"], 1)
                    for slot, n_jobs, n_levels, (_, dst, n, levels, _, _, _, X_T) in two:
                        act.wait_ge(S[f"inv_upd{slot}"], n_levels + n_jobs + levels + 1)
                        for odd in range(2):
                            ins = A(heads(dst, odd), blocks(X_T, odd, n), ACT.Copy)
                        ins.then_inc(S["inv_out"], 1)

            act.wait_ge(S["gm_done"], 2 * NC)
            act.wait_ge(S["at_zero"], 1)
            nc.scalar.preload_act_table(ACT.Silu)
            invert("r")
            act.wait_ge(S["s0_mm"], 1)
            c0 = bk(6, T4, 2, C)
            for x in range(2):
                step(A(C0r[:, :, x, COL_S:], c0[:, :, x, COL_S:], ACT.Copy))
            act.wait_ge(S["sv_zero"], 3)
            act.sem_inc(S["s0_sb"], 1)
            for c in range(NC):
                act.wait_ge(S["ch_rhs"], c + 1)
                A(Rs[0:C, :], bank[0][0:C, :], ACT.Copy).then_inc(S["ch_rhs_sb"], 1)
                act.wait_ge(S["ch_sa"], c + 1)
                A(SV[0:C, c, :], bank[1][0:C, :], ACT.Copy).then_inc(S["ch_sa_sb"], 1)
                act.wait_ge(S["ch_y"], c + 1)
                A(ty[:, :, c * C:c * C + C], bk(3, T4, C), ACT.Copy).then_inc(S["ch_y_sb"], 1)
            for t in range(T4):
                act.wait_ge(S["gn_in"], t + 1)
                ins = A(gn_sqv[:, t, :], ty[:, t, COL_S:], ACT.Square)
            ins.then_inc(S["head_sq"], 1)
            act.wait_ge(S["head_sum"], 2)
            A(small_r[0:8, 0:M], bank[3][0:8, 0:M], ACT.Sqrt, bias=K("gn_eps")[0:8], scale=1.0 / C).then_inc(S["head_root"], 1)

            A(proj[:, RW_T + QKV_T:, :], proj[:, RW_T + QKV_T:, :], ACT.Silu).then_inc(S["z_done"], 1)
            act.wait_ge(S["rwkv_over"], 1)
            act.wait_ge(S["ab_rows"], 1)
            act.wait_ge(S["silu_done"], QKV_T + 2)
            A(sqg[:, 0:8, :], proj[:, RW_T:RW_T + 8, :], ACT.Square).then_inc(S["head_sq"], 1)
            A(rows[32:36, :], ab_raw[32:36, :], ACT.Sigmoid).then_inc(S["ab_lin"], 1)
            nc.scalar.preload_act_table_set("natural_log_exp_and_others")
            step(A(row_tmp[0:4, :], ab_raw[0:4, :], ACT.Abs, bias=W("dt_bias")[0:4]))
            step(A(row_tmp[0:4, :], row_tmp[0:4, :], ACT.Exp, scale=-1.0))
            step(A(row_tmp[0:4, :], row_tmp[0:4, :], ACT.Ln, bias=K("one")[0:4]))
            A(rs[0:4, 0:1], W("A_log")[0:4], ACT.Exp).then_inc(S["g_rows"], 1)
            act.wait_ge(S["g_cum"], 1)
            A(row_tmp[0:4, :], rows[0:4, :], ACT.Exp).then_inc(S["g_exp"], 1)
            for h in range(HG):
                act.wait_ge(S["g_bc"], 3 * h + 3)
                A(eGb[:, h, :], bk(6, N), ACT.Copy).then_inc(S["g_bc_act"], 1)
            act.wait_ge(S["cols_tr"], 1)
            tr = bank[7][0:C, 0:NC * 96].rearrange("p (c r) -> p c r", c=NC)
            step(A(cols[0:C, :, 0:96], tr, ACT.Copy))
            A(ecols[0:C, :, 0:4], tr[:, :, 0:4], ACT.Exp)
            A(ecols[0:C, :, 4:8], tr[:, :, 64:68], ACT.Exp).then_inc(S["ecol"], 1)
            act.wait_ge(S["d_arg"], 1)
            A(Dincl[0:C], Dincl[0:C], ACT.Exp).then_inc(S["d_exp"], 1)
            act.wait_ge(S["head_sum"], 3)
            A(srow[0:8, :], bank[0][0:8, 0:N], ACT.Sqrt, bias=K("eps")[0:8]).then_inc(S["head_root"], 1)
            act.wait_ge(S["ga_done"], NC)
            invert("g")
            act.wait_ge(S["s0_mm"], 2)
            c0 = bk(6, HG, 2, C)
            step(A(C0g[:, :, 0, COL_S:], c0[:, :, 0, COL_S:], ACT.Copy))
            act.sem_inc(S["s0_k"], 1)
            act.wait_ge(S["sv_zero"], 5)
            act.sem_inc(S["s0_sb"], 1)
            for c in range(NC):
                act.wait_ge(S["ch_sa"], NC + c + 1)
                A(VN[0:C, :], bank[1][0:C, :], ACT.Copy).then_inc(S["ch_sa_sb"], 1)
                act.wait_ge(S["ch_y"], NC + c + 1)
                A(oT[:, :, c * C:c * C + C], bk(3, HG, C), ACT.Copy).then_inc(S["ch_y_sb"], 1)
            act.wait_ge(S["ch_y_sb"], 2 * NC)
            A(sqg_o, oT[:, :, COL_S:], ACT.Square).then_inc(S["head_sq"], 1)
            act.wait_ge(S["head_sum"], 4)
            A(srow[0:8, 0:M], bank[0][0:8, 0:M], ACT.Sqrt, bias=K("eps")[0:8], scale=1.0 / P).then_inc(S["head_root"], 1)

            nc.scalar.preload_act_table(ACT.Sigmoid)
            act.wait_ge(S["yB"], 1)
            with act.Fori(0, KD // 2) as i:
                for s in range(2):
                    act.wait_ge(S["op_mm"], 2 * i + s + 1)
                    act.wait_ge(S["op_free"], 2 * i + s + 1)
                    A(sgA[s], bk(4 * s, M), ACT.Sigmoid)
                    A(sgB[s], bk(4 * s + 1, M), ACT.Sigmoid).then_inc(S["op_sig"], 1)
            act.wait_ge(S["h_done"], KD)
            A(acc, hT, ACT.Square).then_inc(S["rms_sq"], 1)
            act.wait_ge(S["rms_mm"], 2)
            A(rs[:, 0:M], bk(7, M), ACT.Sqrt, bias=K("eps"), scale=1.0 / D).then_inc(S["rms_root"], 1)
            nc.scalar.preload_act_table(ACT.Exp)
            act.wait_ge(S["rt_sum"], 1)
            step(A(rt4, rt4, ACT.Exp))
            A(rt1[3], rt1[3], ACT.Exp).then_inc(S["rt_exp"], 1)
            def dense():
                act.wait_ge(S["gt_tr"], 1)
                A(gateT[0:E, :], bank[7][0:E, 0:3 * P], ACT.Copy).then_inc(S["gateT"], 1)
                nc.scalar.preload_act_table(ACT.Silu)
                with act.Fori(0, E // 2) as i:
                    for s in range(2):
                        for f in range(4):
                            act.wait_ge(S["gu_mm"], 8 * i + 4 * s + f + 1)
                            act.wait_ge(S["gu_free"], 8 * i + 4 * s + f + 1)
                            A(silu[f % 2], bk(2 * (f % 2), M), ACT.Silu).then_inc(S["silu"], 1)

            def sparse():
                for n in range(6):
                    act.wait_ge(S["xt_tr"], n + 1)
                    A(xtok[:, n // 2, n % 2 * 512:n % 2 * 512 + 512], bank[n % 4][:, :], ACT.Copy).then_inc(S["xtok"], 1)

                def take(i):
                    act.wait_ge(S["sp_gather"], i + 1)
                    for half in range(2):
                        ins = A(xe[:, 4 * half:4 * half + 4, :].rearrange("p k c -> p (k c)"), bank[2 + half][:, :], ACT.Copy)
                    ins.then_inc(S["xe"], 1)

                def pair(i):
                    act.wait_ge(S["sp_gate"], i + 1)
                    A(silu_s, bank[0][:, :], ACT.Silu).then_inc(S["sp_silu"], 1)
                    take(i + 1)
                    act.wait_ge(S["sp_ht"], i + 1)
                    A(hidT.rearrange("p k c -> p (k c)"), bank[0][:, :], ACT.Copy).then_inc(S["hidT"], 1)
                    act.wait_ge(S["sp_selT"], i + 1)
                    A(selT[:, :], bk(1, 3 * P), ACT.Copy).then_inc(S["selT"], 1)
                    act.wait_ge(S["sp_dn"], i + 1)
                    for half in range(2):
                        ins = A(ye[:, half * 512:half * 512 + 512], bank[4 + half][:, :], ACT.Copy)
                    ins.then_inc(S["sp_ye"], 1)

                take(0)
                nc.scalar.preload_act_table(ACT.Silu)
                with act.Fori(0, E // 2) as i:
                    pair(i)

            act.wait_ge(S["flag"], 1)
            crowded = act.value_load(flag[0:1, 0:1], min_val=0, max_val=1)
            with act.If(crowded < 1):
                sparse()
            with act.Else():
                dense()
            act.wait_ge(S["moe_done"], 1)
            A(xt2[:, :, 0:M], acc, ACT.Square).then_inc(S["rms_sq"], 1)
            act.wait_ge(S["rms_mm"], 3)
            A(rs[:, 0:M], bk(7, M), ACT.Sqrt, bias=K("eps"), scale=1.0 / D).then_inc(S["rms_root"], 1)

        @block.gpsimd
        def _(pool):
            pool.wait_ge(S["ld_par"], 16)
            pool.wait_ge(S["xc_init"], 2)
            pool.wait_ge(S["psum_free"], 2 + IN_T)
            state = W("conv_state").rearrange("p (q b j) -> p q b j", q=QKV_T, b=NSEQ)
            out = conv_out
            with pool.Fori(0, QKV_T // 2) as i:
                for s in range(2):
                    n = 2 * i + s
                    pool.wait_ge(S["xc_used"], n + 1)
                    seqs = xc[s][:, 0:7 * NSEQ].rearrange("p (b t) -> p b t", t=7)
                    src = proj[:, bass.ds(n + RW_T, 1), :]
                    src_s = src[:, :, COL_S:COL_P].rearrange("p a (b t) -> p (a b) t", t=TSEQ)
                    cps = [
                        (seqs[:, :, 0:3], state[:, bass.ds(n, 1)].rearrange("p a b j -> p (a b) j")),
                        (seqs[:, :, 3:7], src_s),
                        (xc[s][:, 59:59 + META], src[:, :, COL_META:COL_S].rearrange("p a b -> p (a b)")),
                        (xc[s][:, 59 + META:], src[:, :, COL_P:].rearrange("p a b -> p (a b)")),
                        (out[:, bass.ds(n, 1), 0:24].rearrange("p a (b j) -> p (a b) j", j=3), src_s[:, :, 1:4]),
                        (out[:, bass.ds(n, 1), 24:27], src[:, :, N - 3:]),
                    ]
                    for d_, s_ in cps:
                        ins = nc.gpsimd.tensor_copy(d_, s_)
                        ins.then_inc(S["xc_step"], 1)
                    pool.wait_ge(S["xc_step"], 12 * i + 6 * s + 6)
                    pool.sem_inc(S["xc_ready"], 1)

        @block.vector
        def _(dve):
            V = nc.vector
            step = own(dve, "dve_own")
            TT, TS, STT, CP = V.tensor_tensor, V.tensor_scalar, V.scalar_tensor_tensor, V.tensor_copy
            step(V.memset(xc[0][:, 56:59], 0.0))
            step(V.memset(xc[1][:, 56:59], 0.0))
            dve.sem_inc(S["xc_init"], 2)
            dve.sem_inc(S["xc_used"], 2)
            dve.sem_inc(S["gu_free"], 2)
            dve.sem_inc(S["acc"], 2)
            dve.wait_ge(S["ld_par"], 16)
            dve.wait_ge(S["ld_cst"], 16)
            dve.wait_ge(S["rms_root"], 1)
            dve.wait_ge(S["ld_x"], 16)
            step(V.reciprocal(rs[:, :], rs[:, :]))
            for k in range(KD):
                last = STT(xnT[:, k, :], xT[:, k, :], W("norm1")[:, k:k + 1], rs[:, :], ALU.mult, ALU.mult)
            step(last)
            CP(xnT[:, :, 0:NSEQ], xT[:, :, 0:NSEQ]).then_inc(S["xn"], 1)
            dve.wait_ge(S["xn"], 1)
            CP(x_out[:, :, 0:NSEQ], xnT[:, :, COL_S + TSEQ - 1:COL_P:TSEQ])
            step(CP(x_out[:, :, NSEQ:], xnT[:, :, N - 1:]))
            dve.sem_inc(S["x_packed"], 1)
            step(V.memset(row_tmp[:, 0:1], 0.0))
            with dve.Fori(0, RW_T) as i:
                dve.wait_ge(S["psum_free"], i + 3)
                z = proj[:, bass.ds(i, 1), :].rearrange("p a b -> p (a b)")
                TT(row_tmp[:, 1:N], z[:, 0:N - 1], z[:, 1:N], ALU.subtract).then_inc(S["shift_step"], 1)
                dve.wait_ge(S["shift_step"], 4 * i + 1)
                TT(row_tmp[:, COL_S:COL_P:TSEQ], z[:, 0:NSEQ], z[:, COL_S:COL_P:TSEQ], ALU.subtract).then_inc(S["shift_step"], 1)
                TT(row_tmp[:, COL_P:COL_P + 1], z[:, COL_S - 1:COL_S], z[:, COL_P:COL_P + 1], ALU.subtract)\
                    .then_inc(S["shift_step"], 1)
                dve.wait_ge(S["shift_step"], 4 * i + 3)
                STT(z, row_tmp[:, :], W("mu")[:, bass.ds(i, 1)], z, ALU.mult, ALU.add).then_inc(S["shift_step"], 1)
                dve.wait_ge(S["shift_step"], 4 * i + 4)
            dve.sem_inc(S["zc_done"], 1)
            zr, zk, zv = proj[:, 0:4, :], proj[:, 4:8, :], proj[:, 8:12, :]
            step(TT(tkk[:, :, :], zk, spread(W("k_k"), N), ALU.mult))
            TT(t2[:, :, :], tkk[:, :, :], tkk[:, :, :], ALU.mult).then_inc(S["head_sq"], 1)
            dve.wait_ge(S["lora_out"], T4)
            step(TS(t1[:, :, :], tL[:, :, :], -float(np.exp(-0.5)), None, ALU.mult))
            for t in range(T4):
                last = V.tensor_tensor_scan(tL[:, t, :], K("carry"), t1[:, t, :], 0.0, ALU.mult, ALU.add)
            last.then_inc(S["cum"], 1)
            dve.wait_ge(S["cum"], 1)
            TT(t1[:, :, :], tL[:, :, :], t1[:, :, :], ALU.subtract).then_inc(S["cum"], 1)
            dve.wait_ge(S["head_root"], 1)
            V.reciprocal(small_r[0:8, :], small_r[0:8, :]).then_inc(S["head_inv"], 1)
            for t in range(T4):
                dve.wait_ge(S["head_spread"], t + 1)
                last = TT(tkk[:, t, :], tkk[:, t, :], bk(4 + t, N), ALU.mult)
            step(last)
            dve.wait_ge(S["exps"], 3)
            AR3 = AR.rearrange("p t c x s -> p (t c) x s")
            BK3 = BK.rearrange("p t c x s -> p (t c) x s")

            def ch(v):
                return v.rearrange("p t (c s) -> p (t c) s", s=C)

            step(STT(AR3[:, :, 0, :], ch(tkk), -1.0, ch(t1), ALU.mult, ALU.mult))
            step(TT(AR3[:, :, 1, :], ch(zr), ch(teL), ALU.mult))
            step(TT(t1[:, :, :], tkk[:, :, :], ta[:, :, :], ALU.mult))
            step(TT(BK3[:, :, 0, :], ch(t1), ch(tL), ALU.mult))
            step(STT(ta[:, :, :], ta[:, :, :], 1.0, spread(W("k_a"), N), ALU.subtract, ALU.mult))
            step(STT(ta[:, :, :], ta[:, :, :], 1.0, zk, ALU.add, ALU.mult))
            TT(BK3[:, :, 1, :], ch(ta), ch(tL), ALU.mult).then_inc(S["bk_done"], 1)
            CP(PTs[:, :, 1:NC], teL[:, :, 2 * C - 1:N:C])
            CP(PTs[:, :, 0:1], teL[:, :, COL_S - 1:COL_S])
            step(CP(PTs[:, :, NC:], teL[:, :, COL_S + TSEQ - 1:COL_P:TSEQ]))
            step(TT(t2[:, :, :], zr, ta[:, :, :], ALU.mult))
            TT(t2[:, :, :], t2[:, :, :], spread(W("r_k"), N), ALU.mult).then_inc(S["bonus_in"], 1)
            for t in range(T4):
                dve.wait_ge(S["bonus_mm"], t + 1)
                last = TT(tbonus[:, t, :], zv[:, t, :], bk(4 + t, N), ALU.mult)
            step(last)
            dve.sem_inc(S["z_dead"], 1)
            for c in range(NC):
                for p_, _ in halves:
                    n = 2 * c + p_
                    dve.wait_ge(S["gram_r"], n + 1)
                    TT(GM[:, c, p_::2, :], bk(4 + n % 4, T4, P), over(K("gmask0" if c == 0 else "gmask1"), T4), ALU.mult)\
                        .then_inc(S["gm_done"], 1)
            for x in range(2):
                TT(BK[:, :, 1:, x, :], BK[:, :, 1:, x, :], spread(PTs[:, :, 1:NC], C), ALU.mult)
                v = BK[:, :, 0, x, COL_S:].rearrange("p t (b s) -> p t b s", s=TSEQ)
                TT(v, v, spread(PTs[:, :, NC:], TSEQ), ALU.mult)
                v = BK[:, :, 0, x, COL_META:COL_S]
                last = TT(v, v, PTs[:, :, 0:1].to_broadcast([P, T4, META]), ALU.mult)
            step(last)
            dve.sem_inc(S["bar_done"], 1)
            V.memset(SV[0:C], 0.0).then_inc(S["sv_zero"], 1)
            dve.wait_ge(S["v_sb"], NC)
            for p_, rows_ in halves:
                last = V.memset(SW[rows_, :, :, (1 - p_) * C:(2 - p_) * C], 0.0)
            step(last)
            dve.sem_inc(S["z_dead"], 1)
            V.memset(C0r[:, :, :, 0:COL_S], 0.0).then_inc(S["sv_zero"], 1)
            V.memset(STr, 0.0).then_inc(S["sv_zero"], 1)

            cw = W("conv").rearrange("p (q j) -> p q j", q=QKV_T)

            def convolve(n):
                dve.wait_ge(S["xc_ready"], n + 1)
                dve.wait_ge(S["silu_done"], n + 1)
                for j in range(4):
                    w_ = cw[:, n, j:j + 1]
                    x = xc[n % 2][:, j:j + CONVN]
                    if j == 0:
                        ins = TS(conv_acc[n % 2], x, w_, None, ALU.mult)
                    else:
                        ins = STT(conv_acc[n % 2], x, w_, conv_acc[n % 2], ALU.mult, ALU.add)
                    if j < 3:
                        ins.then_inc(S["conv_step"], 1)
                        dve.wait_ge(S["conv_step"], 3 * n + j + 1)
                ins.then_inc(S["conv_done"], 1)
                dve.wait_ge(S["conv_done"], n + 1)
                dve.sem_inc(S["xc_used"], 1)

            low = K("low").rearrange("p (l c) -> p l c", l=LEVELS).bitcast(I32)
            up = K("up").rearrange("p (l c) -> p l c", l=LEVELS).bitcast(I32)

            def invert(name):
                n_conv, n_out = 0, 0 if name == "r" else len(jobs_r)
                for two in rounds(name):
                    if n_out:
                        dve.wait_ge(S["inv_out"], n_out)
                    n_out += len(two)
                    for slot, n_jobs, n_levels, (_, _, n, _, A_T, X, _, X_T) in two:
                        dve.wait_ge(S[f"inv_at{slot}"], n_jobs + 1)
                        CP(X[:, 0:n, :], over(K("ident"), n))
                        step(CP(X_T[:, 0:n, :], over(K("ident"), n)))
                        V.copy_predicated(halved(X_T, n), over(up[:, 0, :], 2 * n), halved(A_T, n)).then_inc(S[f"inv_upd{slot}"], 1)
                    for level in range(LEVELS):
                        for slot, n_jobs, n_levels, (_, _, n, levels, _, X, _, X_T) in two:
                            if level >= levels:
                                continue
                            m_low, m_up = over(low[:, level, :], 2 * n), over(up[:, level, :], 2 * n)
                            if level == 0:
                                dve.wait_ge(S[f"inv_t1{slot}"], n_levels + 1)
                                V.copy_predicated(halved(X, n), m_low, bk(3 * slot, HR, C)[:, 0:2 * n, :])\
                                    .then_inc(S[f"inv_upd{slot}"], 1)
                                continue
                            dve.wait_ge(S[f"inv_t2{slot}"], n_levels - n_jobs + level)
                            if level < levels - 1:
                                V.copy_predicated(halved(X, n), m_low, bk(3 * slot + 1, HR, C)[:, 0:2 * n, :])
                            V.copy_predicated(halved(X_T, n), m_up, bk(3 * slot + 2, HR, C)[:, 0:2 * n, :])\
                                .then_inc(S[f"inv_upd{slot}"], 1)
                        if name == "r" and n_conv < QKV_T:
                            convolve(n_conv)
                        n_conv += 1

            dve.wait_ge(S["psum_free"], IN_T + 2)
            for a in invA:
                step(V.memset(a, 0.0))
            dve.sem_inc(S["at_zero"], 1)
            dve.wait_ge(S["gm_done"], 2 * NC)
            invert("r")
            for c in range(NC):
                if c == 0:
                    dve.wait_ge(S["ch_sa_sb"], 1)
                    dve.wait_ge(S["ld_sw"], 32)
                    dve.wait_ge(S["s0_mm"], 1)
                    for b in range(NSEQ + 1):
                        if b >= 2:
                            dve.wait_ge(S["sm_mm"], b - 1)
                        TS(SVm[b % 2], SV[:, 0, :], K("seq")[:, b:b + 1], None, ALU.mult).then_inc(S["svm"], 1)
                        if b < NSEQ:
                            for p_, rows_ in halves:
                                v = SW[rows_, b, :, p_ * C:p_ * C + C]
                                last = TT(v, v, spread(PTs[rows_, :, NC + b], C), ALU.mult)
                            step(last)
                        dve.wait_ge(S["sm_mm"], b + 1)
                        for p_, rows_ in halves:
                            src = bk(4 + b % 2, T4, P)[rows_, :, p_ * C:p_ * C + C]
                            if b < NSEQ:
                                v = SW[rows_, b, :, p_ * C:p_ * C + C]
                                last = TT(v, v, src, ALU.add)
                            else:
                                last = CP(STr[rows_, :, p_ * C:p_ * C + C], src)
                        last.then_inc(S["sm_sb" if b < NSEQ else "ch_st_sb"], 1)
                    continue
                dve.wait_ge(S["ch_st"], c)
                dve.wait_ge(S["ch_y"], c + 1)
                for p_, rows_ in halves:
                    v = STr[rows_, :, p_ * C:p_ * C + C]
                    last = TT(v, v, spread(PTs[rows_, :, c], C), ALU.mult)
                step(last)
                for p_, rows_ in halves:
                    v = STr[rows_, :, p_ * C:p_ * C + C]
                    last = TT(v, v, bk(2, T4, P)[rows_, :, p_ * C:p_ * C + C], ALU.add)
                last.then_inc(S["ch_st_sb"], 1)
            for t in range(T4):
                dve.wait_ge(S["gn_d"], t + 1)
                CP(ty[:, t, COL_S:], bk(4 + t, M)).then_inc(S["gn_in"], 1)
            dve.wait_ge(S["gn_in"], T4)
            dve.wait_ge(S["head_root"], 2)
            V.reciprocal(small_r[0:8, 0:M], small_r[0:8, 0:M]).then_inc(S["head_inv"], 1)
            for t in range(T4):
                dve.wait_ge(S["head_spread"], T4 + t + 1)
                y = ty[:, t, COL_S:]
                step(TT(y, y, bk(4 + t, M), ALU.mult))
                step(TS(y, y, W("ln_w")[:, t:t + 1], W("ln_b")[:, t:t + 1], ALU.mult, ALU.add))
            y = ty[:, :, COL_S:]
            step(TT(y, y, tbonus[:, :, COL_S:], ALU.add))
            TT(yA[:, :, :], y, tg[:, :, :], ALU.mult).then_inc(S["yA"], 1)

            dve.wait_ge(S["rwkv_over"], 1)
            step(V.memset(rows, 0.0))
            dve.sem_inc(S["ab_rows"], 1)
            step(TS(srow[0:4, :], ab_raw[0:4, :], W("dt_bias")[0:4], 0.0, ALU.add, ALU.max))
            dve.wait_ge(S["g_rows"], 1)
            step(TT(srow[0:4, :], srow[0:4, :], row_tmp[0:4, :], ALU.add))
            step(TS(srow[0:4, :], srow[0:4, :], rs[0:4, 0:1], -1.0, ALU.mult, ALU.mult))
            V.tensor_tensor_scan(rows[0:4, :], K("carry")[0:4], srow[0:4, :], 0.0, ALU.mult, ALU.add).then_inc(S["g_cum"], 1)
            dve.wait_ge(S["g_cum"], 1)
            g = rows[0:4, :]
            TT(rows[64:68, COL_P:].rearrange("p (c s) -> p c s", s=C),
               g[:, 2 * C - 1:N:C].unsqueeze(2).to_broadcast([4, NC - 1, C]),
               g[:, COL_P:].rearrange("p (c s) -> p c s", s=C), ALU.subtract)
            TT(rows[64:68, COL_META:COL_S], g[:, COL_S - 1:COL_S].to_broadcast([4, META]), g[:, COL_META:COL_S], ALU.subtract)
            step(TT(rows[64:68, COL_S:COL_P].rearrange("p (b s) -> p b s", s=TSEQ),
                    g[:, COL_S + TSEQ - 1:COL_P:TSEQ].unsqueeze(2).to_broadcast([4, NSEQ, TSEQ]),
                    g[:, COL_S:COL_P].rearrange("p (b s) -> p b s", s=TSEQ), ALU.subtract))
            dve.wait_ge(S["ab_lin"], 1)
            dve.wait_ge(S["g_exp"], 1)
            dve.sem_inc(S["g_kd"], 1)
            for h in range(HG):
                dve.wait_ge(S["g_bc"], 3 * h + 2)
                CP(Dincl[0:C, h, :], bank[4][0:C, 0:N]).then_inc(S["g_bc_dve"], 1)
                TT(Dstr[0:C, h, :], K("strict")[0:C], bank[5][0:C, 0:N], ALU.mult).then_inc(S["g_bc_dve"], 1)
            dve.wait_ge(S["ecol"], 1)
            dve.wait_ge(S["g_bc_dve"], 2 * HG)
            for h in range(HG):
                v = Dincl[0:C, h, :].rearrange("p (c s) -> p c s", s=C)
                last = TT(v, v, spread(cols[0:C, :, h], C), ALU.subtract)
            step(last)
            TS(Dincl[0:C], Dincl[0:C], 0.0, None, ALU.min).then_inc(S["d_arg"], 1)
            STT(cols[0:C, :, 96:100], cols[0:C, :, 32:36], -1.0, ecols[0:C, :, 0:4], ALU.mult, ALU.mult).then_inc(S["ecol2"], 1)
            dve.wait_ge(S["d_exp"], 1)
            step(TT(Dstr[0:C], Dstr[0:C], Dincl[0:C], ALU.mult))
            TT(Dincl[0:C], Dincl[0:C], over(K("incl")[0:C], HG), ALU.mult).then_inc(S["d_done"], 1)
            dve.wait_ge(S["head_root"], 3)
            V.reciprocal(srow[0:8, :], srow[0:8, :]).then_inc(S["head_inv"], 1)
            dve.wait_ge(S["silu_done"], QKV_T + 2)
            for t in range(8):
                dve.wait_ge(S["head_spread"], 2 * T4 + t + 1)
                src = proj[:, RW_T + t, :].rearrange("p (c s) -> p c s", s=C)
                ps = bk(1 + t % 2, NC, C)
                if t < 4:
                    ins = STT(KQ[:, t, :, 1, :], src, float(P ** -0.5), ps, ALU.mult, ALU.mult)
                else:
                    ins = TT(KQ[:, t - 4, :, 0, :], src, ps, ALU.mult)
                ins.then_inc(S["kq_done"], 1)
            dve.wait_ge(S["kq_done"], 8)
            dve.wait_ge(S["g_bc_act"], HG)
            for h in range(HG):
                last = TT(qdec[:, h, :].rearrange("p (c s) -> p c s", s=C), KQ[:, h, :, 1, :],
                          eGb[:, h, :].rearrange("p (c s) -> p c s", s=C), ALU.mult)
            step(last)
            for c in range(NC):
                for w_ in range(2):
                    n = 2 * c + w_
                    dve.wait_ge(S["kv_tr"], n + 1)
                    col = ecols[0:C, c, 4:8] if w_ == 0 else cols[0:C, c, 32:36]
                    TT((kdec, bV)[w_][0:C, c], bk(n % 2, HG, P)[0:C], spread(col, P), ALU.mult).then_inc(S["kv_sb"], 1)
            for c in range(NC):
                dve.wait_ge(S["gram_g"], c + 1)
                ps = bk(2 + c % 2, HG, 2, C)[0:C]
                TT(GA[0:C, c], ps[:, :, 0, :], Dstr[0:C, :, c * C:c * C + C], ALU.mult)
                TT(QKD[0:C, c], ps[:, :, 1, :], Dincl[0:C, :, c * C:c * C + C], ALU.mult).then_inc(S["ga_done"], 1)
            V.memset(C0g[:, :, :, 0:COL_S], 0.0).then_inc(S["sv_zero"], 1)
            dve.wait_ge(S["ga_done"], NC)
            invert("g")
            dve.wait_ge(S["s0_k"], 1)
            TT(C0g[:, :, 1, COL_S:], bk(6, HG, 2, C)[:, :, 1, COL_S:], eGb[:, :, COL_S:COL_P], ALU.mult).then_inc(S["sv_zero"], 1)
            for c in range(NC):
                dve.wait_ge(S["ch_rhs"], NC + c + 1)
                step(TT(Rg[0:C], bk(0, HG, P)[0:C], spread(cols[0:C, c, 96:100], P), ALU.mult))
                TT(Rg[0:C], Rg[0:C], bV[0:C, c], ALU.add).then_inc(S["ch_rhs_sb"], 1)
                if c == 0:
                    dve.wait_ge(S["ch_sa_sb"], NC + 1)
                    dve.wait_ge(S["ld_sw"], 48)
                    for b in range(NSEQ + 1):
                        if b >= 2:
                            dve.wait_ge(S["sm_mm"], NSEQ + 1 + b - 1)
                        TS(VNm[b % 2][0:C], VN[0:C, :], K("seq")[0:C, b:b + 1], None, ALU.mult).then_inc(S["svm"], 1)
                        if b < NSEQ:
                            lo = COL_S + TSEQ * b + TSEQ - 1
                            step(TT(SW[:, b], SW[:, b], eGb[:, :, lo:lo + 1].to_broadcast([P, HG, P]), ALU.mult))
                        dve.wait_ge(S["sm_mm"], NSEQ + 1 + b + 1)
                        if b < NSEQ:
                            TT(SW[:, b], SW[:, b], bk(4 + b % 2, HG, P), ALU.add).then_inc(S["sm_sb"], 1)
                        else:
                            CP(Sg, bk(4 + b % 2, HG, P)).then_inc(S["ch_st_sb"], 1)
                    continue
                dve.wait_ge(S["ch_st"], NC - 1 + c)
                dve.wait_ge(S["ch_y"], NC + c + 1)
                lo = c * C + C - 1
                step(TT(Sg, Sg, eGb[:, :, lo:lo + 1].to_broadcast([P, HG, P]), ALU.mult))
                TT(Sg, Sg, bk(2, HG, P), ALU.add).then_inc(S["ch_st_sb"], 1)
            dve.wait_ge(S["head_root"], 4)
            V.reciprocal(srow[0:8, 0:M], srow[0:8, 0:M]).then_inc(S["head_inv"], 1)
            dve.wait_ge(S["z_done"], 1)
            for h in range(HG):
                dve.wait_ge(S["head_spread"], 2 * T4 + 8 + h + 1)
                o = oT[:, h, COL_S:]
                step(STT(o, o, W("gdn_norm"), bk(4 + h, M), ALU.mult, ALU.mult))
            TT(yB[:, :, :], oT[:, :, COL_S:], proj[:, RW_T + QKV_T:, COL_S:], ALU.mult).then_inc(S["yB"], 1)

            with dve.Fori(0, KD // 2) as i:
                for s in range(2):
                    n = 2 * i + s
                    dve.wait_ge(S["op_sig"], n + 1)
                    TT(sgA[s], sgA[s], bk(4 * s + 2, M), ALU.mult).then_inc(S["moe_own"], 1)
                    TT(sgB[s], sgB[s], bk(4 * s + 3, M), ALU.mult).then_inc(S["moe_own"], 1)
                    dve.wait_ge(S["moe_own"], 4 * i + 2 * s + 2)
                    TT(merged[:, bass.ds(n, 1), :], sgA[s].unsqueeze(1), sgB[s].unsqueeze(1), ALU.add).then_inc(S["op_merge"], 1)
                    dve.wait_ge(S["op_merge"], n + 1)
                    dve.sem_inc(S["op_free"], 1)
            with dve.Fori(0, KD // 2) as i:
                for s in range(2):
                    n = 2 * i + s
                    dve.wait_ge(S["fin_mm"], n + 1)
                    TT(hT[:, bass.ds(n, 1), :], xT[:, bass.ds(n, 1), COL_S:], bk(s, 1, M), ALU.add).then_inc(S["h_done"], 1)
                    dve.wait_ge(S["h_done"], n + 1)
                    dve.sem_inc(S["op_free"], 1)
            V.memset(xt2[:, :, M:], 0.0)
            dve.wait_ge(S["rms_root"], 2)
            step(V.reciprocal(rs[:, 0:M], rs[:, 0:M]))
            for k in range(KD):
                last = STT(xt2[:, k, 0:M], hT[:, k, :], W("norm2")[:, k:k + 1], rs[:, 0:M], ALU.mult, ALU.mult)
            last.then_inc(S["xt2"], 1)
            dve.wait_ge(S["rt_mm"], 1)
            step(TT(rt, bk(6, 3, 36), over(W("router_b"), 3), ALU.add))
            gl = rt[:, :, 0:G]
            el = rt[:, :, G:].rearrange("p m (g e) -> p m g e", g=G)
            gm, den, m1, m2, w1, w2, tmp = rt1

            def first_of(dst, src, top, order, n):
                step(TT(dst, src, spread(top, n), ALU.is_equal))
                step(TT(dst, dst, over(order, 3), ALU.mult))
                step(V.tensor_reduce(tmp, dst, AX.X, ALU.max))
                step(TT(dst, dst, spread(tmp, n), ALU.is_equal))

            ohg, oh1, oh2, ev = rt8[0][:, :, 0:G], rt8[1], rt8[2], rt8[3]
            step(V.tensor_reduce(gm, gl, AX.X, ALU.max))
            step(TT(rt4, gl, spread(gm, G), ALU.subtract))
            first_of(ohg, gl, gm, K("first4"), G)
            for m in range(3):
                last = TT(rte[:, m], el[:, m], spread(ohg[:, m], EG), ALU.mult)
            step(last)
            step(V.tensor_reduce(ev, rte.rearrange("p m g e -> p m e g"), AX.X, ALU.add))
            step(V.tensor_reduce(m1, ev, AX.X, ALU.max))
            first_of(oh1, ev, m1, K("first8"), EG)
            step(STT(ev, oh1, -1e30, ev, ALU.mult, ALU.add))
            step(V.tensor_reduce(m2, ev, AX.X, ALU.max))
            first_of(oh2, ev, m2, K("first8"), EG)
            step(TT(m2, m2, m1, ALU.subtract))
            dve.sem_inc(S["rt_sum"], 1)
            step(TT(ev, oh1, oh2, ALU.add))
            step(TT(ev, ev, spread(K("valid"), EG), ALU.mult))
            for m in range(3):
                last = TT(member[:, m].rearrange("p (g e) -> p g e", g=G), spread(ohg[:, m], EG), over(ev[:, m], G), ALU.mult)
            last.then_inc(S["rt_member"], 1)
            V.memset(slot, -1.0)
            V.memset(gate, 0.0)
            dve.wait_ge(S["rt_exp"], 1)
            step(V.tensor_reduce(den, rt4, AX.X, ALU.add))
            step(STT(w1, m2, 1.0, den, ALU.add, ALU.mult))
            step(V.reciprocal(w1, w1))
            step(TT(w2, w1, m2, ALU.mult))
            step(TT(oh1, oh1, spread(w1, EG), ALU.mult))
            step(TT(oh2, oh2, spread(w2, EG), ALU.mult))
            step(TT(oh1, oh1, oh2, ALU.add))
            for m in range(3):
                last = TT(gate[:, m, 0:E].rearrange("p (g e) -> p g e", g=G), spread(ohg[:, m], EG), over(oh1[:, m], G), ALU.mult)
            last.then_inc(S["gate"], 1)
            dve.wait_ge(S["rt_pos"], 1)
            step(STT(slot[:, :, 0:E], bk(6, 3, E), 1.0, member, ALU.add, ALU.mult))
            step(TS(slot[:, :, 0:E], slot[:, :, 0:E], -1.0, None, ALU.add))
            step(V.tensor_reduce(flag_f, bank[6][:, 3 * E:4 * E], AX.X, ALU.max))
            TS(flag, flag_f, CAP + 0.5, None, ALU.is_gt).then_inc(S["flag"], 1)
            CP(acc, hT).then_inc(S["acc_init"], 1)
            dve.wait_ge(S["acc_init"], 1)

            def dense():
                dve.wait_ge(S["gateT"], 1)
                for s in range(2):
                    TS(gsel[s][0:E], gateT[0:E, 0:M], K("ident")[0:E, s:s + 1], None, ALU.mult).then_inc(S["gsel"], 1)
                with dve.Fori(0, E // 2) as i:
                    for s in range(2):
                        e = 2 * i + s
                        dve.wait_ge(S["gb_mm"], e + 1)
                        for f in range(4):
                            dve.wait_ge(S["silu"], 4 * e + f + 1)
                            TT(hid[s][:, f, :], silu[f % 2], bk(2 * (f % 2) + 1, M), ALU.mult).then_inc(S["hid_step"], 1)
                            dve.wait_ge(S["hid_step"], 8 * i + 4 * s + f + 1)
                            TT(hid[s][:, f, :], hid[s][:, f, :], bk(6, M), ALU.mult).then_inc(S["hid"], 1)
                            dve.wait_ge(S["hid"], 4 * e + f + 1)
                            dve.sem_inc(S["gu_free"], 1)
                        TS(gsel[s][0:E], gateT[0:E, 0:M], K("ident")[0:E, bass.ds(e + 2, 1)], None, ALU.mult).then_inc(S["gsel"], 1)
                        for j in range(KD):
                            dve.wait_ge(S["dn_mm"], KD * e + j + 1)
                            TT(acc[:, j, :], acc[:, j, :], bk(4 + j % 2, M), ALU.add).then_inc(S["acc"], 1)

                dve.wait_ge(S["acc"], 2 + KD * E)
                dve.sem_inc(S["moe_done"], 1)

            def sparse():
                dve.sem_inc(S["sp_acc"], 2)

                def select(i):
                    for s in range(2):
                        ins = TT(sel[:, :, s, :], over(K("iota"), 3),
                                 slot[:, :, bass.ds(2 * i + s, 1)].to_broadcast([P, 3, CAP]), ALU.is_equal)
                    ins.then_inc(S["sp_sel"], 1)

                def weigh(i):
                    for s in range(2):
                        ins = TT(selG[:, :, s, :], sel[:, :, s, :],
                                 gate[:, :, bass.ds(2 * i + s, 1)].to_broadcast([P, 3, CAP]), ALU.mult)
                    ins.then_inc(S["sp_selg"], 1)

                def add(i):
                    for j in range(KD):
                        dve.wait_ge(S["sp_comb"], KD * (i - 1) + j + 1)
                        TT(acc[:, j, :], acc[:, j, :], bk(6 + j % 2, M), ALU.add).then_inc(S["sp_acc"], 1)

                def pair(i, first):
                    dve.wait_ge(S["sp_silu"], i + 1)
                    dve.wait_ge(S["sp_up"], i + 1)
                    TT(hid_s, silu_s, bank[1][:, :], ALU.mult).then_inc(S["sp_hid"], 1)
                    if not first:
                        dve.wait_ge(S["sp_acc"], KD * (i - 1) + 2)
                        add(i)
                    dve.wait_ge(S["sp_selT"], i + 1)
                    weigh(i + 1)
                    dve.wait_ge(S["sp_gather"], i + 2)
                    dve.wait_ge(S["sp_selg"], i + 2)
                    select(i + 2)

                select(0)
                dve.wait_ge(S["sp_sel"], 1)
                weigh(0)
                dve.wait_ge(S["sp_gather"], 1)
                dve.wait_ge(S["sp_selg"], 1)
                select(1)
                dve.wait_ge(S["sp_sel"], 2)
                pair(0, True)
                with dve.Fori(1, E // 2) as i:
                    dve.wait_ge(S["sp_sel"], i + 2)
                    pair(i, False)
                dve.wait_ge(S["sp_acc"], KD * (E // 2 - 1) + 2)
                add(E // 2)
                dve.wait_ge(S["sp_acc"], KD * (E // 2) + 2)
                dve.sem_inc(S["moe_done"], 1)

            dve.wait_ge(S["flag"], 1)
            dve.wait_ge(S["gate"], 1)
            crowded = dve.value_load(flag[0:1, 0:1], min_val=0, max_val=1)
            with dve.If(crowded < 1):
                sparse()
            with dve.Else():
                dense()
            dve.wait_ge(S["rms_root"], 3)
            step(V.reciprocal(rs[:, 0:M], rs[:, 0:M]))
            for k in range(KD):
                last = STT(acc[:, k, :], acc[:, k, :], W("normf")[:, k:k + 1], rs[:, 0:M], ALU.mult, ALU.mult)
            last.then_inc(S["y_ready"], 1)


SHAPES = dict(
    xT=(P, KD, N), cst=(P, CST.width), par=(P, PAR.width), w_in=(IN_T, P, KD, P), wkv_in=(P, NSEQ, T4, C),
    gdn_in=(P, NSEQ, HG, P), w_gab=(KD, P, 2, KD, P), w_oab=(KD, P, 2, T4, P), w_o=(KD, P, KD, P),
    w_gu=(E, P, 2, KD, FF), w_dn=(E, P, 4, D))
OUT_SHAPES = dict(
    y=(P, KD, M), shift_out=(P, KD, NSEQ + 1), wkv_p=(P, T4, C), wkv_s=(P, NSEQ, T4, C), conv_out=(P, QKV_T, 27),
    gdn_p=(P, HG, P), gdn_s=(P, NSEQ, HG, P))


def kernel(**inputs):
    import concourse.bacc as bacc
    from concourse.bass_utils import run_bass_kernel_spmd as run

    x = {k: np.asarray(v) for k, v in inputs.items()}

    def feat(a):
        a = a.reshape(a.shape[0] // P, P, -1)
        return a.transpose(1, 0, 2).reshape(P, -1)

    tokens = np.concatenate([x["state_shift"][0], np.zeros((NSEQ, D), np.float32), x["meta_tokens"],
                             x["x_sample"].reshape(-1, D), x["x_prompt"][0]])
    par = np.zeros((P, PAR.width), np.float32)

    def put(name, a, row=0):
        a = a.reshape(a.shape[0], -1)
        lo = PAR.at[name][0]
        par[row:row + a.shape[0], lo:lo + a.shape[1]] = a

    w_in = x["w_in"][0]
    cut = IN_T * P
    put("norm1", feat(x["norm1_w"][0]))
    put("norm2", feat(x["norm2_w"][0]))
    put("normf", feat(x["norm_f_w"]))
    put("mu", feat(x["mu_shift"][0]))
    for name, key in (("w0", "rw_w0"), ("a0", "rw_a0"), ("k_k", "rw_k_k"), ("k_a", "rw_k_a"), ("r_k", "rw_r_k"),
                      ("ln_w", "rw_lnx_w"), ("ln_b", "rw_lnx_b")):
        put(name, feat(x[key][0].reshape(-1)))
    put("conv", feat(x["gdn_conv_w"][0].T))
    put("gdn_norm", x["gdn_norm_w"][0][:, None])
    put("A_log", x["gdn_A_log"][0][:, None])
    put("dt_bias", x["gdn_dt_bias"][0][:, None])
    put("w2a2", x["rw_w2"][0])
    put("w2a2", x["rw_a2"][0], C)
    put("g2", x["rw_g2"][0])
    put("ab", feat(w_in[:, cut:cut + 8]))
    put("router", feat(np.concatenate([x["router_g"][0], x["router_e"][0]], 1)))
    put("router_b", np.broadcast_to(np.concatenate([x["router_g_b"][0], x["router_e_b"][0]]), (P, 36)))
    put("conv_state", feat(x["state_conv"][0].transpose(2, 0, 1).reshape(QKV_T * P, NSEQ * 3)))

    def tiles(w):
        return w.reshape(w.shape[0] // P, P, w.shape[1] // P, P).transpose(2, 1, 0, 3)

    gates = cut + 8
    wg, wu = (x[f"moe_w_{n}"][0].reshape(E, KD, P, FF).transpose(0, 2, 1, 3) for n in ("gate", "up"))
    arrays = dict(
        xT=feat(tokens.T).reshape(P, KD, N), cst=constants(), par=par, w_in=tiles(w_in[:, :cut]),
        wkv_in=x["state_wkv"][0].reshape(NSEQ, T4, 2, C, C).transpose(2, 4, 0, 1, 3).reshape(P, NSEQ, T4, C),
        gdn_in=x["state_gdn"][0].transpose(2, 0, 1, 3),
        w_gab=np.stack([tiles(w_in[:, gates:gates + D]), tiles(w_in[:, gates + D:])], 2),
        w_oab=np.stack([tiles(x["w_oA"][0]), tiles(x["w_oB"][0])], 2), w_o=tiles(x["w_o"][0]),
        w_gu=np.stack([wg, wu], 2), w_dn=x["moe_w_down"][0].reshape(E, 4, P, D).transpose(0, 2, 1, 3))
    nc = bacc.Bacc("TRN2", target_bir_lowering=False, num_devices=1)
    dram = {}
    for name, shape in SHAPES.items():
        arrays[name] = np.ascontiguousarray(arrays[name])
        assert arrays[name].shape == shape, (name, arrays[name].shape, shape)
        dram[name] = nc.dram_tensor(name, shape, F32, kind="ExternalInput").ap()
    for name, shape in OUT_SHAPES.items():
        dram[name] = nc.dram_tensor(name, shape, F32, kind="ExternalOutput").ap()
    build(nc, dram)
    r = run(nc, [arrays], core_ids=[0]).results[0]
    y = r["y"].transpose(2, 1, 0).reshape(M, D)
    shift = r["shift_out"].transpose(2, 1, 0).reshape(NSEQ + 1, D)
    conv = r["conv_out"].transpose(2, 1, 0).reshape(NSEQ + 1, 3, QKV_T * P)
    wkv_p = r["wkv_p"].reshape(2, C, T4, C).transpose(2, 0, 3, 1).reshape(1, 1, HR, C, C)
    wkv_s = r["wkv_s"].reshape(2, C, NSEQ, T4, C).transpose(2, 3, 0, 4, 1).reshape(1, NSEQ, HR, C, C)
    return (y[32:][None], y[:32].reshape(NSEQ, TSEQ, D), shift[None, NSEQ:], wkv_p, conv[None, NSEQ:],
            r["gdn_p"].transpose(1, 0, 2)[None, None], shift[None, :NSEQ], wkv_s, conv[None, :NSEQ],
            r["gdn_s"].transpose(1, 2, 0, 3)[None])
```

```python
from contextlib import ExitStack

import numpy as np

import concourse.bass as bass
from concourse import mybir

F32 = mybir.dt.float32
I32 = mybir.dt.int32
ACT = mybir.ActivationFunctionType
ALU = mybir.AluOpType
AX = mybir.AxisListType

P = 128
D = 1024
KD = D // P
NSEQ, TSEQ, META, SEQ = 8, 4, 16, 256
C = 64
COL_META, COL_S, COL_P = 16, 32, 64
N = COL_P + SEQ
NC = N // C
M = N - COL_S
RW_T, QKV_T, Z_T = 14, 12, 4
IN_T = RW_T + QKV_T + Z_T
HR, HG = 8, 4
T4 = 4
G, EG, E, FF = 4, 8, 32, 512
LEVELS = 6
SEG = (RW_T // 2, 9, 10, 13)
TAPS = 3
CAP = 64
E2 = E + 4
XC = 7 * NSEQ + 3 + META + SEQ
CONVN = XC - 3


class Cols:

    def __init__(self):
        self.at, self.width = {}, 0

    def add(self, name, n):
        self.at[name] = (self.width, self.width + n)
        self.width += n


CST = Cols()
for _name, _n in (("ident", P), ("ones", P), ("blockones", P), ("center", P), ("sum_r", T4 * 8),
                  ("spread_r", T4 * P), ("sum_g", 8 * 8), ("spread_g", 8 * P), ("gmask0", P),
                  ("gmask1", P), ("incl", N), ("strict", N), ("low", LEVELS * C), ("up", LEVELS * C),
                  ("seq", NSEQ + 1), ("carry", N), ("eps", 1), ("gn_eps", 1), ("one", 1),
                  ("first4", 4), ("first8", 8), ("before", P), ("iota", CAP), ("valid", 3)):
    CST.add(_name, _n)
PAR = Cols()
for _name, _n in (("norm1", KD), ("norm2", KD), ("normf", KD), ("mu", RW_T), ("w0", T4), ("a0", T4),
                  ("k_k", T4), ("k_a", T4), ("r_k", T4), ("ln_w", T4), ("ln_b", T4), ("conv", QKV_T * 4),
                  ("gdn_norm", 1), ("A_log", 1), ("dt_bias", 1), ("w2a2", 512), ("g2", 512), ("ab", KD * 8),
                  ("router", KD * 36), ("router_b", 36), ("conv_state", QKV_T * 24)):
    PAR.add(_name, _n)


def constants():
    c = np.zeros((P, CST.width), np.float32)

    def put(name, a, row=0):
        a = np.asarray(a, np.float32).reshape(len(a), -1)
        c[row:row + a.shape[0], CST.at[name][0]:CST.at[name][1]] = a

    i = np.arange(P)
    same = (i[:, None] // C == i[None] // C).astype(np.float32)
    put("ident", np.eye(P))
    put("ones", np.ones((P, P)))
    put("blockones", same)
    put("center", np.eye(P) - same / C)
    t, h = np.arange(T4), np.arange(8)
    put("sum_r", (2 * t[None, :, None] + (i // C)[:, None, None] == h[None, None]).astype(np.float32))
    put("spread_r", (h[:, None, None] == 2 * t[None, :, None] + (i // C)[None, None]).astype(np.float32))
    put("sum_g", np.broadcast_to((h[:, None] == h[None]), (P, 8, 8)))
    spread = np.broadcast_to((h[:, None, None] == h[None, :, None]), (8, 8, P))
    put("spread_g", spread)
    put("spread_g", spread, 32)
    seq = np.full(C, -1)
    seq[COL_META:COL_S] = NSEQ
    seq[COL_S:C] = np.arange(32) // TSEQ
    j = np.arange(C)
    together = [(seq[:, None] == seq[None]) & (seq[:, None] >= 0)] + [np.ones((C, C), bool)] * (NC - 1)
    incl = [g & (j[:, None] <= j[None]) for g in together]
    strict = [g & (j[:, None] < j[None]) for g in together]
    for n in (0, 1):
        put(f"gmask{n}", np.tile(np.concatenate([strict[n], incl[n]], 1), (2, 1)))
    put("incl", np.concatenate(incl, 1))
    put("strict", -np.concatenate(strict, 1).astype(np.float32))
    low = np.stack([(j[:, None] >> (n + 1) == j[None] >> (n + 1)) & (j[:, None] >> n & 1 == 1) & (j[None] >> n & 1 == 0)
                    for n in range(LEVELS)], 1)
    put("low", np.tile(low, (2, 1, 1)))
    put("up", np.tile(low.transpose(2, 1, 0), (2, 1, 1)))
    put("seq", np.tile(seq[:, None] == np.arange(NSEQ + 1)[None], (2, 1)))
    carry = np.ones(N)
    carry[[COL_META, *range(COL_S, C, TSEQ), *range(C, N, C)]] = 0
    put("carry", np.tile(carry, (P, 1)))
    put("eps", np.full(P, 1e-6))
    put("gn_eps", np.full(P, C * 1e-5))
    put("one", np.ones(P))
    put("first4", np.tile(np.arange(4, 0, -1), (P, 1)))
    put("first8", np.tile(np.arange(8, 0, -1), (P, 1)))
    put("before", i[:, None] < i[None])
    put("iota", np.tile(np.arange(CAP), (P, 1)))
    put("valid", i[:, None] + P * np.arange(3)[None] < M)
    return c


def build(nc, dram):
    ctx = ExitStack()
    with ctx:
        def sb(name, *shape):
            return ctx.enter_context(nc.sbuf_tensor(f"sb_{name}", [P, *shape], F32))

        def sem(name):
            return ctx.enter_context(nc.semaphore(name))

        cst = sb("cst", CST.width)
        par = sb("par", PAR.width)

        def K(name):
            return cst[:, CST.at[name][0]:CST.at[name][1]]

        def W(name):
            return par[:, PAR.at[name][0]:PAR.at[name][1]]

        def spread(ap, n):
            return ap.unsqueeze(len(ap.shape)).to_broadcast([*ap.shape, n])

        def over(ap, n):
            return ap.unsqueeze(1).to_broadcast([ap.shape[0], n, *ap.shape[1:]])

        xT = sb("xT", KD, N)
        yA = sb("yA", T4, M)
        yB = sb("yB", T4, M)
        rs = sb("rs", N)
        row_tmp = sb("row_tmp", N)
        ab_raw = sb("ab_raw", N)
        ARENA = 41200
        arena = sb("arena", ARENA)

        def at(start, *shape):
            n = int(np.prod(shape))
            assert start + n <= ARENA, (start, shape)
            v = arena[:, start:start + n]
            if len(shape) > 1:
                names = "abcde"[:len(shape)]
                v = v.rearrange(f"p ({' '.join(names)}) -> p {' '.join(names)}", **dict(zip(names, shape)))
            return v

        class Region:

            def __init__(self, start):
                self.pos = start

            def take(self, *shape):
                v = at(self.pos, *shape)
                self.pos += int(np.prod(shape))
                return v

        r = Region(0)
        xnT = r.take(KD, N)
        w_ring = [r.take(KD, P) for _ in range(2)]
        proj_at = r.pos
        proj = r.take(IN_T, N)
        xc = [r.take(XC) for _ in range(2)]
        conv_acc = [r.take(CONVN) for _ in range(2)]
        conv_out = r.take(QKV_T, 27)
        x_out = r.take(KD, NSEQ + 1)
        work_at = r.pos
        r = Region(work_at)
        temps_at = r.pos
        ta, tL, teL, tkk, t1, t2 = [r.take(T4, N) for _ in range(6)]
        bonus_at = r.pos
        tbonus = r.take(T4, N)
        tg = yB
        AR = r.take(T4, NC, 2, C)
        bk_at = r.pos
        BK = r.take(T4, NC, 2, C)
        GM = r.take(NC, HR, P)
        SV = r.take(NC, HR * C)
        BKt = r.take(NC, T4, P)
        PTs = r.take(T4, NC + NSEQ)
        small_r = rs
        r_end = r.pos
        r = Region(temps_at)
        XTr = r.take(NC, HR, C)
        invX = [r.take(T4, P) for _ in range(2)]
        invT = [r.take(T4, P) for _ in range(2)]
        Rs = r.take(HR * C)
        C0r = r.take(T4, 2, C)
        SVm = [r.take(HR * C) for _ in range(2)]
        STr = r.take(2, T4, P)
        assert r.pos <= temps_at + 6 * T4 * N
        r = Region(bk_at)
        ty, gn_sqv = r.take(T4, N), r.take(T4, M)
        r = Region(KD * N)
        invA, invXT = [r.take(T4, P) for _ in range(2)], [r.take(T4, P) for _ in range(2)]
        assert r.pos <= proj_at
        SW = at(proj_at, NSEQ, T4, P)
        assert NSEQ * T4 * P <= RW_T * N
        r = Region(work_at)
        KQ = r.take(HG, NC, 2, C)
        qdec = r.take(HG, N)
        eGb = r.take(HG, N)
        Dincl = r.take(HG, N)
        Dstr = r.take(HG, N)
        assert r.pos == bonus_at
        XTg = r.take(NC, HG, C)
        GA = r.take(NC, HG, C)
        QKD = r.take(NC, HG, C)
        assert r.pos == bk_at
        invXg, invTg = ([r.take(T4, P) for _ in range(2)] for _ in range(2))
        Rg = r.take(HG, P)
        sqg = at(r.pos, 8, N)
        kdec = r.take(NC, HG, P)
        bV = r.take(NC, HG, P)
        VNs = [r.take(HG * P) for _ in range(2)]
        VNm = [r.take(HG * P) for _ in range(2)]
        Sg = r.take(2, HG, P)
        C0g = r.take(HG, 2, C)
        rows = r.take(N)
        srow = xc[0][:, 0:N]
        cols = r.take(NC, P)
        ecols = r.take(NC, 8)
        oT = r.take(HG, N)
        g_end = r.pos
        r = Region(KD * N)
        wg_ring = [r.take(2, KD, P) for _ in range(2)]
        wo_ring = [r.take(2, T4, P) for _ in range(2)]
        wf_ring = [r.take(KD, P) for _ in range(2)]
        merged = r.take(KD, M)
        sgA = [r.take(M) for _ in range(2)]
        sgB = [r.take(M) for _ in range(2)]
        assert r.pos <= work_at
        r = Region(0)
        hT = r.take(KD, M)
        xt2 = r.take(KD, 3 * P)
        acc = r.take(KD, M)
        rt = r.take(3, 36)
        rte = r.take(3, G, EG)
        rt8 = [r.take(3, EG) for _ in range(4)]
        rt4 = r.take(3, G)
        rt1 = [r.take(3) for _ in range(7)]
        gate = r.take(3, E2)
        member = r.take(3, E)
        slot = r.take(3, E2)
        flag_f = r.take(1)
        flag = r.take(1).bitcast(I32)
        pair_at = r.pos
        sel, selG = r.take(3, 2, CAP), r.take(3, 2, CAP)
        selT = r.take(3 * P)
        logitsT = selT
        hidT = r.take(4, 2 * CAP)
        dense_at = r.pos
        gateT = r.take(3 * P)
        gsel = [r.take(M) for _ in range(2)]
        silu = [r.take(M) for _ in range(2)]
        hid = [r.take(4, M) for _ in range(2)]
        e_end = r.pos
        r = Region(dense_at)
        xtok = r.take(3, D)
        assert r.pos <= e_end
        r = Region(KD * M)
        xe = r.take(KD, 2 * CAP)
        ye = r.take(D)
        silu_s, hid_s = r.take(FF), r.take(FF)
        assert r.pos <= KD * M + KD * 3 * P
        assert e_end <= work_at
        r = Region(work_at)
        wgu = [r.take(2, KD, FF) for _ in range(1)]
        wdn = [r.take(4, D) for _ in range(1)]
        wgu.append(r.take(2, KD, FF))
        wdn.append(r.take(4, D))

        bank = [ctx.enter_context(nc.psum_tensor(f"bank{i}", [P, 512], F32)) for i in range(8)]

        def bk(i, *shape):
            v = bank[i][:, 0:int(np.prod(shape))]
            if len(shape) > 1:
                names = "abcde"[:len(shape)]
                v = v.rearrange(f"p ({' '.join(names)}) -> p {' '.join(names)}", **dict(zip(names, shape)))
            return v

        S = {n: sem(n) for n in (
            "rms_sq", "rms_mm", "rms_root", "head_sq", "head_sum", "head_root", "head_inv", "head_spread",
            "ld_cst", "ld_par", "ld_x", "xn", "x_packed",
            "ld_w0", "ld_w1", "proj_done", "psum_free", "ab_done",
            "shift_step", "zc_done", "lora_in", "lora_mm", "lora_out", "cum", "exps",
            "bonus_in", "bonus_mm", "bk_done", "gram_r",
            "gm_done", "bar_done", "v_tr", "v_sb", "bt_tr", "bt_sb", "z_dead",
            "sv_zero", "ld_sw", 
            "s0_mm", "s0_k", "s0_sb", "ch_rhs", "ch_rhs_sb", "ch_sa", "ch_sa_sb", "ch_y", "ch_y_sb", "ch_st", "ch_st_sb",
            "svm", "sm_mm", "sm_sb", "gn_in", "gn_d", "yA",
            "xc_init", "xc_step", "xc_ready", "xc_used", "conv_step", "conv_done", "silu_done", "z_done",
            "ab_rows", "ab_lin", "g_rows", "g_cum", "g_exp", "g_kd", "g_bc", "g_bc_dve", "g_bc_act", "d_arg", "d_exp", "d_done", "cols_tr", "ecol", "ecol2",
            "kq_done", "gram_g", "ga_done", "kv_tr", "kv_sb",
            "rwkv_over", "yB",
            "ld_wg0", "ld_wg1", "ld_wf0", "ld_wf1", "op_mm", "op_sig", "op_free", "op_merge", "fin_mm", "h_done",
            "xt2", "rt_mm", "rt_lin", "rt_sb", "rt_sum", "rt_exp", "gate",
            "ld_e0", "ld_e1", "ld_d0", "ld_d1", "acc", "gu_free",
            "rt_member", "rt_pos", "flag", "xt_tr", "xtok", "sp_sel", "sp_selg", "sp_gather", "xe", "sp_gate", "sp_up", "sp_silu",
            "sp_hid", "sp_ht", "hidT", "sp_dn", "sp_ye", "ld_gate", "ld_up", "ld_dn", "sp_comb", "sp_acc", "sp_selT", "selT", "moe_done", "y_ready",
            "act_own", "dve_own", "moe_own", "ab_sb", "acc_init", "stores",
            "at_zero", "inv_out", "inv_at0", "inv_at1", "inv_t10", "inv_t11", "inv_t1s0", "inv_t1s1", "inv_t20", "inv_t21", "inv_upd0", "inv_upd1")}
        for dense_step, same_as in (("gsel", "sp_sel"), ("gb_mm", "sp_comb"), ("gu_mm", "sp_gate"), ("silu", "sp_silu"),
                                    ("hid_step", "hidT"), ("hid", "sp_hid"), ("dn_mm", "sp_dn"), ("gt_tr", "sp_selT"),
                                    ("gateT", "selT")):
            S[dense_step] = S[same_as]

        rate = eGb[0:4, 0, 0:1]
        ones_at_start, eps_at_start = yA[:, 0, 0:P], yA[:, 1, 0:1]
        t_sq = AR.rearrange("p t c x s -> p (t c x s)").rearrange("p (k n) -> p k n", k=KD)
        xw, sgx = tbonus[0:C, 0, :], tbonus[:, 1, :]
        sqg_o = sqg.rearrange("p t n -> p (t n)")[:, 0:HG * M].rearrange("p (t n) -> p t n", t=HG)

        jobs_r = [(GM[0:C, c, :, 0:C], XTr[0:C, c], T4, LEVELS if c else 4, invA[q], invX[q], invT[q], invXT[q])
                  for q, c in ((0, 1), (1, 2), (0, 3), (1, 4), (0, 0))]
        jobs_g = []
        for n, c in enumerate(range(0, NC, 2)):
            end, q = min(c + 2, NC), n % 2
            jobs_g.append((GA[0:C, c:end].rearrange("p c h s -> p (c h) s"), XTg[0:C, c:end].rearrange("p c h s -> p (c h) s"),
                           (end - c) * HG // 2, LEVELS, invA[q], invXg[q], invTg[q], invXT[q]))
        before = {}
        slot_sum = [[0, 0], [0, 0]]
        for name, jobs in (("r", jobs_r), ("g", jobs_g)):
            before[name] = []
            for n, job in enumerate(jobs):
                before[name].append(tuple(slot_sum[n % 2]))
                slot_sum[n % 2][0] += 1
                slot_sum[n % 2][1] += job[3]

        def rounds(name):
            jobs = jobs_r if name == "r" else jobs_g
            for n in range(0, len(jobs), 2):
                yield [(q, *before[name][n + q], job) for q, job in enumerate(jobs[n:n + 2])]

        def heads(v, odd):
            return v[:, odd::2, :]

        def blocks(v, odd, n):
            return v[C:P, 0:n, C:P] if odd else v[0:C, 0:n, 0:C]

        def halved(v, n):
            return v[:, 0:n, :].rearrange("p t (x s) -> p (t x) s", x=2)

        block = ctx.enter_context(nc.Block())

        def own(eng, name):
            count = [0]

            def step(ins):
                count[0] += 1
                ins.then_inc(S[name], 1)
                eng.wait_ge(S[name], count[0])
            return step

        halves = [(0, slice(0, C)), (1, slice(C, P))]
        n_stores = 7

        @block.sync
        def _(sp):
            sp.dma_start(xT[:, :, :], dram["xT"]).then_inc(S["ld_x"], 16)
            sp.dma_start(par[:, :], dram["par"]).then_inc(S["ld_par"], 16)
            for k in range(2):
                sp.dma_start(w_ring[k], dram["w_in"][k]).then_inc(S[f"ld_w{k}"], 16)
            sp.dma_start(cst[:, :], dram["cst"]).then_inc(S["ld_cst"], 16)
            with sp.Fori(1, IN_T // 2) as i:
                for k in range(2):
                    sp.wait_ge(S["proj_done"], 2 * i + k - 1)
                    sp.dma_start(w_ring[k], dram["w_in"][bass.ds(2 * i + k, 1)].rearrange("a p k c -> p (a k) c"))\
                      .then_inc(S[f"ld_w{k}"], 16)
            sp.wait_ge(S["x_packed"], 1)
            sp.dma_start(dram["shift_out"], x_out).then_inc(S["stores"], 16)
            sp.wait_ge(S["z_dead"], 3)
            for par_, rows_ in halves:
                sp.dma_start(SW[rows_, :, :, par_ * C:par_ * C + C], dram["wkv_in"][rows_]).then_inc(S["ld_sw"], 16)
            sp.wait_ge(S["conv_done"], QKV_T)
            sp.wait_ge(S["xc_ready"], QKV_T)
            sp.dma_start(dram["conv_out"], conv_out).then_inc(S["stores"], 16)
            sp.wait_ge(S["ch_st_sb"], NC)
            for par_, rows_ in halves:
                sp.dma_start(dram["wkv_p"][rows_], STr[rows_, (NC - 1) % 2, :, par_ * C:par_ * C + C]).then_inc(S["stores"], 16)
            sp.wait_ge(S["sm_sb"], NSEQ)
            sp.wait_ge(S["ch_y_sb"], NC)
            sp.wait_ge(S["stores"], 16 * 4)
            sp.sem_inc(S["rwkv_over"], 1)
            for par_, rows_ in halves:
                sp.dma_start(dram["wkv_s"][rows_], SW[rows_, :, :, par_ * C:par_ * C + C]).then_inc(S["stores"], 16)
            sp.wait_ge(S["stores"], 16 * 6)
            sp.dma_start(SW, dram["gdn_in"]).then_inc(S["ld_sw"], 16)
            sp.wait_ge(S["sm_sb"], 2 * NSEQ)
            sp.dma_start(dram["gdn_s"], SW).then_inc(S["stores"], 16)
            sp.wait_ge(S["ch_st_sb"], 2 * NC)
            sp.dma_start(dram["gdn_p"], Sg[:, (NC - 1) % 2]).then_inc(S["stores"], 16)
            sp.wait_ge(S["inv_out"], len(jobs_r) + len(jobs_g))
            sp.wait_ge(S["stores"], 16 * 8)

            def load_out(i, k):
                one = dram["w_gab"][bass.ds(i, 1)] if not isinstance(i, int) else dram["w_gab"][i:i + 1]
                two = dram["w_oab"][bass.ds(i, 1)] if not isinstance(i, int) else dram["w_oab"][i:i + 1]
                sp.dma_start(wg_ring[k], one.rearrange("a p g k c -> p (a g) k c")).then_inc(S[f"ld_wg{k}"], 16)
                sp.dma_start(wo_ring[k], two.rearrange("a p g k c -> p (a g) k c")).then_inc(S[f"ld_wg{k}"], 16)

            parts = (("ld_gate", "sp_gate"), ("ld_up", "sp_up"), ("ld_dn", "sp_dn"))

            def load_pair(i, part):
                for k in range(2):
                    if part < 2:
                        src = dram["w_gu"][bass.ds(2 * i + k, 1), :, part].rearrange("a p k c -> p (a k) c")
                        dst = wgu[k][:, part]
                    else:
                        src = dram["w_dn"][bass.ds(2 * i + k, 1)].rearrange("a p k c -> p (a k) c")
                        dst = wdn[k]
                    sp.dma_start(dst, src).then_inc(S[parts[part][0]], 16)

            for k in range(2):
                load_out(k, k)
            for k in range(2):
                sp.dma_start(wf_ring[k], dram["w_o"][k]).then_inc(S[f"ld_wf{k}"], 16)
            for i in range(1, KD // 2):
                for k in range(2):
                    sp.wait_ge(S["op_mm"], 2 * i + k - 1)
                    load_out(2 * i + k, k)
                load_pair(0, i - 1)
            with sp.Fori(1, KD // 2) as i:
                for k in range(2):
                    sp.wait_ge(S["fin_mm"], 2 * i + k - 1)
                    sp.dma_start(wf_ring[k], dram["w_o"][bass.ds(2 * i + k, 1)].rearrange("a p k c -> p (a k) c"))\
                      .then_inc(S[f"ld_wf{k}"], 16)
            def load_by_pairs():
                with sp.Fori(1, E // 2) as i:
                    for part in range(3):
                        sp.wait_ge(S[parts[part][1]], i)
                        load_pair(i, part)

            def load_by_experts():
                for ld, _ in parts:
                    sp.wait_ge(S[ld], 32)
                for k in range(2):
                    sp.sem_inc(S[f"ld_e{k}"], 16)
                    sp.sem_inc(S[f"ld_d{k}"], 16)
                with sp.Fori(1, E // 2) as i:
                    for k in range(2):
                        sp.wait_ge(S["gu_mm"], 4 * (2 * i + k - 1))
                        sp.dma_start(wgu[k], dram["w_gu"][bass.ds(2 * i + k, 1)].rearrange("a p g k c -> p (a g) k c"))\
                          .then_inc(S[f"ld_e{k}"], 16)
                        sp.wait_ge(S["dn_mm"], KD * (2 * i + k - 1))
                        sp.dma_start(wdn[k], dram["w_dn"][bass.ds(2 * i + k, 1)].rearrange("a p k c -> p (a k) c"))\
                          .then_inc(S[f"ld_d{k}"], 16)

            sp.wait_ge(S["flag"], 1)
            crowded = sp.value_load(flag[0:1, 0:1], min_val=0, max_val=1)
            with sp.If(crowded < 1):
                load_by_pairs()
            with sp.Else():
                load_by_experts()
            sp.wait_ge(S["y_ready"], 1)
            sp.dma_start(dram["y"], acc).then_inc(S["stores"], 16)
            sp.wait_ge(S["stores"], 16 * 9)

        @block.tensor
        def _(pe):
            mm = pe.matmul
            pe.wait_ge(S["xc_init"], 1)
            pe.wait_ge(S["rms_sq"], 1)
            for k in range(KD):
                last = mm(bk(7, N), ones_at_start, t_sq[:, k, :], start=(k == 0), stop=(k == KD - 1))
            last.then_inc(S["rms_mm"], 1)
            pe.wait_ge(S["xn"], 1)

            def project_in(first, end):
                with pe.Fori(first, end) as i:
                    for s in range(2):
                        pe.wait_ge(S[f"ld_w{s}"], 16 * i + 16)
                        pe.wait_ge(S["psum_free"], 2 * i + s + 1)
                        for k in range(KD):
                            last = mm(bk(s, N), w_ring[s][:, k, :], xnT[:, k, :], start=(k == 0), stop=(k == KD - 1))
                        last.then_inc(S["proj_done"], 1)

            project_in(0, SEG[0])
            pe.wait_ge(S["ld_cst"], 16)
            pe.wait_ge(S["ld_par"], 16)
            wab = W("ab").rearrange("p (k c) -> p k c", k=KD)
            for b, lo, rows_ in ((2, 0, slice(0, 4)), (3, 4, slice(32, 36))):
                for k in range(KD):
                    last = mm(bank[b][rows_, 0:N], wab[:, k, lo:lo + 4], xnT[:, k, :], start=(k == 0), stop=(k == KD - 1))
                last.then_inc(S["ab_done"], 1)

            project_in(SEG[0], SEG[1])
            pe.wait_ge(S["ab_sb"], 2)
            pe.wait_ge(S["lora_in"], 2)
            for part in range(3):
                for t in range(T4):
                    if part:
                        pe.wait_ge(S["lora_out"], T4 * (part - 1) + t + 1)
                    lo = slice(t * P, t * P + P)
                    if part == 0:
                        ins = mm(bk(4 + t, N), W("w2a2")[0:C, lo], xw, start=True, stop=True)
                    elif part == 1:
                        ins = mm(bk(4 + t, N), W("w2a2")[C:P, lo], proj[C:P, 12, :], start=True, stop=True)
                    else:
                        ins = mm(bk(4 + t, N), W("g2")[:, lo], sgx, start=True, stop=True)
                    ins.then_inc(S["lora_mm"], 1)
            sum_r = K("sum_r").rearrange("p (t h) -> p t h", t=T4)
            spread_r = K("spread_r").rearrange("p (t c) -> p t c", t=T4)
            pe.wait_ge(S["head_sq"], 1)
            for t in range(T4):
                last = mm(bank[3][0:8, 0:N], sum_r[:, t, :], t2[:, t, :], start=(t == 0), stop=(t == T4 - 1))
            last.then_inc(S["head_sum"], 1)
            project_in(SEG[1], SEG[2])
            pe.wait_ge(S["head_inv"], 1)
            pe.wait_ge(S["lora_out"], 3 * T4)
            for t in range(T4):
                mm(bk(4 + t, N), spread_r[0:8, t, :], small_r[0:8, :], start=True, stop=True).then_inc(S["head_spread"], 1)
            project_in(SEG[2], SEG[3])
            pe.wait_ge(S["bonus_in"], 1)
            for t in range(T4):
                mm(bk(4 + t, N), K("blockones"), t2[:, t, :], start=True, stop=True).then_inc(S["bonus_mm"], 1)
            pe.wait_ge(S["bk_done"], 1)
            pe.wait_ge(S["z_dead"], 1)
            for c in range(NC):
                for p_, rows_ in halves:
                    n = 2 * c + p_
                    if n >= 4:
                        pe.wait_ge(S["gm_done"], n - 3)
                    for t in range(T4):
                        last = mm(bank[4 + n % 4][:, t * P:t * P + P], BK[rows_, t, c].rearrange("p a b -> p (a b)"),
                                  AR[rows_, t, c].rearrange("p a b -> p (a b)"), start=True, stop=True)
                    last.then_inc(S["gram_r"], 1)
            flat = arena[:, proj_at:proj_at + IN_T * N]
            for c in range(NC):
                if c >= 2:
                    pe.wait_ge(S["v_sb"], c - 1)
                for t in range(T4):
                    lo = (8 + t) * N + C * c - C
                    last = pe.transpose(bank[2 + c % 2][:, t * P:t * P + P], flat[:, lo:lo + P], K("ident"))
                last.then_inc(S["v_tr"], 1)
            project_in(SEG[3], IN_T // 2)
            pe.wait_ge(S["psum_free"], IN_T + 2)
            pe.wait_ge(S["bar_done"], 1)
            pe.wait_ge(S["v_sb"], NC)
            for c in range(NC):
                if c >= 4:
                    pe.wait_ge(S["bt_sb"], c - 3)
                for t in range(T4):
                    last = pe.transpose(bank[c % 4][:, t * P:t * P + P], BK[:, t, c].rearrange("p a b -> p (a b)"), K("ident"))
                last.then_inc(S["bt_tr"], 1)

            def start_states(name, b):
                r, end = name == "r", COL_S + TSEQ * (b + 1)
                c0 = bk(6, T4, 2, C)
                if b == NSEQ - 1:
                    pe.wait_ge(S["ld_sw"], 32 if r else 48)
                    pe.wait_ge(S["z_dead"], 3)
                for t in range(T4):
                    src = AR[:, t, 0, :, 0:end] if r else KQ[:, t, 0, :, 0:end]
                    last = mm(c0[:, t, :, 0:end], SW[:, b, t, :], src, start=True, stop=True)
                if b == 0:
                    last.then_inc(S["s0_mm"], 1)

            def invert(name):
                done = 0
                for two in rounds(name):
                    last_round = len(two) == 1
                    for level in range(max(j[3][3] for j in two)):
                        now = [j for j in two if level < j[3][3]]
                        for slot, n_jobs, n_levels, (_, _, n, levels, A_T, X, T1, X_T) in now:
                            pe.wait_ge(S[f"inv_upd{slot}"], n_levels + n_jobs + level + 1)
                            for t in range(n):
                                rhs = K("ident") if level == 0 else X[:, t, :]
                                last = mm(bank[3 * slot][:, t * P:t * P + P], A_T[:, t, :], rhs, start=True, stop=True)
                            last.then_inc(S[f"inv_t1{slot}"], 1)
                        if last_round:
                            for b in range(done, min(done + 2, NSEQ)):
                                start_states(name, NSEQ - 1 - b)
                            done = min(done + 2, NSEQ)
                        if level == 0:
                            continue
                        for slot, n_jobs, n_levels, (_, _, n, levels, A_T, X, T1, X_T) in now:
                            pe.wait_ge(S[f"inv_t1s{slot}"], n_levels - n_jobs + level)
                            for t in range(n):
                                if level < levels - 1:
                                    mm(bank[3 * slot + 1][:, t * P:t * P + P], X_T[:, t, :], T1[:, t, :], start=True, stop=True)
                                last = mm(bank[3 * slot + 2][:, t * P:t * P + P], T1[:, t, :], X_T[:, t, :], start=True, stop=True)
                            last.then_inc(S[f"inv_t2{slot}"], 1)
                pe.wait_ge(S["inv_out"], len(jobs_r) + (len(jobs_g) if name == "g" else 0))

            pe.wait_ge(S["gm_done"], 2 * NC)
            pe.wait_ge(S["bt_sb"], NC)
            invert("r")

            pe.wait_ge(S["s0_sb"], 1)

            def sample_state(name, n):
                k = n + (0 if name == "r" else NSEQ + 1)
                pe.wait_ge(S["svm"], k + 1)
                if n >= 3:
                    pe.wait_ge(S["sm_sb"], n - 2 + (0 if name == "r" else NSEQ))
                for t in range(T4):
                    lo = slice(t * P, t * P + P)
                    if name == "r":
                        last = mm(bank[4 + n % 2][:, lo], BKt[:, 0, t, :], SVm[n % 2][:, lo], start=True, stop=True)
                    else:
                        last = mm(bank[4 + n % 2][:, lo], kdec[0:C, 0, t, :], VNm[n % 2][0:C, lo], start=True, stop=True)
                last.then_inc(S["sm_mm"], 1)

            for c in range(NC):
                if c:
                    pe.wait_ge(S["ch_st_sb"], c)
                for t in range(T4):
                    lhs, rhs = (C0r[:, t, 0, :], K("ident")) if c == 0 else (AR[:, t, c, 0, :], STr[:, (c - 1) % 2, t, :])
                    mm(bank[0][0:C, t * P:t * P + P], lhs, rhs, start=True, stop=False)
                    for h in (2 * t, 2 * t + 1):
                        last = mm(bank[0][0:C, h * C:h * C + C], GM[:, c, h, 0:C], SV[:, c, h * C:h * C + C],
                                  start=False, stop=(h % 2 == 1))
                last.then_inc(S["ch_rhs"], 1)
                if c:
                    sample_state("r", 2 * c - 1)
                pe.wait_ge(S["ch_rhs_sb"], c + 1)
                for h in range(HR):
                    last = mm(bank[1][0:C, h * C:h * C + C], XTr[0:C, c, h, :], Rs[0:C, h * C:h * C + C], start=True, stop=True)
                last.then_inc(S["ch_sa"], 1)
                if c:
                    sample_state("r", 2 * c)
                pe.wait_ge(S["ch_sa_sb"], c + 1)
                if c == 0:
                    sample_state("r", 0)
                else:
                    for t in range(T4):
                        last = mm(bank[2][:, t * P:t * P + P], BKt[:, c, t, :], SV[:, c, t * P:t * P + P], start=True, stop=True)
                    last.then_inc(S["ch_st"], 1)
                if c:
                    pe.wait_ge(S["ch_y_sb"], c)
                for t in range(T4):
                    lhs, rhs = (K("ident"), C0r[:, t, 1, :]) if c == 0 else (STr[:, (c - 1) % 2, t, :], AR[:, t, c, 1, :])
                    mm(bank[3][:, t * C:t * C + C], lhs, rhs, start=True, stop=False)
                    for p_, rows_ in halves:
                        h = 2 * t + p_
                        last = mm(bank[3][rows_, t * C:t * C + C], SV[:, c, h * C:h * C + C], GM[:, c, h, C:P],
                                  start=False, stop=True)
                last.then_inc(S["ch_y"], 1)
            pe.wait_ge(S["ch_y_sb"], NC)
            pe.wait_ge(S["sm_sb"], NSEQ)
            for t in range(T4):
                mm(bk(4 + t, M), K("center"), ty[:, t, COL_S:], start=True, stop=True).then_inc(S["gn_d"], 1)
            pe.wait_ge(S["head_sq"], 2)
            for t in range(T4):
                last = mm(bank[3][0:8, 0:M], sum_r[:, t, :], gn_sqv[:, t, :], start=(t == 0), stop=(t == T4 - 1))
            last.then_inc(S["head_sum"], 1)
            pe.wait_ge(S["head_inv"], 2)
            for t in range(T4):
                mm(bk(4 + t, M), spread_r[0:8, t, :], small_r[0:8, 0:M], start=True, stop=True).then_inc(S["head_spread"], 1)

            sum_g = K("sum_g").rearrange("p (t h) -> p t h", t=8)
            spread_g = K("spread_g").rearrange("p (t c) -> p t c", t=8)
            pe.wait_ge(S["head_sq"], 3)
            for t in range(8):
                last = mm(bank[0][0:8, 0:N], sum_g[:, t, :], sqg[:, t, :], start=(t == 0), stop=(t == 7))
            last.then_inc(S["head_sum"], 1)
            pe.wait_ge(S["yA"], 1)
            pe.wait_ge(S["g_kd"], 1)
            for h in range(HG):
                if h:
                    pe.wait_ge(S["g_bc_dve"], 2 * h)
                    pe.wait_ge(S["g_bc_act"], h)
                mm(bank[4][0:C, 0:N], spread_g[0:4, h, 0:C], rows[0:4, :], start=True, stop=True).then_inc(S["g_bc"], 1)
                mm(bank[5][0:C, 0:N], spread_g[32:36, h, 0:C], rows[32:36, :], start=True, stop=True).then_inc(S["g_bc"], 1)
                mm(bk(6, N), spread_g[0:4, h, :], row_tmp[0:4, :], start=True, stop=True).then_inc(S["g_bc"], 1)
            for c in range(NC):
                last = pe.transpose(bank[7][0:C, c * 96:c * 96 + 96], rows[0:96, c * C:c * C + C], K("ident")[0:96, 0:96])
            last.then_inc(S["cols_tr"], 1)
            pe.wait_ge(S["head_inv"], 3)
            for t in range(8):
                if t >= 3:
                    pe.wait_ge(S["kq_done"], t - 2)
                mm(bk(1 + t % 3, N), spread_g[0:8, t, :], srow[0:8, :], start=True, stop=True).then_inc(S["head_spread"], 1)
            pe.wait_ge(S["kq_done"], 8)
            pe.wait_ge(S["ecol2"], 1)
            for c in range(NC):
                for w_ in range(2):
                    n = 2 * c + w_
                    if n >= 4:
                        pe.wait_ge(S["kv_sb"], n - 3)
                    for h in range(HG):
                        src = KQ[:, h, c, 0, :] if w_ == 0 else proj[:, 22 + h, c * C:c * C + C]
                        last = pe.transpose(bank[(0, 1, 4, 5)[n % 4]][0:C, h * P:h * P + P], src, K("ident"))
                    last.then_inc(S["kv_tr"], 1)
            pe.wait_ge(S["d_done"], 1)
            for c in range(NC):
                if c >= 2:
                    pe.wait_ge(S["ga_done"], c - 1)
                for h in range(HG):
                    last = mm(bank[2 + c % 2][0:C, h * P:h * P + P], KQ[:, h, c, 0, :],
                              KQ[:, h, c].rearrange("p a b -> p (a b)"), start=True, stop=True)
                last.then_inc(S["gram_g"], 1)
            pe.wait_ge(S["ga_done"], NC)
            pe.wait_ge(S["kv_sb"], 2 * NC)
            invert("g")
            pe.wait_ge(S["s0_sb"], 2)
            for c in range(NC):
                if c:
                    pe.wait_ge(S["ch_st_sb"], NC + c)
                for h in range(HG):
                    lhs, rhs = (C0g[:, h, 0, :], K("ident")) if c == 0 else (KQ[:, h, c, 0, :], Sg[:, (c - 1) % 2, h, :])
                    last = mm(bank[0][0:C, h * P:h * P + P], lhs, rhs, start=True, stop=True)
                last.then_inc(S["ch_rhs"], 1)
                if c:
                    sample_state("g", 2 * c - 1)
                pe.wait_ge(S["ch_rhs_sb"], NC + c + 1)
                for h in range(HG):
                    last = mm(bank[1][0:C, h * P:h * P + P], XTg[0:C, c, h, :], Rg[0:C, h, :], start=True, stop=True)
                last.then_inc(S["ch_sa"], 1)
                if c:
                    sample_state("g", 2 * c)
                pe.wait_ge(S["ch_sa_sb"], NC + c + 1)
                if c == 0:
                    sample_state("g", 0)
                else:
                    for h in range(HG):
                        last = mm(bank[2][:, h * P:h * P + P], kdec[0:C, c, h, :], VNs[c > 0][0:C, h * P:h * P + P], start=True, stop=True)
                    last.then_inc(S["ch_st"], 1)
                if c:
                    pe.wait_ge(S["ch_y_sb"], NC + c)
                for h in range(HG):
                    lhs, rhs = (K("ident"), C0g[:, h, 1, :]) if c == 0 else (Sg[:, (c - 1) % 2, h, :], qdec[:, h, c * C:c * C + C])
                    mm(bank[3][:, h * C:h * C + C], lhs, rhs, start=True, stop=False)
                    last = mm(bank[3][:, h * C:h * C + C], VNs[c > 0][0:C, h * P:h * P + P], QKD[0:C, c, h, :], start=False, stop=True)
                last.then_inc(S["ch_y"], 1)
            pe.wait_ge(S["head_sq"], 4)
            for h in range(HG):
                last = mm(bank[0][0:8, 0:M], sum_g[:, h, :], sqg_o[:, h, :], start=(h == 0), stop=(h == HG - 1))
            last.then_inc(S["head_sum"], 1)
            pe.wait_ge(S["head_inv"], 4)
            pe.wait_ge(S["sm_sb"], 2 * NSEQ)
            for h in range(HG):
                mm(bk(4 + h, M), spread_g[0:8, h, :], srow[0:8, 0:M], start=True, stop=True).then_inc(S["head_spread"], 1)

            pe.wait_ge(S["yB"], 1)
            with pe.Fori(0, KD // 2) as i:
                for s in range(2):
                    pe.wait_ge(S[f"ld_wg{s}"], 32 * i + 32)
                    pe.wait_ge(S["op_free"], 2 * i + s + 1)
                    for g in range(2):
                        for k in range(KD):
                            mm(bk(4 * s + g, M), wg_ring[s][:, g, k, :], xnT[:, k, COL_S:], start=(k == 0), stop=(k == KD - 1))
                    for g, y_ in ((0, yA), (1, yB)):
                        for k in range(T4):
                            last = mm(bk(4 * s + 2 + g, M), wo_ring[s][:, g, k, :], y_[:, k, :], start=(k == 0), stop=(k == T4 - 1))
                    last.then_inc(S["op_mm"], 1)
            pe.wait_ge(S["op_merge"], KD)
            with pe.Fori(0, KD // 2) as i:
                for s in range(2):
                    pe.wait_ge(S[f"ld_wf{s}"], 16 * i + 16)
                    pe.wait_ge(S["op_free"], KD + 2 * i + s + 1)
                    for k in range(KD):
                        last = mm(bk(s, M), wf_ring[s][:, k, :], merged[:, k, :], start=(k == 0), stop=(k == KD - 1))
                    last.then_inc(S["fin_mm"], 1)
            pe.wait_ge(S["rms_sq"], 1 + KD)
            for k in range(KD):
                last = mm(bk(7, M), K("ones"), acc[:, k, :], start=(k == 0), stop=(k == KD - 1))
            last.then_inc(S["rms_mm"], 1)
            pe.wait_ge(S["xt2"], 1)
            router = W("router").rearrange("p (k c) -> p k c", k=KD)
            for k in range(KD):
                last = mm(bank[5][0:36, 0:3 * P], router[:, k, :], xt2[:, k, :], start=(k == 0), stop=(k == KD - 1))
            last.then_inc(S["rt_lin"], 1)
            for m in range(3):
                for half in range(2):
                    n = 2 * m + half
                    if n >= 4:
                        pe.wait_ge(S["xtok"], n - 3)
                    for k in range(4):
                        last = pe.transpose(bank[n % 4][:, k * P:k * P + P], xt2[:, 4 * half + k, m * P:m * P + P], K("ident"))
                    last.then_inc(S["xt_tr"], 1)
                    if n == 0:
                        pe.wait_ge(S["rt_sb"], 1)
                        for q in range(3):
                            last = pe.transpose(bank[6][:, q * 36:q * 36 + 36], logitsT[0:36, q * P:q * P + P], K("ident")[0:36, 0:36])
                        last.then_inc(S["rt_mm"], 1)
            pe.wait_ge(S["rt_member"], 1)
            for m in range(3):
                for q in range(m + 1):
                    last = mm(bank[6][:, m * E:m * E + E], K("before" if q == m else "ones"), member[:, q, :],
                              start=(q == 0), stop=(q == m))
            for m in range(3):
                last = mm(bank[6][:, 3 * E:4 * E], K("ones"), member[:, m, :], start=(m == 0), stop=(m == 2))
            last.then_inc(S["rt_pos"], 1)

            def dense():
                pe.wait_ge(S["gate"], 1)
                for m in range(3):
                    last = pe.transpose(bank[7][0:E, m * P:m * P + P], gate[:, m, 0:E], K("ident"))
                last.then_inc(S["gt_tr"], 1)
                pe.wait_ge(S["gateT"], 1)
                with pe.Fori(0, E // 2) as i:
                    for s in range(2):
                        e = 2 * i + s
                        pe.wait_ge(S["gsel"], e + 1)
                        mm(bk(6, M), K("ones")[0:E, :], gsel[s][0:E, :], start=True, stop=True).then_inc(S["gb_mm"], 1)
                        pe.wait_ge(S[f"ld_e{s}"], 16 * i + 16)
                        for f in range(4):
                            pe.wait_ge(S["gu_free"], 4 * e + f + 1)
                            for g in range(2):
                                for k in range(KD):
                                    last = mm(bk(2 * (f % 2) + g, M), wgu[s][:, g, k, f * P:f * P + P], xt2[:, k, 0:M],
                                              start=(k == 0), stop=(k == KD - 1))
                            last.then_inc(S["gu_mm"], 1)
                        pe.wait_ge(S[f"ld_d{s}"], 16 * i + 16)
                        pe.wait_ge(S["hid"], 4 * e + 4)
                        for j in range(KD):
                            pe.wait_ge(S["acc"], KD * e + j + 1)
                            for k in range(4):
                                last = mm(bk(4 + j % 2, M), wdn[s][:, k, j * P:j * P + P], hid[s][:, k, :], start=(k == 0), stop=(k == 3))
                            last.then_inc(S["dn_mm"], 1)

            def sparse():
                pe.wait_ge(S["xtok"], 6)

                def gather():
                    for k in range(KD):
                        for m in range(3):
                            last = mm(bank[2 + k // 4][:, k % 4 * P:k % 4 * P + P], xtok[:, m, k * P:k * P + P],
                                      sel[:, m].rearrange("p s c -> p (s c)"), start=(m == 0), stop=(m == 2))
                    last.then_inc(S["sp_gather"], 1)

                def project(b, n_k, rows, weights):
                    for k in range(n_k):
                        for s in range(2):
                            half = slice(s * CAP, s * CAP + CAP)
                            last = mm(bank[b][half, :], rows[:, k, half], weights(s, k), start=(k == 0), stop=(k == n_k - 1))
                    return last

                def hidden(i, first):
                    pe.wait_ge(S["ld_gate"], 32 * i + 32)
                    pe.wait_ge(S["xe"], i + 1)
                    if not first:
                        pe.wait_ge(S["hidT"], i)
                    project(0, KD, xe, lambda s, k: wgu[s][:, 0, k, :]).then_inc(S["sp_gate"], 1)
                    pe.wait_ge(S["ld_up"], 32 * i + 32)
                    if not first:
                        pe.wait_ge(S["selT"], i)
                    project(1, KD, xe, lambda s, k: wgu[s][:, 1, k, :]).then_inc(S["sp_up"], 1)

                def turn_hidden(i):
                    pe.wait_ge(S["sp_hid"], i + 1)
                    for f in range(4):
                        last = pe.transpose(bank[0][:, f * P:f * P + P], hid_s[:, f * P:f * P + P], K("ident"))
                    last.then_inc(S["sp_ht"], 1)

                def turn_gates(i):
                    pe.wait_ge(S["sp_selg"], i + 1)
                    for m in range(3):
                        last = pe.transpose(bank[1][:, m * P:m * P + P], selG[:, m].rearrange("p s c -> p (s c)"), K("ident"))
                    last.then_inc(S["sp_selT"], 1)

                def combine(i):
                    pe.wait_ge(S["sp_ye"], i)
                    pe.wait_ge(S["selT"], i)
                    for j in range(KD):
                        pe.wait_ge(S["sp_acc"], KD * (i - 1) + j + 1)
                        mm(bk(6 + j % 2, M), ye[:, j * P:j * P + P], selT[:, 0:M], start=True, stop=True).then_inc(S["sp_comb"], 1)

                def down(i, first):
                    pe.wait_ge(S["ld_dn"], 32 * i + 32)
                    pe.wait_ge(S["hidT"], i + 1)
                    if not first:
                        pe.wait_ge(S["sp_ye"], i)
                    for half in range(2):
                        last = project(4 + half, 4, hidT, lambda s, k: wdn[s][:, k, half * 512:half * 512 + 512])
                    last.then_inc(S["sp_dn"], 1)

                def pair(i, first):
                    hidden(i, first)
                    pe.wait_ge(S["sp_sel"], i + 2)
                    gather()
                    turn_hidden(i)
                    if not first:
                        combine(i)
                    turn_gates(i)
                    down(i, first)

                pe.wait_ge(S["sp_sel"], 1)
                gather()
                pair(0, True)
                with pe.Fori(1, E // 2) as i:
                    pair(i, False)
                combine(E // 2)

            pe.wait_ge(S["flag"], 1)
            crowded = pe.value_load(flag[0:1, 0:1], min_val=0, max_val=1)
            with pe.If(crowded < 1):
                sparse()
            with pe.Else():
                dense()
            pe.wait_ge(S["rms_sq"], 2 + KD)
            for k in range(KD):
                last = mm(bk(7, M), K("ones"), xt2[:, k, 0:M], start=(k == 0), stop=(k == KD - 1))
            last.then_inc(S["rms_mm"], 1)

        @block.scalar
        def _(act):
            A = nc.scalar.activation
            step = own(act, "act_own")
            act.wait_ge(S["ld_x"], 16)
            A(t_sq, xT[:, :, :], ACT.Square).then_inc(S["rms_sq"], 1)
            act.wait_ge(S["xc_init"], 1)
            act.wait_ge(S["rms_mm"], 1)
            A(rs[:, :], bk(7, N), ACT.Sqrt, bias=eps_at_start, scale=1.0 / D).then_inc(S["rms_root"], 1)
            act.sem_inc(S["psum_free"], 2)
            act.sem_inc(S["op_free"], 2)
            act.sem_inc(S["silu_done"], 2)

            def evict(first, end):
                with act.Fori(first, end) as i:
                    for s in range(2):
                        act.wait_ge(S["proj_done"], 2 * i + s + 1)
                        A(proj[:, bass.ds(2 * i + s, 1), :], bk(s, 1, N), ACT.Copy).then_inc(S["psum_free"], 1)

            evict(0, SEG[0])
            act.wait_ge(S["ab_done"], 2)
            A(ab_raw[0:4, :], bank[2][0:4, 0:N], ACT.Copy).then_inc(S["ab_sb"], 1)
            A(ab_raw[32:36, :], bank[3][32:36, 0:N], ACT.Copy).then_inc(S["ab_sb"], 1)
            act.wait_ge(S["zc_done"], 1)
            A(sgx, proj[:, 13, :], ACT.Sigmoid).then_inc(S["lora_in"], 1)
            A(xw, proj[0:C, 12, :], ACT.Tanh).then_inc(S["lora_in"], 1)
            evict(SEG[0], SEG[1])
            for part, (dst, bias) in enumerate(((tL, "w0"), (ta, "a0"), (tg, None))):
                for t in range(T4):
                    act.wait_ge(S["lora_mm"], T4 * part + t + 1)
                    if bias:
                        ins = A(dst[:, t, :], bk(4 + t, N), ACT.Sigmoid, bias=W(bias)[:, t:t + 1])
                    else:
                        ins = A(dst[:, t, :], bk(4 + t, N)[:, COL_S:], ACT.Copy)
                    ins.then_inc(S["lora_out"], 1)
            act.wait_ge(S["cum"], 2)
            A(teL[:, :, :], tL[:, :, :], ACT.Exp).then_inc(S["exps"], 1)
            A(t1[:, :, :], t1[:, :, :], ACT.Exp).then_inc(S["exps"], 1)
            act.wait_ge(S["exps"], 1)
            A(tL[:, :, :], tL[:, :, :], ACT.Exp, scale=-1.0).then_inc(S["exps"], 1)
            act.wait_ge(S["head_sum"], 1)
            A(small_r[0:8, :], bank[3][0:8, 0:N], ACT.Sqrt, bias=K("eps")[0:8]).then_inc(S["head_root"], 1)
            evict(SEG[1], SEG[3])
            for c in range(NC):
                act.wait_ge(S["v_tr"], c + 1)
                A(SV[C:P, c, :], bank[2 + c % 2][C:P, :], ACT.Copy).then_inc(S["v_sb"], 1)
            evict(SEG[3], IN_T // 2)
            for c in range(NC):
                act.wait_ge(S["bt_tr"], c + 1)
                A(BKt[:, c].rearrange("p a b -> p (a b)"), bank[c % 4][:, :], ACT.Copy).then_inc(S["bt_sb"], 1)
            def silu_conv(n):
                act.wait_ge(S["conv_done"], n + 1)
                cv, dst = conv_acc[n % 2], proj[:, RW_T + n, :]
                A(dst[:, COL_S:COL_P].rearrange("p (b t) -> p b t", t=TSEQ),
                  cv[:, 0:7 * NSEQ].rearrange("p (b t) -> p b t", t=7)[:, :, 0:TSEQ], ACT.Silu)
                A(dst[:, COL_META:COL_S], cv[:, 56:56 + META], ACT.Silu)
                A(dst[:, COL_P:], cv[:, 56 + META:], ACT.Silu).then_inc(S["silu_done"], 1)

            def invert(name):
                n_conv = 0
                for two in rounds(name):
                    for slot, _, _, (src, _, n, _, A_T, _, _, _) in two:
                        for odd in range(2):
                            ins = A(blocks(A_T, odd, n), heads(src, odd), ACT.Copy)
                        ins.then_inc(S[f"inv_at{slot}"], 1)
                    for level in range(max(j[3][3] for j in two)):
                        for slot, n_jobs, n_levels, (_, _, n, levels, _, _, T1, _) in two:
                            if 0 < level < levels:
                                act.wait_ge(S[f"inv_t1{slot}"], n_levels + level + 1)
                                A(T1[:, 0:n].rearrange("p a b -> p (a b)"), bank[3 * slot][:, 0:n * P], ACT.Copy)\
                                    .then_inc(S[f"inv_t1s{slot}"], 1)
                        if name == "r":
                            for tile in range(QKV_T):
                                if (4 * tile + 3) // TAPS == n_conv - 1:
                                    silu_conv(tile)
                        n_conv += 1
                    for slot, n_jobs, n_levels, (_, dst, n, levels, _, _, _, X_T) in two:
                        act.wait_ge(S[f"inv_upd{slot}"], n_levels + n_jobs + levels + 1)
                        for odd in range(2):
                            ins = A(heads(dst, odd), blocks(X_T, odd, n), ACT.Copy)
                        ins.then_inc(S["inv_out"], 1)
                if name == "r":
                    for tile in range(QKV_T):
                        if (4 * tile + 3) // TAPS >= n_conv - 1:
                            silu_conv(tile)

            act.wait_ge(S["gm_done"], 2 * NC)
            act.wait_ge(S["at_zero"], 1)
            nc.scalar.preload_act_table(ACT.Silu)
            invert("r")
            A(proj[:, RW_T + QKV_T:, :], proj[:, RW_T + QKV_T:, :], ACT.Silu).then_inc(S["z_done"], 1)
            act.wait_ge(S["s0_mm"], 1)
            c0 = bk(6, T4, 2, C)
            for x in range(2):
                step(A(C0r[:, :, x, COL_S:], c0[:, :, x, COL_S:], ACT.Copy))
            act.wait_ge(S["sv_zero"], 3)
            act.sem_inc(S["s0_sb"], 1)
            for c in range(NC):
                act.wait_ge(S["ch_rhs"], c + 1)
                A(Rs[0:C, :], bank[0][0:C, :], ACT.Copy).then_inc(S["ch_rhs_sb"], 1)
                act.wait_ge(S["ch_sa"], c + 1)
                A(SV[0:C, c, :], bank[1][0:C, :], ACT.Copy).then_inc(S["ch_sa_sb"], 1)
                act.wait_ge(S["ch_y"], c + 1)
                A(ty[:, :, c * C:c * C + C], bk(3, T4, C), ACT.Copy).then_inc(S["ch_y_sb"], 1)
            for t in range(T4):
                act.wait_ge(S["gn_in"], t + 1)
                ins = A(gn_sqv[:, t, :], ty[:, t, COL_S:], ACT.Square)
            ins.then_inc(S["head_sq"], 1)
            act.wait_ge(S["head_sum"], 2)
            A(small_r[0:8, 0:M], bank[3][0:8, 0:M], ACT.Sqrt, bias=K("gn_eps")[0:8], scale=1.0 / C).then_inc(S["head_root"], 1)

            act.wait_ge(S["rwkv_over"], 1)
            act.wait_ge(S["silu_done"], QKV_T + 2)
            A(sqg[:, 0:8, :], proj[:, RW_T:RW_T + 8, :], ACT.Square).then_inc(S["head_sq"], 1)
            act.wait_ge(S["ab_rows"], 1)
            A(rows[32:36, :], ab_raw[32:36, :], ACT.Sigmoid).then_inc(S["ab_lin"], 1)
            nc.scalar.preload_act_table_set("natural_log_exp_and_others")
            step(A(row_tmp[0:4, :], ab_raw[0:4, :], ACT.Abs, bias=W("dt_bias")[0:4]))
            step(A(row_tmp[0:4, :], row_tmp[0:4, :], ACT.Exp, scale=-1.0))
            step(A(row_tmp[0:4, :], row_tmp[0:4, :], ACT.Ln, bias=K("one")[0:4]))
            A(rate, W("A_log")[0:4], ACT.Exp).then_inc(S["g_rows"], 1)
            act.wait_ge(S["g_cum"], 1)
            A(row_tmp[0:4, :], rows[0:4, :], ACT.Exp).then_inc(S["g_exp"], 1)
            act.wait_ge(S["head_sum"], 3)
            A(srow[0:8, :], bank[0][0:8, 0:N], ACT.Sqrt, bias=K("eps")[0:8]).then_inc(S["head_root"], 1)
            for h in range(HG):
                act.wait_ge(S["g_bc"], 3 * h + 3)
                A(eGb[:, h, :], bk(6, N), ACT.Copy).then_inc(S["g_bc_act"], 1)
            act.wait_ge(S["cols_tr"], 1)
            tr = bank[7][0:C, 0:NC * 96].rearrange("p (c r) -> p c r", c=NC)
            step(A(cols[0:C, :, 0:96], tr, ACT.Copy))
            A(ecols[0:C, :, 0:4], tr[:, :, 0:4], ACT.Exp)
            A(ecols[0:C, :, 4:8], tr[:, :, 64:68], ACT.Exp).then_inc(S["ecol"], 1)
            act.wait_ge(S["d_arg"], 1)
            A(Dincl[0:C], Dincl[0:C], ACT.Exp).then_inc(S["d_exp"], 1)
            act.wait_ge(S["ga_done"], NC)
            invert("g")
            act.wait_ge(S["s0_mm"], 2)
            c0 = bk(6, HG, 2, C)
            step(A(C0g[:, :, 0, COL_S:], c0[:, :, 0, COL_S:], ACT.Copy))
            act.sem_inc(S["s0_k"], 1)
            act.wait_ge(S["sv_zero"], 5)
            act.sem_inc(S["s0_sb"], 1)
            for c in range(NC):
                act.wait_ge(S["ch_sa"], NC + c + 1)
                A(VNs[c > 0][0:C, :], bank[1][0:C, :], ACT.Copy).then_inc(S["ch_sa_sb"], 1)
                act.wait_ge(S["ch_y"], NC + c + 1)
                A(oT[:, :, c * C:c * C + C], bk(3, HG, C), ACT.Copy).then_inc(S["ch_y_sb"], 1)
            act.wait_ge(S["ch_y_sb"], 2 * NC)
            A(sqg_o, oT[:, :, COL_S:], ACT.Square).then_inc(S["head_sq"], 1)
            act.wait_ge(S["head_sum"], 4)
            A(srow[0:8, 0:M], bank[0][0:8, 0:M], ACT.Sqrt, bias=K("eps")[0:8], scale=1.0 / P).then_inc(S["head_root"], 1)

            nc.scalar.preload_act_table(ACT.Sigmoid)
            act.wait_ge(S["yB"], 1)
            with act.Fori(0, KD // 2) as i:
                for s in range(2):
                    act.wait_ge(S["op_mm"], 2 * i + s + 1)
                    act.wait_ge(S["op_free"], 2 * i + s + 1)
                    A(sgA[s], bk(4 * s, M), ACT.Sigmoid)
                    A(sgB[s], bk(4 * s + 1, M), ACT.Sigmoid).then_inc(S["op_sig"], 1)
            with act.Fori(0, KD // 2) as i:
                for s in range(2):
                    act.wait_ge(S["h_done"], 2 * i + s + 1)
                    A(acc[:, bass.ds(2 * i + s, 1), :], hT[:, bass.ds(2 * i + s, 1), :], ACT.Square).then_inc(S["rms_sq"], 1)
            act.wait_ge(S["rms_mm"], 2)
            A(rs[:, 0:M], bk(7, M), ACT.Sqrt, bias=K("eps"), scale=1.0 / D).then_inc(S["rms_root"], 1)
            act.wait_ge(S["rt_lin"], 1)
            A(logitsT[0:36, :], bank[5][0:36, 0:3 * P], ACT.Copy).then_inc(S["rt_sb"], 1)
            for n in range(6):
                act.wait_ge(S["xt_tr"], n + 1)
                A(xtok[:, n // 2, n % 2 * 512:n % 2 * 512 + 512], bank[n % 4][:, :], ACT.Copy).then_inc(S["xtok"], 1)
            nc.scalar.preload_act_table(ACT.Exp)
            act.wait_ge(S["rt_sum"], 1)
            step(A(rt4, rt4, ACT.Exp))
            A(rt1[3], rt1[3], ACT.Exp).then_inc(S["rt_exp"], 1)
            def dense():
                act.wait_ge(S["gt_tr"], 1)
                act.wait_ge(S["xtok"], 6)
                A(gateT[0:E, :], bank[7][0:E, 0:3 * P], ACT.Copy).then_inc(S["gateT"], 1)
                nc.scalar.preload_act_table(ACT.Silu)
                with act.Fori(0, E // 2) as i:
                    for s in range(2):
                        for f in range(4):
                            act.wait_ge(S["gu_mm"], 8 * i + 4 * s + f + 1)
                            act.wait_ge(S["gu_free"], 8 * i + 4 * s + f + 1)
                            A(silu[f % 2], bk(2 * (f % 2), M), ACT.Silu).then_inc(S["silu"], 1)

            def sparse():
                def take(i):
                    act.wait_ge(S["sp_gather"], i + 1)
                    for half in range(2):
                        ins = A(xe[:, 4 * half:4 * half + 4, :].rearrange("p k c -> p (k c)"), bank[2 + half][:, :], ACT.Copy)
                    ins.then_inc(S["xe"], 1)

                def pair(i):
                    act.wait_ge(S["sp_gate"], i + 1)
                    A(silu_s, bank[0][:, :], ACT.Silu).then_inc(S["sp_silu"], 1)
                    take(i + 1)
                    act.wait_ge(S["sp_ht"], i + 1)
                    A(hidT.rearrange("p k c -> p (k c)"), bank[0][:, :], ACT.Copy).then_inc(S["hidT"], 1)
                    act.wait_ge(S["sp_selT"], i + 1)
                    A(selT[:, :], bk(1, 3 * P), ACT.Copy).then_inc(S["selT"], 1)
                    act.wait_ge(S["sp_dn"], i + 1)
                    for half in range(2):
                        ins = A(ye[:, half * 512:half * 512 + 512], bank[4 + half][:, :], ACT.Copy)
                    ins.then_inc(S["sp_ye"], 1)

                take(0)
                nc.scalar.preload_act_table(ACT.Silu)
                with act.Fori(0, E // 2) as i:
                    pair(i)

            act.wait_ge(S["flag"], 1)
            crowded = act.value_load(flag[0:1, 0:1], min_val=0, max_val=1)
            with act.If(crowded < 1):
                sparse()
            with act.Else():
                dense()
            act.wait_ge(S["moe_done"], 1)
            A(xt2[:, :, 0:M], acc, ACT.Square).then_inc(S["rms_sq"], 1)
            act.wait_ge(S["rms_mm"], 3)
            A(rs[:, 0:M], bk(7, M), ACT.Sqrt, bias=K("eps"), scale=1.0 / D).then_inc(S["rms_root"], 1)

        @block.gpsimd
        def _(pool):
            pool.wait_ge(S["ld_par"], 16)
            pool.wait_ge(S["xc_init"], 3)
            pool.wait_ge(S["psum_free"], 2 + IN_T)
            state = W("conv_state").rearrange("p (q b j) -> p q b j", q=QKV_T, b=NSEQ)
            out = conv_out

            def pad(i):
                for s in range(2):
                    n = 2 * i + s
                    pool.wait_ge(S["xc_used"], n + 1)
                    seqs = xc[s][:, 0:7 * NSEQ].rearrange("p (b t) -> p b t", t=7)
                    src = proj[:, bass.ds(n + RW_T, 1), :]
                    src_s = src[:, :, COL_S:COL_P].rearrange("p a (b t) -> p (a b) t", t=TSEQ)
                    cps = [
                        (seqs[:, :, 0:3], state[:, bass.ds(n, 1)].rearrange("p a b j -> p (a b) j")),
                        (seqs[:, :, 3:7], src_s),
                        (xc[s][:, 59:59 + META], src[:, :, COL_META:COL_S].rearrange("p a b -> p (a b)")),
                        (xc[s][:, 59 + META:], src[:, :, COL_P:].rearrange("p a b -> p (a b)")),
                        (out[:, bass.ds(n, 1), 0:24].rearrange("p a (b j) -> p (a b) j", j=3), src_s[:, :, 1:4]),
                        (out[:, bass.ds(n, 1), 24:27], src[:, :, N - 3:]),
                    ]
                    for d_, s_ in cps:
                        ins = nc.gpsimd.tensor_copy(d_, s_)
                        ins.then_inc(S["xc_step"], 1)
                    pool.wait_ge(S["xc_step"], 12 * i + 6 * s + 6)
                    pool.sem_inc(S["xc_ready"], 1)

            pad(0)
            pool.wait_ge(S["v_sb"], NC)
            pool.wait_ge(S["bar_done"], 1)
            nc.gpsimd.memset(SV[0:C], 0.0).then_inc(S["sv_zero"], 1)
            nc.gpsimd.memset(C0r[:, :, :, 0:COL_S], 0.0).then_inc(S["sv_zero"], 1)
            nc.gpsimd.memset(STr, 0.0).then_inc(S["sv_zero"], 1)
            pool.wait_ge(S["sv_zero"], 3)
            pool.wait_ge(S["z_dead"], 1)
            for p_, rows_ in halves:
                nc.gpsimd.memset(SW[rows_, :, :, (1 - p_) * C:(2 - p_) * C], 0.0).then_inc(S["z_dead"], 1)
            pool.wait_ge(S["z_dead"], 3)
            with pool.Fori(1, QKV_T // 2) as i:
                pad(i)

        @block.vector
        def _(dve):
            V = nc.vector
            step = own(dve, "dve_own")
            TT, TS, STT, CP = V.tensor_tensor, V.tensor_scalar, V.scalar_tensor_tensor, V.tensor_copy

            V.memset(eps_at_start, 1e-6)
            V.memset(ones_at_start, 1.0).then_inc(S["xc_init"], 1)
            step(V.memset(xc[0][:, 56:59], 0.0))
            step(V.memset(xc[1][:, 56:59], 0.0))
            dve.sem_inc(S["xc_init"], 2)
            dve.sem_inc(S["xc_used"], 2)
            dve.sem_inc(S["gu_free"], 2)
            dve.sem_inc(S["acc"], 2)
            dve.wait_ge(S["ld_par"], 16)
            dve.wait_ge(S["rms_root"], 1)
            dve.wait_ge(S["ld_x"], 16)
            step(V.reciprocal(rs[:, :], rs[:, :]))
            for k in range(KD):
                last = STT(xnT[:, k, :], xT[:, k, :], W("norm1")[:, k:k + 1], rs[:, :], ALU.mult, ALU.mult)
            step(last)
            CP(xnT[:, :, 0:NSEQ], xT[:, :, 0:NSEQ]).then_inc(S["xn"], 1)
            dve.wait_ge(S["xn"], 1)
            CP(x_out[:, :, 0:NSEQ], xnT[:, :, COL_S + TSEQ - 1:COL_P:TSEQ])
            step(CP(x_out[:, :, NSEQ:], xnT[:, :, N - 1:]))
            dve.sem_inc(S["x_packed"], 1)
            step(V.memset(row_tmp[:, 0:1], 0.0))
            with dve.Fori(0, RW_T) as i:
                dve.wait_ge(S["psum_free"], i + 3)
                z = proj[:, bass.ds(i, 1), :].rearrange("p a b -> p (a b)")
                TT(row_tmp[:, 1:N], z[:, 0:N - 1], z[:, 1:N], ALU.subtract).then_inc(S["shift_step"], 1)
                dve.wait_ge(S["shift_step"], 4 * i + 1)
                TT(row_tmp[:, COL_S:COL_P:TSEQ], z[:, 0:NSEQ], z[:, COL_S:COL_P:TSEQ], ALU.subtract).then_inc(S["shift_step"], 1)
                TT(row_tmp[:, COL_P:COL_P + 1], z[:, COL_S - 1:COL_S], z[:, COL_P:COL_P + 1], ALU.subtract)\
                    .then_inc(S["shift_step"], 1)
                dve.wait_ge(S["shift_step"], 4 * i + 3)
                STT(z, row_tmp[:, :], W("mu")[:, bass.ds(i, 1)], z, ALU.mult, ALU.add).then_inc(S["shift_step"], 1)
                dve.wait_ge(S["shift_step"], 4 * i + 4)
            dve.sem_inc(S["zc_done"], 1)
            dve.wait_ge(S["ld_cst"], 16)
            zr, zk, zv = proj[:, 0:4, :], proj[:, 4:8, :], proj[:, 8:12, :]
            step(TT(tkk[:, :, :], zk, spread(W("k_k"), N), ALU.mult))
            TT(t2[:, :, :], tkk[:, :, :], tkk[:, :, :], ALU.mult).then_inc(S["head_sq"], 1)
            dve.wait_ge(S["lora_out"], T4)
            step(TS(t1[:, :, :], tL[:, :, :], -float(np.exp(-0.5)), None, ALU.mult))
            for t in range(T4):
                last = V.tensor_tensor_scan(tL[:, t, :], K("carry"), t1[:, t, :], 0.0, ALU.mult, ALU.add)
            last.then_inc(S["cum"], 1)
            dve.wait_ge(S["cum"], 1)
            TT(t1[:, :, :], tL[:, :, :], t1[:, :, :], ALU.subtract).then_inc(S["cum"], 1)
            dve.wait_ge(S["head_root"], 1)
            V.reciprocal(small_r[0:8, :], small_r[0:8, :]).then_inc(S["head_inv"], 1)
            for t in range(T4):
                dve.wait_ge(S["head_spread"], t + 1)
                last = TT(tkk[:, t, :], tkk[:, t, :], bk(4 + t, N), ALU.mult)
            step(last)
            dve.wait_ge(S["exps"], 3)
            AR3 = AR.rearrange("p t c x s -> p (t c) x s")
            BK3 = BK.rearrange("p t c x s -> p (t c) x s")

            def ch(v):
                return v.rearrange("p t (c s) -> p (t c) s", s=C)

            step(STT(AR3[:, :, 0, :], ch(tkk), -1.0, ch(t1), ALU.mult, ALU.mult))
            step(TT(AR3[:, :, 1, :], ch(zr), ch(teL), ALU.mult))
            step(TT(t1[:, :, :], tkk[:, :, :], ta[:, :, :], ALU.mult))
            step(TT(BK3[:, :, 0, :], ch(t1), ch(tL), ALU.mult))
            step(STT(ta[:, :, :], ta[:, :, :], 1.0, spread(W("k_a"), N), ALU.subtract, ALU.mult))
            step(STT(ta[:, :, :], ta[:, :, :], 1.0, zk, ALU.add, ALU.mult))
            TT(BK3[:, :, 1, :], ch(ta), ch(tL), ALU.mult).then_inc(S["bk_done"], 1)
            CP(PTs[:, :, 1:NC], teL[:, :, 2 * C - 1:N:C])
            CP(PTs[:, :, 0:1], teL[:, :, COL_S - 1:COL_S])
            step(CP(PTs[:, :, NC:], teL[:, :, COL_S + TSEQ - 1:COL_P:TSEQ]))
            step(TT(t2[:, :, :], zr, ta[:, :, :], ALU.mult))
            TT(t2[:, :, :], t2[:, :, :], spread(W("r_k"), N), ALU.mult).then_inc(S["bonus_in"], 1)
            for t in range(T4):
                dve.wait_ge(S["bonus_mm"], t + 1)
                last = TT(tbonus[:, t, :], zv[:, t, :], bk(4 + t, N), ALU.mult)
            step(last)
            dve.sem_inc(S["z_dead"], 1)
            for c in range(NC):
                for p_, _ in halves:
                    n = 2 * c + p_
                    dve.wait_ge(S["gram_r"], n + 1)
                    TT(GM[:, c, p_::2, :], bk(4 + n % 4, T4, P), over(K("gmask0" if c == 0 else "gmask1"), T4), ALU.mult)\
                        .then_inc(S["gm_done"], 1)
            for x in range(2):
                TT(BK[:, :, 1:, x, :], BK[:, :, 1:, x, :], spread(PTs[:, :, 1:NC], C), ALU.mult)
                v = BK[:, :, 0, x, COL_S:].rearrange("p t (b s) -> p t b s", s=TSEQ)
                TT(v, v, spread(PTs[:, :, NC:], TSEQ), ALU.mult)
                v = BK[:, :, 0, x, COL_META:COL_S]
                last = TT(v, v, PTs[:, :, 0:1].to_broadcast([P, T4, META]), ALU.mult)
            step(last)
            dve.sem_inc(S["bar_done"], 1)
            cw = W("conv").rearrange("p (q j) -> p q j", q=QKV_T)

            def convolve(n, j):
                w_, x, acc_ = cw[:, n, j:j + 1], xc[n % 2][:, j:j + CONVN], conv_acc[n % 2]
                if j == 0:
                    dve.wait_ge(S["xc_ready"], n + 1)
                    dve.wait_ge(S["silu_done"], n + 1)
                    TS(acc_, x, w_, None, ALU.mult).then_inc(S["conv_step"], 1)
                elif j < 3:
                    dve.wait_ge(S["conv_step"], 3 * n + j)
                    STT(acc_, x, w_, acc_, ALU.mult, ALU.add).then_inc(S["conv_step"], 1)
                else:
                    dve.wait_ge(S["conv_step"], 3 * n + 3)
                    STT(acc_, x, w_, acc_, ALU.mult, ALU.add).then_inc(S["conv_done"], 1)
                    dve.wait_ge(S["conv_done"], n + 1)
                    dve.sem_inc(S["xc_used"], 1)

            low = K("low").rearrange("p (l c) -> p l c", l=LEVELS).bitcast(I32)
            up = K("up").rearrange("p (l c) -> p l c", l=LEVELS).bitcast(I32)

            def invert(name):
                n_conv, n_out = 0, 0 if name == "r" else len(jobs_r)
                for two in rounds(name):
                    if n_out:
                        dve.wait_ge(S["inv_out"], n_out)
                    n_out += len(two)
                    for slot, n_jobs, n_levels, (_, _, n, _, A_T, X, _, X_T) in two:
                        dve.wait_ge(S[f"inv_at{slot}"], n_jobs + 1)
                        CP(X[:, 0:n, :], over(K("ident"), n))
                        step(CP(X_T[:, 0:n, :], over(K("ident"), n)))
                        V.copy_predicated(halved(X_T, n), over(up[:, 0, :], 2 * n), halved(A_T, n)).then_inc(S[f"inv_upd{slot}"], 1)
                    for level in range(max(j[3][3] for j in two)):
                        for slot, n_jobs, n_levels, (_, _, n, levels, _, X, _, X_T) in two:
                            if level >= levels:
                                continue
                            m_low, m_up = over(low[:, level, :], 2 * n), over(up[:, level, :], 2 * n)
                            if level == 0:
                                dve.wait_ge(S[f"inv_t1{slot}"], n_levels + 1)
                                V.copy_predicated(halved(X, n), m_low, bk(3 * slot, HR, C)[:, 0:2 * n, :])\
                                    .then_inc(S[f"inv_upd{slot}"], 1)
                                continue
                            dve.wait_ge(S[f"inv_t2{slot}"], n_levels - n_jobs + level)
                            if level < levels - 1:
                                V.copy_predicated(halved(X, n), m_low, bk(3 * slot + 1, HR, C)[:, 0:2 * n, :])
                            V.copy_predicated(halved(X_T, n), m_up, bk(3 * slot + 2, HR, C)[:, 0:2 * n, :])\
                                .then_inc(S[f"inv_upd{slot}"], 1)
                        if name == "r":
                            for tap in range(TAPS * n_conv, min(TAPS * n_conv + TAPS, 4 * QKV_T)):
                                convolve(tap // 4, tap % 4)
                        n_conv += 1

            dve.wait_ge(S["psum_free"], IN_T + 2)
            for a in invA:
                step(V.memset(a, 0.0))
            dve.sem_inc(S["at_zero"], 1)
            dve.wait_ge(S["gm_done"], 2 * NC)
            invert("r")
            def mask_r(n):
                b = NSEQ if n == 0 else n - 1
                if n >= 2:
                    dve.wait_ge(S["sm_mm"], n - 1)
                TS(SVm[n % 2], SV[:, 0, :], K("seq")[:, b:b + 1], None, ALU.mult).then_inc(S["svm"], 1)

            def decay_r(n):
                b = n - 1
                for p_, rows_ in halves:
                    v = SW[rows_, b, :, p_ * C:p_ * C + C]
                    last = TT(v, v, spread(PTs[rows_, :, NC + b], C), ALU.mult)
                return last

            def sample_r(n):
                dve.wait_ge(S["sm_mm"], n + 1)
                for p_, rows_ in halves:
                    v = SW[rows_, n - 1, :, p_ * C:p_ * C + C]
                    last = TT(v, v, bk(4 + n % 2, T4, P)[rows_, :, p_ * C:p_ * C + C], ALU.add)
                last.then_inc(S["sm_sb"], 1)

            dve.wait_ge(S["ch_sa_sb"], 1)
            mask_r(0)
            mask_r(1)
            dve.wait_ge(S["sm_mm"], 1)
            for p_, rows_ in halves:
                last = CP(STr[rows_, 0, :, p_ * C:p_ * C + C], bk(4, T4, P)[rows_, :, p_ * C:p_ * C + C])
            last.then_inc(S["ch_st_sb"], 1)
            mask_r(2)
            dve.wait_ge(S["ld_sw"], 32)
            dve.wait_ge(S["s0_mm"], 1)
            for c in range(1, NC):
                dve.wait_ge(S["ch_st_sb"], c)
                dve.wait_ge(S["ch_y"], c)
                for p_, rows_ in halves:
                    half = slice(p_ * C, p_ * C + C)
                    TT(STr[rows_, c % 2, :, half], STr[rows_, (c - 1) % 2, :, half], spread(PTs[rows_, :, c], C), ALU.mult)
                decay_r(2 * c - 1)
                step(decay_r(2 * c))
                sample_r(2 * c - 1)
                if c < NC - 1:
                    mask_r(2 * c + 1)
                dve.wait_ge(S["ch_st"], c)
                for p_, rows_ in halves:
                    v = STr[rows_, c % 2, :, p_ * C:p_ * C + C]
                    last = TT(v, v, bk(2, T4, P)[rows_, :, p_ * C:p_ * C + C], ALU.add)
                last.then_inc(S["ch_st_sb"], 1)
                sample_r(2 * c)
                if c < NC - 1:
                    mask_r(2 * c + 2)
            for t in range(T4):
                dve.wait_ge(S["gn_d"], t + 1)
                CP(ty[:, t, COL_S:], bk(4 + t, M)).then_inc(S["gn_in"], 1)
            dve.wait_ge(S["gn_in"], T4)
            dve.wait_ge(S["head_root"], 2)
            V.reciprocal(small_r[0:8, 0:M], small_r[0:8, 0:M]).then_inc(S["head_inv"], 1)
            dve.wait_ge(S["rwkv_over"], 1)
            step(V.memset(rows, 0.0))
            dve.sem_inc(S["ab_rows"], 1)
            step(TS(srow[0:4, :], ab_raw[0:4, :], W("dt_bias")[0:4], 0.0, ALU.add, ALU.max))
            for t in range(T4):
                dve.wait_ge(S["head_spread"], T4 + t + 1)
                y = ty[:, t, COL_S:]
                step(TT(y, y, bk(4 + t, M), ALU.mult))
                step(TS(y, y, W("ln_w")[:, t:t + 1], W("ln_b")[:, t:t + 1], ALU.mult, ALU.add))
            y = ty[:, :, COL_S:]
            step(TT(y, y, tbonus[:, :, COL_S:], ALU.add))
            TT(yA[:, :, :], y, tg[:, :, :], ALU.mult).then_inc(S["yA"], 1)

            dve.wait_ge(S["g_rows"], 1)
            step(TT(srow[0:4, :], srow[0:4, :], row_tmp[0:4, :], ALU.add))
            step(TS(srow[0:4, :], srow[0:4, :], rate, -1.0, ALU.mult, ALU.mult))
            V.tensor_tensor_scan(rows[0:4, :], K("carry")[0:4], srow[0:4, :], 0.0, ALU.mult, ALU.add).then_inc(S["g_cum"], 1)
            dve.wait_ge(S["g_cum"], 1)
            g = rows[0:4, :]
            TT(rows[64:68, COL_P:].rearrange("p (c s) -> p c s", s=C),
               g[:, 2 * C - 1:N:C].unsqueeze(2).to_broadcast([4, NC - 1, C]),
               g[:, COL_P:].rearrange("p (c s) -> p c s", s=C), ALU.subtract)
            TT(rows[64:68, COL_META:COL_S], g[:, COL_S - 1:COL_S].to_broadcast([4, META]), g[:, COL_META:COL_S], ALU.subtract)
            step(TT(rows[64:68, COL_S:COL_P].rearrange("p (b s) -> p b s", s=TSEQ),
                    g[:, COL_S + TSEQ - 1:COL_P:TSEQ].unsqueeze(2).to_broadcast([4, NSEQ, TSEQ]),
                    g[:, COL_S:COL_P].rearrange("p (b s) -> p b s", s=TSEQ), ALU.subtract))
            dve.wait_ge(S["ab_lin"], 1)
            dve.wait_ge(S["g_exp"], 1)
            dve.sem_inc(S["g_kd"], 1)
            dve.wait_ge(S["head_root"], 3)
            V.reciprocal(srow[0:8, :], srow[0:8, :]).then_inc(S["head_inv"], 1)
            for h in range(HG):
                dve.wait_ge(S["g_bc"], 3 * h + 2)
                CP(Dincl[0:C, h, :], bank[4][0:C, 0:N]).then_inc(S["g_bc_dve"], 1)
                TT(Dstr[0:C, h, :], K("strict")[0:C], bank[5][0:C, 0:N], ALU.mult).then_inc(S["g_bc_dve"], 1)
            dve.wait_ge(S["ecol"], 1)
            dve.wait_ge(S["g_bc_dve"], 2 * HG)
            for h in range(HG):
                v = Dincl[0:C, h, :].rearrange("p (c s) -> p c s", s=C)
                last = TT(v, v, spread(cols[0:C, :, h], C), ALU.subtract)
            step(last)
            TS(Dincl[0:C], Dincl[0:C], 0.0, None, ALU.min).then_inc(S["d_arg"], 1)
            STT(cols[0:C, :, 96:100], cols[0:C, :, 32:36], -1.0, ecols[0:C, :, 0:4], ALU.mult, ALU.mult).then_inc(S["ecol2"], 1)
            dve.wait_ge(S["silu_done"], QKV_T + 2)
            for t in range(8):
                dve.wait_ge(S["head_spread"], 2 * T4 + t + 1)
                src = proj[:, RW_T + t, :].rearrange("p (c s) -> p c s", s=C)
                ps = bk(1 + t % 3, NC, C)
                if t < 4:
                    ins = STT(KQ[:, t, :, 1, :], src, float(P ** -0.5), ps, ALU.mult, ALU.mult)
                else:
                    ins = TT(KQ[:, t - 4, :, 0, :], src, ps, ALU.mult)
                ins.then_inc(S["kq_done"], 1)
            dve.wait_ge(S["kq_done"], 8)
            dve.wait_ge(S["g_bc_act"], HG)
            for h in range(HG):
                last = TT(qdec[:, h, :].rearrange("p (c s) -> p c s", s=C), KQ[:, h, :, 1, :],
                          eGb[:, h, :].rearrange("p (c s) -> p c s", s=C), ALU.mult)
            step(last)
            for c in range(NC):
                for w_ in range(2):
                    n = 2 * c + w_
                    dve.wait_ge(S["kv_tr"], n + 1)
                    col = ecols[0:C, c, 4:8] if w_ == 0 else cols[0:C, c, 32:36]
                    TT((kdec, bV)[w_][0:C, c], bk((0, 1, 4, 5)[n % 4], HG, P)[0:C], spread(col, P), ALU.mult).then_inc(S["kv_sb"], 1)
            dve.wait_ge(S["d_exp"], 1)
            step(TT(Dstr[0:C], Dstr[0:C], Dincl[0:C], ALU.mult))
            TT(Dincl[0:C], Dincl[0:C], over(K("incl")[0:C], HG), ALU.mult).then_inc(S["d_done"], 1)
            for c in range(NC):
                dve.wait_ge(S["gram_g"], c + 1)
                ps = bk(2 + c % 2, HG, 2, C)[0:C]
                TT(GA[0:C, c], ps[:, :, 0, :], Dstr[0:C, :, c * C:c * C + C], ALU.mult)
                TT(QKD[0:C, c], ps[:, :, 1, :], Dincl[0:C, :, c * C:c * C + C], ALU.mult).then_inc(S["ga_done"], 1)
            V.memset(C0g[:, :, :, 0:COL_S], 0.0).then_inc(S["sv_zero"], 1)
            dve.wait_ge(S["ga_done"], NC)
            dve.wait_ge(S["yA"], 1)
            invert("g")
            dve.wait_ge(S["s0_k"], 1)
            TT(C0g[:, :, 1, COL_S:], bk(6, HG, 2, C)[:, :, 1, COL_S:], eGb[:, :, COL_S:COL_P], ALU.mult).then_inc(S["sv_zero"], 1)

            def mask_g(n):
                b = NSEQ if n == 0 else n - 1
                if n >= 2:
                    dve.wait_ge(S["sm_mm"], NSEQ + 1 + n - 1)
                TS(VNm[n % 2][0:C], VNs[0][0:C, :], K("seq")[0:C, b:b + 1], None, ALU.mult).then_inc(S["svm"], 1)

            def decay_g(n):
                lo = COL_S + TSEQ * n - 1
                return TT(SW[:, n - 1], SW[:, n - 1], eGb[:, :, lo:lo + 1].to_broadcast([P, HG, P]), ALU.mult)

            def sample_g(n):
                dve.wait_ge(S["sm_mm"], NSEQ + 1 + n + 1)
                TT(SW[:, n - 1], SW[:, n - 1], bk(4 + n % 2, HG, P), ALU.add).then_inc(S["sm_sb"], 1)

            for c in range(NC):
                dve.wait_ge(S["ch_rhs"], NC + c + 1)
                step(TT(Rg[0:C], bk(0, HG, P)[0:C], spread(cols[0:C, c, 96:100], P), ALU.mult))
                TT(Rg[0:C], Rg[0:C], bV[0:C, c], ALU.add).then_inc(S["ch_rhs_sb"], 1)
                if c == 0:
                    dve.wait_ge(S["ch_sa_sb"], NC + 1)
                    mask_g(0)
                    mask_g(1)
                    dve.wait_ge(S["sm_mm"], NSEQ + 2)
                    CP(Sg[:, 0], bk(4, HG, P)).then_inc(S["ch_st_sb"], 1)
                    mask_g(2)
                    dve.wait_ge(S["ld_sw"], 48)
                    dve.wait_ge(S["s0_mm"], 2)
                    continue
                dve.wait_ge(S["ch_st_sb"], NC + c)
                dve.wait_ge(S["ch_y"], NC + c)
                lo = c * C + C - 1
                TT(Sg[:, c % 2], Sg[:, (c - 1) % 2], eGb[:, :, lo:lo + 1].to_broadcast([P, HG, P]), ALU.mult)
                decay_g(2 * c - 1)
                step(decay_g(2 * c))
                sample_g(2 * c - 1)
                if c < NC - 1:
                    mask_g(2 * c + 1)
                dve.wait_ge(S["ch_st"], NC - 1 + c)
                TT(Sg[:, c % 2], Sg[:, c % 2], bk(2, HG, P), ALU.add).then_inc(S["ch_st_sb"], 1)
                sample_g(2 * c)
                if c < NC - 1:
                    mask_g(2 * c + 2)
            dve.wait_ge(S["head_root"], 4)
            V.reciprocal(srow[0:8, 0:M], srow[0:8, 0:M]).then_inc(S["head_inv"], 1)
            dve.wait_ge(S["z_done"], 1)
            for h in range(HG):
                dve.wait_ge(S["head_spread"], 2 * T4 + 8 + h + 1)
                o = oT[:, h, COL_S:]
                step(STT(o, o, W("gdn_norm"), bk(4 + h, M), ALU.mult, ALU.mult))
            TT(yB[:, :, :], oT[:, :, COL_S:], proj[:, RW_T + QKV_T:, COL_S:], ALU.mult).then_inc(S["yB"], 1)

            with dve.Fori(0, KD // 2) as i:
                for s in range(2):
                    n = 2 * i + s
                    dve.wait_ge(S["op_sig"], n + 1)
                    TT(sgA[s], sgA[s], bk(4 * s + 2, M), ALU.mult).then_inc(S["moe_own"], 1)
                    TT(sgB[s], sgB[s], bk(4 * s + 3, M), ALU.mult).then_inc(S["moe_own"], 1)
                    dve.wait_ge(S["moe_own"], 4 * i + 2 * s + 2)
                    TT(merged[:, bass.ds(n, 1), :], sgA[s].unsqueeze(1), sgB[s].unsqueeze(1), ALU.add).then_inc(S["op_merge"], 1)
                    dve.wait_ge(S["op_merge"], n + 1)
                    dve.sem_inc(S["op_free"], 1)
            with dve.Fori(0, KD // 2) as i:
                for s in range(2):
                    n = 2 * i + s
                    dve.wait_ge(S["fin_mm"], n + 1)
                    TT(hT[:, bass.ds(n, 1), :], xT[:, bass.ds(n, 1), COL_S:], bk(s, 1, M), ALU.add).then_inc(S["h_done"], 1)
                    dve.wait_ge(S["h_done"], n + 1)
                    dve.sem_inc(S["op_free"], 1)
            V.memset(xt2[:, :, M:], 0.0)
            dve.wait_ge(S["rms_root"], 2)
            step(V.reciprocal(rs[:, 0:M], rs[:, 0:M]))
            for k in range(KD):
                last = STT(xt2[:, k, 0:M], hT[:, k, :], W("norm2")[:, k:k + 1], rs[:, 0:M], ALU.mult, ALU.mult)
            last.then_inc(S["xt2"], 1)
            dve.wait_ge(S["rt_mm"], 1)
            step(TT(rt, bk(6, 3, 36), over(W("router_b"), 3), ALU.add))
            gl = rt[:, :, 0:G]
            el = rt[:, :, G:].rearrange("p m (g e) -> p m g e", g=G)
            gm, den, m1, m2, w1, w2, tmp = rt1

            def first_of(dst, src, top, order, n):
                step(TT(dst, src, spread(top, n), ALU.is_equal))
                step(TT(dst, dst, over(order, 3), ALU.mult))
                step(V.tensor_reduce(tmp, dst, AX.X, ALU.max))
                step(TT(dst, dst, spread(tmp, n), ALU.is_equal))

            ohg, oh1, oh2, ev = rt8[0][:, :, 0:G], rt8[1], rt8[2], rt8[3]
            step(V.tensor_reduce(gm, gl, AX.X, ALU.max))
            step(TT(rt4, gl, spread(gm, G), ALU.subtract))
            first_of(ohg, gl, gm, K("first4"), G)
            for m in range(3):
                last = TT(rte[:, m], el[:, m], spread(ohg[:, m], EG), ALU.mult)
            step(last)
            step(V.tensor_reduce(ev, rte.rearrange("p m g e -> p m e g"), AX.X, ALU.add))
            step(V.tensor_reduce(m1, ev, AX.X, ALU.max))
            first_of(oh1, ev, m1, K("first8"), EG)
            step(STT(ev, oh1, -1e30, ev, ALU.mult, ALU.add))
            step(V.tensor_reduce(m2, ev, AX.X, ALU.max))
            first_of(oh2, ev, m2, K("first8"), EG)
            step(TT(m2, m2, m1, ALU.subtract))
            dve.sem_inc(S["rt_sum"], 1)
            step(TT(ev, oh1, oh2, ALU.add))
            step(TT(ev, ev, spread(K("valid"), EG), ALU.mult))
            for m in range(3):
                last = TT(member[:, m].rearrange("p (g e) -> p g e", g=G), spread(ohg[:, m], EG), over(ev[:, m], G), ALU.mult)
            last.then_inc(S["rt_member"], 1)
            V.memset(slot, -1.0)
            V.memset(gate, 0.0)
            dve.wait_ge(S["rt_exp"], 1)
            step(V.tensor_reduce(den, rt4, AX.X, ALU.add))
            step(STT(w1, m2, 1.0, den, ALU.add, ALU.mult))
            step(V.reciprocal(w1, w1))
            step(TT(w2, w1, m2, ALU.mult))
            step(TT(oh1, oh1, spread(w1, EG), ALU.mult))
            step(TT(oh2, oh2, spread(w2, EG), ALU.mult))
            step(TT(oh1, oh1, oh2, ALU.add))
            for m in range(3):
                last = TT(gate[:, m, 0:E].rearrange("p (g e) -> p g e", g=G), spread(ohg[:, m], EG), over(oh1[:, m], G), ALU.mult)
            last.then_inc(S["gate"], 1)
            dve.wait_ge(S["rt_pos"], 1)
            step(STT(slot[:, :, 0:E], bk(6, 3, E), 1.0, member, ALU.add, ALU.mult))
            step(TS(slot[:, :, 0:E], slot[:, :, 0:E], -1.0, None, ALU.add))
            step(V.tensor_reduce(flag_f, bank[6][:, 3 * E:4 * E], AX.X, ALU.max))
            TS(flag, flag_f, CAP + 0.5, None, ALU.is_gt).then_inc(S["flag"], 1)
            CP(acc, hT).then_inc(S["acc_init"], 1)
            dve.wait_ge(S["acc_init"], 1)

            def dense():
                dve.wait_ge(S["gateT"], 1)
                for s in range(2):
                    TS(gsel[s][0:E], gateT[0:E, 0:M], K("ident")[0:E, s:s + 1], None, ALU.mult).then_inc(S["gsel"], 1)
                with dve.Fori(0, E // 2) as i:
                    for s in range(2):
                        e = 2 * i + s
                        dve.wait_ge(S["gb_mm"], e + 1)
                        for f in range(4):
                            dve.wait_ge(S["silu"], 4 * e + f + 1)
                            TT(hid[s][:, f, :], silu[f % 2], bk(2 * (f % 2) + 1, M), ALU.mult).then_inc(S["hid_step"], 1)
                            dve.wait_ge(S["hid_step"], 8 * i + 4 * s + f + 1)
                            TT(hid[s][:, f, :], hid[s][:, f, :], bk(6, M), ALU.mult).then_inc(S["hid"], 1)
                            dve.wait_ge(S["hid"], 4 * e + f + 1)
                            dve.sem_inc(S["gu_free"], 1)
                        TS(gsel[s][0:E], gateT[0:E, 0:M], K("ident")[0:E, bass.ds(e + 2, 1)], None, ALU.mult).then_inc(S["gsel"], 1)
                        for j in range(KD):
                            dve.wait_ge(S["dn_mm"], KD * e + j + 1)
                            TT(acc[:, j, :], acc[:, j, :], bk(4 + j % 2, M), ALU.add).then_inc(S["acc"], 1)

                dve.wait_ge(S["acc"], 2 + KD * E)
                dve.sem_inc(S["moe_done"], 1)

            def sparse():
                dve.sem_inc(S["sp_acc"], 2)

                def select(i):
                    for s in range(2):
                        ins = TT(sel[:, :, s, :], over(K("iota"), 3),
                                 slot[:, :, bass.ds(2 * i + s, 1)].to_broadcast([P, 3, CAP]), ALU.is_equal)
                    ins.then_inc(S["sp_sel"], 1)

                def weigh(i):
                    for s in range(2):
                        ins = TT(selG[:, :, s, :], sel[:, :, s, :],
                                 gate[:, :, bass.ds(2 * i + s, 1)].to_broadcast([P, 3, CAP]), ALU.mult)
                    ins.then_inc(S["sp_selg"], 1)

                def add(i):
                    for j in range(KD):
                        dve.wait_ge(S["sp_comb"], KD * (i - 1) + j + 1)
                        TT(acc[:, j, :], acc[:, j, :], bk(6 + j % 2, M), ALU.add).then_inc(S["sp_acc"], 1)

                def pair(i, first):
                    dve.wait_ge(S["sp_silu"], i + 1)
                    dve.wait_ge(S["sp_up"], i + 1)
                    TT(hid_s, silu_s, bank[1][:, :], ALU.mult).then_inc(S["sp_hid"], 1)
                    if not first:
                        dve.wait_ge(S["sp_acc"], KD * (i - 1) + 2)
                        add(i)
                    dve.wait_ge(S["sp_selT"], i + 1)
                    weigh(i + 1)
                    dve.wait_ge(S["sp_gather"], i + 2)
                    dve.wait_ge(S["sp_selg"], i + 2)
                    select(i + 2)

                select(0)
                dve.wait_ge(S["sp_sel"], 1)
                weigh(0)
                dve.wait_ge(S["sp_gather"], 1)
                dve.wait_ge(S["sp_selg"], 1)
                select(1)
                dve.wait_ge(S["sp_sel"], 2)
                pair(0, True)
                with dve.Fori(1, E // 2) as i:
                    dve.wait_ge(S["sp_sel"], i + 2)
                    pair(i, False)
                dve.wait_ge(S["sp_acc"], KD * (E // 2 - 1) + 2)
                add(E // 2)
                dve.wait_ge(S["sp_acc"], KD * (E // 2) + 2)
                dve.sem_inc(S["moe_done"], 1)

            dve.wait_ge(S["flag"], 1)
            dve.wait_ge(S["gate"], 1)
            crowded = dve.value_load(flag[0:1, 0:1], min_val=0, max_val=1)
            with dve.If(crowded < 1):
                sparse()
            with dve.Else():
                dense()
            dve.wait_ge(S["rms_root"], 3)
            step(V.reciprocal(rs[:, 0:M], rs[:, 0:M]))
            for k in range(KD):
                last = STT(acc[:, k, :], acc[:, k, :], W("normf")[:, k:k + 1], rs[:, 0:M], ALU.mult, ALU.mult)
            last.then_inc(S["y_ready"], 1)


SHAPES = dict(
    xT=(P, KD, N), cst=(P, CST.width), par=(P, PAR.width), w_in=(IN_T, P, KD, P), wkv_in=(P, NSEQ, T4, C),
    gdn_in=(P, NSEQ, HG, P), w_gab=(KD, P, 2, KD, P), w_oab=(KD, P, 2, T4, P), w_o=(KD, P, KD, P),
    w_gu=(E, P, 2, KD, FF), w_dn=(E, P, 4, D))
OUT_SHAPES = dict(
    y=(P, KD, M), shift_out=(P, KD, NSEQ + 1), wkv_p=(P, T4, C), wkv_s=(P, NSEQ, T4, C), conv_out=(P, QKV_T, 27),
    gdn_p=(P, HG, P), gdn_s=(P, NSEQ, HG, P))


def kernel(**inputs):
    import concourse.bacc as bacc
    from concourse.bass_utils import run_bass_kernel_spmd as run

    x = {k: np.asarray(v) for k, v in inputs.items()}

    def feat(a):
        a = a.reshape(a.shape[0] // P, P, -1)
        return a.transpose(1, 0, 2).reshape(P, -1)

    tokens = np.concatenate([x["state_shift"][0], np.zeros((NSEQ, D), np.float32), x["meta_tokens"],
                             x["x_sample"].reshape(-1, D), x["x_prompt"][0]])
    par = np.zeros((P, PAR.width), np.float32)

    def put(name, a, row=0):
        a = a.reshape(a.shape[0], -1)
        lo = PAR.at[name][0]
        par[row:row + a.shape[0], lo:lo + a.shape[1]] = a

    w_in = x["w_in"][0]
    cut = IN_T * P
    put("norm1", feat(x["norm1_w"][0]))
    put("norm2", feat(x["norm2_w"][0]))
    put("normf", feat(x["norm_f_w"]))
    put("mu", feat(x["mu_shift"][0]))
    for name, key in (("w0", "rw_w0"), ("a0", "rw_a0"), ("k_k", "rw_k_k"), ("k_a", "rw_k_a"), ("r_k", "rw_r_k"),
                      ("ln_w", "rw_lnx_w"), ("ln_b", "rw_lnx_b")):
        put(name, feat(x[key][0].reshape(-1)))
    put("conv", feat(x["gdn_conv_w"][0].T))
    put("gdn_norm", x["gdn_norm_w"][0][:, None])
    put("A_log", x["gdn_A_log"][0][:, None])
    put("dt_bias", x["gdn_dt_bias"][0][:, None])
    put("w2a2", x["rw_w2"][0])
    put("w2a2", x["rw_a2"][0], C)
    put("g2", x["rw_g2"][0])
    put("ab", feat(w_in[:, cut:cut + 8]))
    put("router", feat(np.concatenate([x["router_g"][0], x["router_e"][0]], 1)))
    put("router_b", np.broadcast_to(np.concatenate([x["router_g_b"][0], x["router_e_b"][0]]), (P, 36)))
    put("conv_state", feat(x["state_conv"][0].transpose(2, 0, 1).reshape(QKV_T * P, NSEQ * 3)))

    def tiles(w):
        return w.reshape(w.shape[0] // P, P, w.shape[1] // P, P).transpose(2, 1, 0, 3)

    gates = cut + 8
    wg, wu = (x[f"moe_w_{n}"][0].reshape(E, KD, P, FF).transpose(0, 2, 1, 3) for n in ("gate", "up"))
    arrays = dict(
        xT=feat(tokens.T).reshape(P, KD, N), cst=constants(), par=par, w_in=tiles(w_in[:, :cut]),
        wkv_in=x["state_wkv"][0].reshape(NSEQ, T4, 2, C, C).transpose(2, 4, 0, 1, 3).reshape(P, NSEQ, T4, C),
        gdn_in=x["state_gdn"][0].transpose(2, 0, 1, 3),
        w_gab=np.stack([tiles(w_in[:, gates:gates + D]), tiles(w_in[:, gates + D:])], 2),
        w_oab=np.stack([tiles(x["w_oA"][0]), tiles(x["w_oB"][0])], 2), w_o=tiles(x["w_o"][0]),
        w_gu=np.stack([wg, wu], 2), w_dn=x["moe_w_down"][0].reshape(E, 4, P, D).transpose(0, 2, 1, 3))
    nc = bacc.Bacc("TRN2", target_bir_lowering=False, num_devices=1)
    dram = {}
    for name, shape in SHAPES.items():
        arrays[name] = np.ascontiguousarray(arrays[name])
        assert arrays[name].shape == shape, (name, arrays[name].shape, shape)
        dram[name] = nc.dram_tensor(name, shape, F32, kind="ExternalInput").ap()
    for name, shape in OUT_SHAPES.items():
        dram[name] = nc.dram_tensor(name, shape, F32, kind="ExternalOutput").ap()
    build(nc, dram)
    r = run(nc, [arrays], core_ids=[0]).results[0]
    y = r["y"].transpose(2, 1, 0).reshape(M, D)
    shift = r["shift_out"].transpose(2, 1, 0).reshape(NSEQ + 1, D)
    conv = r["conv_out"].transpose(2, 1, 0).reshape(NSEQ + 1, 3, QKV_T * P)
    wkv_p = r["wkv_p"].reshape(2, C, T4, C).transpose(2, 0, 3, 1).reshape(1, 1, HR, C, C)
    wkv_s = r["wkv_s"].reshape(2, C, NSEQ, T4, C).transpose(2, 3, 0, 4, 1).reshape(1, NSEQ, HR, C, C)
    return (y[32:][None], y[:32].reshape(NSEQ, TSEQ, D), shift[None, NSEQ:], wkv_p, conv[None, NSEQ:],
            r["gdn_p"].transpose(1, 0, 2)[None, None], shift[None, :NSEQ], wkv_s, conv[None, :NSEQ],
            r["gdn_s"].transpose(1, 2, 0, 3)[None])
```
